# Optimizing a Trainium2 kernel written in Bass

```python
import jax
import jax.numpy as jnp
from jax import lax
import numpy as np
import math
import jax, jax.numpy as jnp

D_MODEL = 1024
BATCH = 1
SEQ = 256
DEPTH = 2

CHUNK = 64
N_META = 16
N_HEADS_A = 8
HEAD_DIM = 64
D_A = N_HEADS_A * HEAD_DIM
N_IDX_HEADS = 8
IDX_DIM = HEAD_DIM
TOPK_MAX = 256
POOL_WINDOWS = (2, 4, 8, 16)
N_POOL_GROUPS = len(POOL_WINDOWS)
D_B = D_MODEL // 2
POOL_GROUP_DIM = D_B // N_POOL_GROUPS
Q_BLOCK = 128
ROPE_THETA = 10000.0
EPS = 1e-6
NEG_INF = -1e30
IN_WIDTHS = (D_A, HEAD_DIM, HEAD_DIM, D_A, D_B, D_B, N_IDX_HEADS * IDX_DIM, IDX_DIM, N_IDX_HEADS, 2 * D_MODEL)
D_IN = sum(IN_WIDTHS)


def rms_norm(x, g):
    xf = x.astype(jnp.float32)
    y = xf * lax.rsqrt(jnp.mean(xf * xf, axis=-1, keepdims=True) + EPS)
    return (y * g.astype(jnp.float32)).astype(x.dtype)

def rope_tables(length, dim):
    inv_freq = 1.0 / (ROPE_THETA ** (jnp.arange(0, dim, 2, dtype=jnp.float32) / dim))
    ang = jnp.arange(length, dtype=jnp.float32)[:, None] * inv_freq[None, :]
    ang = jnp.concatenate([ang, ang], axis=-1)
    return jnp.cos(ang), jnp.sin(ang)

def apply_rope(x, cos, sin):
    half = x.shape[-1] // 2
    xf = x.astype(jnp.float32)
    rot = jnp.concatenate([-xf[..., half:], xf[..., :half]], axis=-1)
    return (xf * cos + rot * sin).astype(x.dtype)

def chunk_id(pos):
    return jnp.where(pos < N_META, 0, 1 + (pos - N_META) // CHUNK)

def indexer_sparse_attention(q, k, v, q_idx, k_idx, w_idx, k_top):
    B, T = q.shape[0], q.shape[1]
    n_blk = -(-T // Q_BLOCK)
    t_pad = n_blk * Q_BLOCK

    def to_blocks(a):
        a = jnp.pad(a, [(0, 0), (0, t_pad - T)] + [(0, 0)] * (a.ndim - 2))
        return jnp.moveaxis(a.reshape((B, n_blk, Q_BLOCK) + a.shape[2:]), 1, 0)

    key_chunk = chunk_id(jnp.arange(T))
    query_chunk = chunk_id(jnp.arange(t_pad)).reshape(n_blk, Q_BLOCK)
    k_idx_f = k_idx.astype(jnp.float32)
    idx_scale = (N_IDX_HEADS ** -0.5) * (IDX_DIM ** -0.5)
    attn_scale = HEAD_DIM ** -0.5
    gather = jax.vmap(lambda table, ids: table[ids])

    def one_block(args):
        qb, qib, wib, qcb = args
        s = jnp.einsum('bqhd,bkd->bqhk', qib.astype(jnp.float32), k_idx_f)
        score = jnp.einsum('bqhk,bqh->bqk', jax.nn.relu(s), wib.astype(jnp.float32) * idx_scale)
        visible = key_chunk[None, :] <= qcb[:, None]
        score = jnp.where(visible[None], score, NEG_INF)
        _, sel = lax.top_k(score, k_top)
        valid = key_chunk[sel] <= qcb[None, :, None]
        kg = gather(k, sel)
        vg = gather(v, sel)
        logits = jnp.einsum('bqhd,bqkd->bqhk', qb, kg).astype(jnp.float32) * attn_scale
        logits = jnp.where(valid[:, :, None, :], logits, NEG_INF)
        p = jax.nn.softmax(logits, axis=-1).astype(vg.dtype)
        return jnp.einsum('bqhk,bqkd->bqhd', p, vg)

    out = lax.map(one_block, (to_blocks(q), to_blocks(q_idx), to_blocks(w_idx), query_chunk))
    return jnp.moveaxis(out, 0, 1).reshape(B, t_pad, N_HEADS_A, HEAD_DIM)[:, :T]

def multiscale_pool(u, pool_w, pool_b, pool_s):
    B, T, C = u.shape
    G = POOL_GROUP_DIM
    uf = u.astype(jnp.float32)
    cs = jnp.concatenate([jnp.zeros((B, 1, C), jnp.float32), jnp.cumsum(uf, axis=1)], axis=1)
    t1 = jnp.arange(1, T + 1, dtype=jnp.float32)
    means = []
    for g, w in enumerate(POOL_WINDOWS):
        csg = cs[..., g * G:(g + 1) * G]
        lag = jnp.concatenate([jnp.zeros((B, w, G), jnp.float32), csg[:, :T + 1 - w]], axis=1)
        cnt = jnp.minimum(t1, float(w))
        means.append((csg[:, 1:] - lag[:, 1:]) / cnt[None, :, None])
    pooled = (jnp.concatenate(means, axis=-1) - uf).astype(u.dtype).reshape(B, T, N_POOL_GROUPS, G)
    mixed = jnp.einsum('btgc,gcd->btgd', pooled, pool_w) + pool_b.reshape(N_POOL_GROUPS, G)
    return mixed.reshape(B, T, C) * pool_s

def hybrid_layer(x, norm_g, w_in, qn_g, kn_g, pool_w, pool_b, pool_s, w_a, w_b, w_out, cos, sin, k_top):
    B, T, _ = x.shape
    h = rms_norm(x, norm_g)
    proj = jnp.einsum('btd,de->bte', h, w_in)
    q, k, v, gate_a, u_b, gate_b, q_idx, k_idx, w_idx, merge = jnp.split(
        proj, np.cumsum(IN_WIDTHS)[:-1].tolist(), axis=-1)
    cos_h, sin_h = cos[:, None, :], sin[:, None, :]
    q = apply_rope(rms_norm(q.reshape(B, T, N_HEADS_A, HEAD_DIM), qn_g), cos_h, sin_h)
    k = apply_rope(rms_norm(k, kn_g), cos, sin)
    q_idx = apply_rope(q_idx.reshape(B, T, N_IDX_HEADS, IDX_DIM), cos_h, sin_h)
    k_idx = apply_rope(k_idx, cos, sin)
    attn = indexer_sparse_attention(q, k, v, q_idx, k_idx, w_idx, k_top).reshape(B, T, D_A)
    y_a = jnp.einsum('bte,ed->btd', attn * jax.nn.silu(gate_a), w_a)
    pooled = multiscale_pool(u_b, pool_w, pool_b, pool_s)
    y_b = jnp.einsum('bte,ed->btd', pooled * jax.nn.silu(gate_b), w_b)
    g_a, g_b = jnp.split(jax.nn.sigmoid(merge), 2, axis=-1)
    return x + jnp.einsum('btd,de->bte', g_a * y_a + g_b * y_b, w_out)

def first_inputs(seed: int = 0) -> dict:
    key = jax.random.key(seed)
    ks = jax.random.split(key, 12)

    def nrm(k, shape, scale):
        return scale * jax.random.normal(k, shape, jnp.float32)

    return {
        'x': nrm(ks[0], (BATCH, SEQ, D_MODEL), 1.0),
        'meta_tokens': nrm(ks[1], (N_META, D_MODEL), 1.0),
        'norm_gain': 1.0 + nrm(ks[2], (DEPTH, D_MODEL), 0.05),
        'w_in': nrm(ks[3], (DEPTH, D_MODEL, D_IN), D_MODEL ** -0.5),
        'q_norm_gain': 1.0 + nrm(ks[4], (DEPTH, HEAD_DIM), 0.05),
        'k_norm_gain': 1.0 + nrm(ks[5], (DEPTH, HEAD_DIM), 0.05),
        'pool_w': nrm(ks[6], (DEPTH, N_POOL_GROUPS, POOL_GROUP_DIM, POOL_GROUP_DIM), POOL_GROUP_DIM ** -0.5),
        'pool_b': nrm(ks[7], (DEPTH, D_B), 0.02),
        'pool_scale': 1.0 + nrm(ks[8], (DEPTH, D_B), 0.1),
        'w_branch_a': nrm(ks[9], (DEPTH, D_A, D_MODEL), D_A ** -0.5),
        'w_branch_b': nrm(ks[10], (DEPTH, D_B, D_MODEL), D_B ** -0.5),
        'w_out': nrm(ks[11], (DEPTH, D_MODEL, D_MODEL), D_MODEL ** -0.5),
    }

def first_block(x, meta_tokens, norm_gain, w_in, q_norm_gain, k_norm_gain, pool_w, pool_b, pool_scale,
              w_branch_a, w_branch_b, w_out):
    B, S, _ = x.shape
    k_top = min(TOPK_MAX, S // 4)
    meta = jnp.broadcast_to(meta_tokens.astype(x.dtype)[None], (B, N_META, D_MODEL))
    h = jnp.concatenate([meta, x], axis=1)
    T = S + N_META
    cos, sin = rope_tables(T, HEAD_DIM)
    for l in range(DEPTH):
        h = hybrid_layer(h, norm_gain[l], w_in[l], q_norm_gain[l], k_norm_gain[l], pool_w[l], pool_b[l],
                         pool_scale[l], w_branch_a[l], w_branch_b[l], w_out[l], cos, sin, k_top)
    return h[:, N_META:]


DEPTH_2 = 1

MEM_LEN = 256
D_FF = 2816
FFN_RES_WEIGHT = 0.5
CONV_A_WIDTH = D_MODEL
CONV_A_K = 3
SSM_D_INNER = 2 * D_MODEL
SSM_HEAD_DIM = 64
SSM_HEADS = SSM_D_INNER // SSM_HEAD_DIM
SSM_GROUPS = 4
SSM_STATE = 128
SSM_CONV_K = 4
SSM_CHUNK = 128
SSM_CONV_CH = SSM_D_INNER + 2 * SSM_GROUPS * SSM_STATE
XATTN_HEADS = 4
XATTN_HEAD_DIM = D_MODEL // XATTN_HEADS
XATTN_SCALE = 1.0 / math.sqrt(XATTN_HEAD_DIM)
IN_SIZES = (CONV_A_WIDTH, CONV_A_WIDTH, CONV_A_WIDTH,
            SSM_D_INNER, SSM_CONV_CH, SSM_HEADS,
            D_MODEL, D_MODEL)
D_IN_PROJ = sum(IN_SIZES)
IN_SPLITS = tuple(int(v) for v in np.cumsum(IN_SIZES)[:-1])


def rmsnorm(x, g):
    xf = x.astype(jnp.float32)
    y = xf * lax.rsqrt(jnp.mean(xf * xf, axis=-1, keepdims=True) + EPS)
    return (y * g.astype(jnp.float32)).astype(x.dtype)

def swiglu(u, w_gate_up, w_down):
    gate, up = jnp.split(u @ w_gate_up, 2, axis=-1)
    return (jax.nn.silu(gate) * up) @ w_down

def causal_dwconv(x, w):
    k, c = w.shape
    return lax.conv_general_dilated(
        x, w[:, None, :].astype(x.dtype), window_strides=(1,),
        padding=[(k - 1, 0)], dimension_numbers=('NWC', 'WIO', 'NWC'),
        feature_group_count=c)

def short_conv_branch(b_gate, c_gate, v, conv_w, w_out):
    return (b_gate * causal_dwconv(c_gate * v, conv_w)) @ w_out

def ssd_chunked(xh, dt, a, bm, cm):
    b, s, h, p = xh.shape
    g, n = bm.shape[-2:]
    k = h // g
    l = SSM_CHUNK
    c = s // l
    x = (xh.astype(jnp.float32) * dt[..., None]).reshape(b, c, l, g, k, p)
    la = (dt * a).reshape(b, c, l, g, k).transpose(0, 1, 3, 4, 2)
    acs = jnp.cumsum(la, axis=-1)
    bc = bm.astype(jnp.float32).reshape(b, c, l, g, n)
    cc = cm.astype(jnp.float32).reshape(b, c, l, g, n)
    seg = acs[..., :, None] - acs[..., None, :]
    causal = jnp.tril(jnp.ones((l, l), dtype=bool))
    decay = jnp.exp(jnp.where(causal, seg, -jnp.inf))
    cb = jnp.einsum('bclgn,bcsgn->bcgls', cc, bc)
    y_diag = jnp.einsum('bcgls,bcgkls,bcsgkp->bclgkp', cb, decay, x)
    decay_to_end = jnp.exp(acs[..., -1:] - acs)
    states = jnp.einsum('bclgn,bcgkl,bclgkp->bcgkpn', bc, decay_to_end, x)
    chunk_decay = jnp.exp(acs[..., -1])

    def step(carry, inp):
        st, dec = inp
        return carry * dec[..., None, None] + st, carry

    init = jnp.zeros((b, g, k, p, n), jnp.float32)
    _, prev = lax.scan(step, init, (jnp.moveaxis(states, 1, 0), jnp.moveaxis(chunk_decay, 1, 0)))
    prev = jnp.moveaxis(prev, 0, 1)
    y_off = jnp.einsum('bclgn,bcgkpn,bcgkl->bclgkp', cc, prev, jnp.exp(acs))
    return (y_diag + y_off).reshape(b, s, h, p)

def mamba2_branch(z, xbc, dt_raw, conv_w, conv_b, dt_bias, a_log, d_skip, norm_g, w_out):
    xbc = jax.nn.silu(causal_dwconv(xbc, conv_w) + conv_b.astype(xbc.dtype))
    xs, bm, cm = jnp.split(xbc, (SSM_D_INNER, SSM_D_INNER + SSM_GROUPS * SSM_STATE), axis=-1)
    b, s, _ = xs.shape
    xh = xs.reshape(b, s, SSM_HEADS, SSM_HEAD_DIM)
    dt = jax.nn.softplus(dt_raw.astype(jnp.float32) + dt_bias.astype(jnp.float32))
    a = -jnp.exp(a_log.astype(jnp.float32))
    y = ssd_chunked(xh, dt, a,
                    bm.reshape(b, s, SSM_GROUPS, SSM_STATE),
                    cm.reshape(b, s, SSM_GROUPS, SSM_STATE))
    y = y + d_skip.astype(jnp.float32)[:, None] * xh.astype(jnp.float32)
    yg = (y.reshape(b, s, SSM_D_INNER) * jax.nn.silu(z.astype(jnp.float32)))
    yg = yg.reshape(b, s, SSM_GROUPS, SSM_D_INNER // SSM_GROUPS)
    yg = yg * lax.rsqrt(jnp.mean(yg * yg, axis=-1, keepdims=True) + EPS)
    y = (yg.reshape(b, s, SSM_D_INNER) * norm_g.astype(jnp.float32)).astype(z.dtype)
    return y @ w_out

def memory_cross_attention(u, mem_n, w_q, w_kv, w_o):
    b, s, _ = u.shape
    m = mem_n.shape[1]
    q = (u @ w_q).reshape(b, s, XATTN_HEADS, XATTN_HEAD_DIM)
    k, v = jnp.split(mem_n @ w_kv, 2, axis=-1)
    k = k.reshape(b, m, XATTN_HEADS, XATTN_HEAD_DIM)
    v = v.reshape(b, m, XATTN_HEADS, XATTN_HEAD_DIM)
    scores = jnp.einsum('bshd,bmhd->bhsm', q, k).astype(jnp.float32) * XATTN_SCALE
    probs = jax.nn.softmax(scores, axis=-1).astype(v.dtype)
    o = jnp.einsum('bhsm,bmhd->bshd', probs, v).reshape(b, s, D_MODEL)
    return o @ w_o

def second_inputs(seed: int = 0) -> dict:
    key = jax.random.key(seed)
    ks = iter(jax.random.split(key, 40))

    def w(shape, fan_in):
        return jax.random.normal(next(ks), shape, jnp.float32) * (fan_in ** -0.5)

    def gain(shape):
        return 1.0 + 0.02 * jax.random.normal(next(ks), shape, jnp.float32)

    L = DEPTH_2
    x = jax.random.normal(next(ks), (BATCH, SEQ, D_MODEL), jnp.float32)
    mem = jax.random.normal(next(ks), (BATCH, MEM_LEN, D_MODEL), jnp.float32)
    dt0 = jnp.exp(jax.random.uniform(next(ks), (L, SSM_HEADS), jnp.float32,
                                     math.log(1e-3), math.log(1e-1)))
    dt_bias = dt0 + jnp.log(-jnp.expm1(-dt0))
    a_log = jnp.log(jax.random.uniform(next(ks), (L, SSM_HEADS), jnp.float32, 1.0, 16.0))
    return {
        "x": x,
        "mem": mem,
        "ffn1_norm": gain((L, D_MODEL)),
        "ffn1_w_gate_up": w((L, D_MODEL, 2 * D_FF), D_MODEL),
        "ffn1_w_down": w((L, D_FF, D_MODEL), D_FF),
        "mix_norm": gain((L, D_MODEL)),
        "w_in": w((L, D_MODEL, D_IN_PROJ), D_MODEL),
        "conv_a_w": w((L, CONV_A_K, CONV_A_WIDTH), CONV_A_K),
        "w_out_a": w((L, CONV_A_WIDTH, D_MODEL), CONV_A_WIDTH),
        "ssm_conv_w": w((L, SSM_CONV_K, SSM_CONV_CH), SSM_CONV_K),
        "ssm_conv_b": 0.02 * jax.random.normal(next(ks), (L, SSM_CONV_CH), jnp.float32),
        "ssm_dt_bias": dt_bias,
        "ssm_a_log": a_log,
        "ssm_d": gain((L, SSM_HEADS)),
        "ssm_norm": gain((L, SSM_D_INNER)),
        "w_out_ssm": w((L, SSM_D_INNER, D_MODEL), SSM_D_INNER),
        "w_mix_out": w((L, D_MODEL, D_MODEL), D_MODEL),
        "xattn_norm": gain((L, D_MODEL)),
        "mem_norm": gain((L, D_MODEL)),
        "w_q": w((L, D_MODEL, D_MODEL), D_MODEL),
        "w_kv": w((L, D_MODEL, 2 * D_MODEL), D_MODEL),
        "w_o_x": w((L, D_MODEL, D_MODEL), D_MODEL),
        "ffn2_norm": gain((L, D_MODEL)),
        "ffn2_w_gate_up": w((L, D_MODEL, 2 * D_FF), D_MODEL),
        "ffn2_w_down": w((L, D_FF, D_MODEL), D_FF),
        "final_norm": gain((D_MODEL,)),
    }

def second_block(x, mem, ffn1_norm, ffn1_w_gate_up, ffn1_w_down, mix_norm, w_in, conv_a_w,
              w_out_a, ssm_conv_w, ssm_conv_b, ssm_dt_bias, ssm_a_log, ssm_d, ssm_norm,
              w_out_ssm, w_mix_out, xattn_norm, mem_norm, w_q, w_kv, w_o_x,
              ffn2_norm, ffn2_w_gate_up, ffn2_w_down, final_norm):
    h = x
    for i in range(DEPTH_2):
        h = h + FFN_RES_WEIGHT * swiglu(rmsnorm(h, ffn1_norm[i]), ffn1_w_gate_up[i], ffn1_w_down[i])
        u = rmsnorm(h, mix_norm[i])
        proj = u @ w_in[i]
        a_b, a_c, a_v, z, xbc, dt_raw, g_a, g_b = jnp.split(proj, IN_SPLITS, axis=-1)
        y_a = short_conv_branch(a_b, a_c, a_v, conv_a_w[i], w_out_a[i])
        y_b = mamba2_branch(z, xbc, dt_raw, ssm_conv_w[i], ssm_conv_b[i], ssm_dt_bias[i],
                            ssm_a_log[i], ssm_d[i], ssm_norm[i], w_out_ssm[i])
        merged = jax.nn.sigmoid(g_a) * y_a + jax.nn.sigmoid(g_b) * y_b
        h = h + merged @ w_mix_out[i]
        h = h + memory_cross_attention(rmsnorm(h, xattn_norm[i]), rmsnorm(mem, mem_norm[i]),
                                       w_q[i], w_kv[i], w_o_x[i])
        h = h + FFN_RES_WEIGHT * swiglu(rmsnorm(h, ffn2_norm[i]), ffn2_w_gate_up[i], ffn2_w_down[i])
    return rmsnorm(h, final_norm)


def setup_inputs(seed=0):
    out = dict(first_inputs(seed))
    for name, value in second_inputs(seed + 1).items():
        if name != "x":
            out[name + "_2"] = value
    return out


def reference(
    x, meta_tokens, norm_gain, w_in, q_norm_gain, k_norm_gain, pool_w, pool_b, pool_scale,
    w_branch_a, w_branch_b, w_out, mem_2, ffn1_norm_2, ffn1_w_gate_up_2, ffn1_w_down_2,
    mix_norm_2, w_in_2, conv_a_w_2, w_out_a_2, ssm_conv_w_2, ssm_conv_b_2, ssm_dt_bias_2,
    ssm_a_log_2, ssm_d_2, ssm_norm_2, w_out_ssm_2, w_mix_out_2, xattn_norm_2, mem_norm_2, w_q_2,
    w_kv_2, w_o_x_2, ffn2_norm_2, ffn2_w_gate_up_2, ffn2_w_down_2, final_norm_2,
):
    x = first_block(
        x, meta_tokens, norm_gain, w_in, q_norm_gain, k_norm_gain, pool_w, pool_b, pool_scale,
        w_branch_a, w_branch_b, w_out,
    )
    return second_block(
        x, mem_2, ffn1_norm_2, ffn1_w_gate_up_2, ffn1_w_down_2, mix_norm_2, w_in_2, conv_a_w_2,
        w_out_a_2, ssm_conv_w_2, ssm_conv_b_2, ssm_dt_bias_2, ssm_a_log_2, ssm_d_2, ssm_norm_2,
        w_out_ssm_2, w_mix_out_2, xattn_norm_2, mem_norm_2, w_q_2, w_kv_2, w_o_x_2, ffn2_norm_2,
        ffn2_w_gate_up_2, ffn2_w_down_2, final_norm_2,
    )


_drawn_inputs = setup_inputs


def setup_inputs(seed=0):
    import zlib

    import numpy as np

    out = dict(_drawn_inputs(seed))
    spreads = {}
    factors = {'q_norm_gain': 7.481,
     'k_norm_gain': 7.002,
     'pool_b': 4.183,
     'ffn1_norm_2': 5.935,
     'mix_norm_2': 2.935,
     'ssm_conv_b_2': 4.957,
     'ssm_d_2': 64.0,
     'ssm_norm_2': 26.652,
     'xattn_norm_2': 8.0,
     'mem_norm_2': 8.0,
     'ffn2_norm_2': 22.948,
     'final_norm_2': 7.928}
    for name, (base, spread) in spreads.items():
        noise = np.random.default_rng([zlib.crc32(name.encode()), seed]).standard_normal(out[name].shape)
        drawn = base * np.exp(spread * noise) if base else spread * noise
        out[name] = jnp.asarray(drawn.astype(out[name].dtype))
    for name, factor in factors.items():
        out[name] = (out[name] * factor).astype(out[name].dtype)
    return out
```

```python
from contextlib import ExitStack

import numpy as np

import concourse.bass as bass
from concourse import mybir

F = mybir.dt.float32
R = mybir.dt.float32r
ALU = mybir.AluOpType
ACT = mybir.ActivationFunctionType
AX = mybir.AxisListType.X

T = 272
S = 256
META = 16
EPS = 1e-6
NEG = -1e30
TILES = 8
SLOT = TILES * 128
NRAW = 5
NSPL = 4
LOOK = 2
YCOLS = 24 * 256

C_ID, C_ONE, C_PERM = 0, 128, 256
C_COS, C_SIN = 384, 656
C_VA, C_VB = 928, 1072
C_CM, C_CN = 1344, 1600
C_RC = 1856
C_S10 = 1920
C_B10 = 1970
C_EPS = 2610
NCONST = 2612

PARAMS = {}


def _param_table():
    at = 0
    for name, n in (("ng0", 8), ("ng1", 8), ("qn0", 1), ("qn1", 1), ("kn0", 1), ("kn1", 1),
                    ("pb0", 4), ("pb1", 4), ("ps0", 4), ("ps1", 4), ("f1n", 8), ("mxn", 8),
                    ("ca", 24), ("cw", 96), ("cb", 24), ("sd", 16), ("sn", 16), ("xn", 8),
                    ("mn", 8), ("f2n", 8), ("fn", 8), ("dtb", 1), ("alog", 1)):
        PARAMS[name] = at
        at += n
    return at


NPARAM = _param_table()


def constants():
    c = np.zeros((128, NCONST), np.float32)
    p = np.arange(128)
    c[p, C_ID + p] = 1.0
    c[:, C_ONE:C_ONE + 128] = 1.0
    for m in range(128):
        if m % 64 < 32:
            c[m + 32, C_PERM + m] = -1.0
        else:
            c[m - 32, C_PERM + m] = 1.0
    inv = (1.0 / (np.float32(10000.0) ** (np.arange(0, 64, 2, dtype=np.float32) / np.float32(64)))).astype(np.float32)
    ang = np.arange(T, dtype=np.float32)[:, None] * inv[None, :]
    ang = np.concatenate([ang, ang], -1).astype(np.float32)
    c[:, C_COS:C_COS + T] = np.tile(np.cos(ang).astype(np.float32).T, (2, 1))
    c[:, C_SIN:C_SIN + T] = np.tile(np.sin(ang).astype(np.float32).T, (2, 1))

    def chunk(x):
        return np.where(x < META, 0, 1 + (x - META) // 64)

    keys = np.arange(T)
    for base, q0, nk in ((C_VA, META, 144), (C_VB, META + 128, T)):
        vis = chunk(keys[:nk])[None, :] <= chunk(q0 + p)[:, None]
        c[:, base:base + nk] = np.where(vis, 0.0, NEG)
    causal = p[:, None] <= p[None, :]
    for half in range(2):
        c[:, C_CM + 128 * half:C_CM + 128 * half + 128] = causal
        c[:, C_CN + 128 * half:C_CN + 128 * half + 128] = np.where(causal, 0.0, NEG)
    for g in range(4):
        c[:, C_RC + 16 * g:C_RC + 16 * g + 16] = 1.0 / np.minimum(np.arange(1, 17), 2 << g)
    for b in range(5):
        c[0:64, C_S10 + 10 * b + 2 * b] = 1.0
        c[64:128, C_S10 + 10 * b + 2 * b + 1] = 1.0
        c[2 * b, C_B10 + 128 * b:C_B10 + 128 * b + 64] = 1.0
        c[2 * b + 1, C_B10 + 128 * b + 64:C_B10 + 128 * b + 128] = 1.0
    c[:, C_EPS] = EPS
    c[:, C_EPS + 1] = 1.0
    return c


class Later:

    def matmul(self, *a, **k):
        return lambda e: e.matmul(*a, **k)

    def transpose(self, *a, **k):
        return lambda e: e.transpose(*a, **k)

    def activation(self, *a, **k):
        return lambda e: e.activation(*a, **k)

    def tensor_tensor(self, *a, **k):
        return lambda e: e.tensor_tensor(*a, **k)

    def tensor_scalar(self, *a, **k):
        return lambda e: e.tensor_scalar(*a, **k)

    def scalar_tensor_tensor(self, *a, **k):
        return lambda e: e.scalar_tensor_tensor(*a, **k)

    def tensor_copy(self, *a, **k):
        return lambda e: e.tensor_copy(*a, **k)

    def reciprocal(self, *a, **k):
        return lambda e: e.reciprocal(*a, **k)

    def tensor_reduce(self, *a, **k):
        return lambda e: e.tensor_reduce(*a, **k)

    def max(self, *a, **k):
        return lambda e: e.max(*a, **k)

    def match_replace(self, *a, **k):
        return lambda e: e.match_replace(*a, **k)

    def memset(self, *a, **k):
        return lambda e: e.memset(*a, **k)

    def tensor_tensor_scan(self, *a, **k):
        return lambda e: e.tensor_tensor_scan(*a, **k)

    def dma_start(self, dst, src, sem):
        return lambda e: e.dma_start(dst, src).then_inc(sem, 16)


LATER = Later()


class Eng:

    def __init__(self, sem):
        self.sem, self.n, self.list, self.seen = sem, 0, [], {}

    def wait(self, *toks):
        for t in toks:
            if t is None:
                continue
            if isinstance(t, list):
                self.wait(*t)
                continue
            sem, v = t
            if self.seen.get(sem.name, 0) < v:
                self.seen[sem.name] = v
                self.list.append((0, sem, v))

    def do(self, fn, *toks):
        self.wait(*toks)
        self.n += 1
        self.list.append((1, fn(LATER), self.sem))
        return (self.sem, self.n)

    def put(self, fn, *toks):
        self.wait(*toks)
        self.list.append((1, fn(LATER), None))

    def last(self):
        return (self.sem, self.n) if self.n else None

    def run(self, e):
        for kind, a, b in self.list:
            if kind == 0:
                e.wait_ge(a, b)
            elif b is None:
                a(e)
            else:
                a(e).then_inc(b, 1)


class Ring:

    def __init__(self, bufs):
        self.bufs = bufs
        self.free = [(k, []) for k in range(len(bufs))]

    def take(self):
        k, toks = self.free.pop(0)
        return k, self.bufs[k], toks

    def give(self, k, *toks):
        self.free.append((k, list(toks)))


def build(nc, wts, small, par, con, mem, out, nslots, plan, tens, sems):
    P, D, A = Eng(sems["pe"]), Eng(sems["dve"]), Eng(sems["act"])
    SP = Eng(sems["sp"])
    raw, whi, wlo = tens["raw"], tens["whi"], tens["wlo"]
    h, xh, xl, yh, yl = tens["h"], tens["xh"], tens["xl"], tens["yh"], tens["yl"]
    cst, prm, ar, banks = tens["cst"], tens["prm"], tens["ar"], tens["banks"]
    ident = cst[:, C_ID:C_ID + 128]
    ones = cst[:, C_ONE:C_ONE + 128]
    eps = cst[:, C_EPS:C_EPS + 1]

    def pc(name, i=0, rows=128):
        return prm[0:rows, PARAMS[name] + i:PARAMS[name] + i + 1]

    arena = {"at": 0, "top": 0}

    def alloc(*shape):
        n = int(np.prod(shape))
        a = ar[:, arena["at"]:arena["at"] + n]
        arena["at"] += n
        arena["top"] = max(arena["top"], arena["at"])
        if len(shape) == 2:
            a = a.rearrange("p (a b) -> p a b", a=shape[0])
        if len(shape) == 3:
            a = a.rearrange("p (a b c) -> p a b c", a=shape[0], b=shape[1])
        return a

    ld = {}

    def load(key, dst, src):
        sem = sems[key]
        SP.put(lambda e: e.dma_start(dst, src, sem))
        ld[key] = (sem, 16)

    load("l_h", h[:, :, :], small)
    load("l_c", cst[:, :], con)
    load("l_p", prm[:, :], par)

    split_tok, pe_done, state = {}, {}, {"loads": 0, "splits": 0}

    def issue_load():
        i = state["loads"]
        if i >= nslots:
            return
        state["loads"] += 1
        k = i % NRAW
        if i >= NRAW:
            SP.wait(*split_tok[i - NRAW])
        sem = sems[f"w{k}"]
        SP.put(lambda e: e.dma_start(raw[:, k, :], None if wts is None else wts[i], sem))

    def issue_split():
        i = state["splits"]
        if i >= nslots:
            return
        state["splits"] += 1
        k, q = i % NRAW, i % NSPL
        landed = (sems[f"w{k}"], 16 * (i // NRAW + 1))
        freed = pe_done[i - NSPL] if i >= NSPL else None
        th = A.do(lambda e: e.activation(whi[:, q, :], raw[:, k, :], ACT.Copy), landed, freed)
        tl = D.do(lambda e: e.tensor_tensor(wlo[:, q, :], raw[:, k, :], whi[:, q, :].bitcast(F), ALU.subtract),
                  landed, freed, th)
        split_tok[i] = [th, tl]
        issue_load()

    for _ in range(NRAW):
        issue_load()

    def tile(desc):
        n = len(plan)
        plan.append(desc)
        slot, j = divmod(n, TILES)
        if j == 0:
            while state["splits"] <= slot + LOOK and state["splits"] < nslots:
                issue_split()
        q = slot % NSPL
        P.wait(*split_tok.get(slot, []))
        return (whi[:, q, 128 * j:128 * j + 128], wlo[:, q, 128 * j:128 * j + 128], slot if j == TILES - 1 else None)

    def align():
        if len(plan) % TILES:
            pe_done[len(plan) // TILES] = P.last()
            plan.extend([None] * (-len(plan) % TILES))

    def mm3(o, a, b, first, last, inc):
        (ah, al), (bh, bl) = a, b
        P.put(lambda e: e.matmul(o, ah, bh, start=first, stop=False))
        P.put(lambda e: e.matmul(o, ah, bl, start=False, stop=False))
        f = lambda e: e.matmul(o, al, bh, start=False, stop=last)
        if inc:
            return P.do(f)
        P.put(f)
        return None

    main = Ring([banks[i] for i in range(4)])
    side = Ring([banks[i] for i in range(4, 8)])

    active = []

    def tick():
        for g in list(active):
            if next(g, "end") == "end":
                active.remove(g)

    def drain(g=None):
        while (g in active) if g is not None else active:
            tick()

    def block(name, l, col, src, n, o=None, free=None, wrap=None):
        k, b = None, None
        if o is None:
            k, b, free = main.take()
            o = b[:, 0:n]
        P.wait(*(free or []))
        tok = None
        for i, (sh, sl, toks) in enumerate(src):
            cols = col if isinstance(col, list) else [(col, 128, 0)]
            wh, wl, ends = tile((name, l, 128 * i, cols))
            P.wait(*toks)
            lastk = i == len(src) - 1
            tok = mm3(o, (wh, wl), (sh, sl), i == 0, lastk, lastk or ends is not None)
            if ends is not None:
                pe_done[ends] = tok
        return k, o, tok

    sqb = Ring([tens["sq"][:, i, :] for i in range(2)])
    xtok = [None] * 8

    class Norm:

        def __init__(self, gain, row, c0=0, src=None, xhi=None, xlo=None):
            self.gain, self.row, self.c0 = gain, row, c0
            self.src = h if src is None else src
            self.xh = xh if xhi is None else xhi
            self.xl = xl if xlo is None else xlo
            self.k, self.bank, self.free = side.take()
            self.tok = [None] * 8
            self.pend = []

        def chunk(self, c, *toks):
            c0, n = self.c0, self.src.shape[2]
            hc = self.src[:, c, c0:n]
            a, b = self.xh[:, c, c0:n], self.xl[:, c, c0:n]
            g = pc(self.gain, c)
            t1 = A.do(lambda e: e.activation(a, hc, ACT.Copy, scale=g), *toks)
            t2 = D.do(lambda e: e.scalar_tensor_tensor(b, hc, g, a.bitcast(F), ALU.mult, ALU.subtract), t1, *toks)
            self.tok[c] = [t1, t2]
            k, sq, free = sqb.take()
            sq = sq[:, 0:n - c0]
            t3 = A.do(lambda e: e.activation(sq, hc, ACT.Square), *free)
            self.pend.append((c, k, sq, t3))

        def sums(self, keep=0):
            w = self.src.shape[2] - self.c0
            while len(self.pend) > keep:
                c, k, sq, t3 = self.pend.pop(0)
                o = self.bank[:, 0:w]
                self.t = P.do(lambda e: e.matmul(o, ones, sq, start=(c == 0), stop=(c == 7)), t3, *self.free)
                sqb.give(k, self.t)

        def rstd(self, newton=False, *free):
            n, c0 = self.src.shape[2], self.c0
            o, row = self.bank[:, 0:n - c0], self.row[:, c0:n]
            rt = tens["rt"][:, 0:n - c0]
            t1 = A.do(lambda e: e.activation(rt, o, ACT.Sqrt, scale=1.0 / 1024, bias=eps), self.t, D.last(), *free)
            t = D.do(lambda e: e.reciprocal(row, rt), t1, *free)
            if newton:
                t = D.do(lambda e: e.tensor_scalar(rt, o, -0.5 / 1024, -0.5 * EPS, ALU.mult, ALU.add), t)
                t = D.do(lambda e: e.tensor_tensor(rt, rt, row, ALU.mult), t)
                t = D.do(lambda e: e.tensor_tensor(rt, rt, row, ALU.mult), t)
                t = D.do(lambda e: e.scalar_tensor_tensor(row, rt, 1.5, row, ALU.add, ALU.mult), t)
            side.give(self.k, t, t1)
            self.rtok = t
            return t

        def feed(self, c0=None):
            n = self.src.shape[2]
            c0 = self.c0 if c0 is None else c0
            return [(self.xh[:, c, c0:n], self.xl[:, c, c0:n], self.tok[c]) for c in range(8)]

    def residual(c, ps, k, tok, scale, nxt, c0):
        n = T - c0
        hc = h[:, c, c0:T]
        t = D.do(lambda e: e.scalar_tensor_tensor(hc, ps, scale, hc, ALU.mult, ALU.add), tok)
        main.give(k, t)
        nxt.sums(0)
        nxt.chunk(c, t)

    def barrier():
        toks = [P.last(), D.last(), A.last()]
        D.wait(*toks)
        A.wait(*toks)

    def transposed(dst, src, tok=None, *free):
        k = src.shape[0]
        P.put(lambda e: e.transpose(dst, src, ident[0:k, 0:k]), tok, *free)

    rows = [tens["rows"][:, i, :] for i in range(2)]
    SP_in = ld["l_h"]
    for e in (A, D, P):
        e.wait(ld["l_h"], ld["l_c"], ld["l_p"])

    norm = Norm("ng0", rows[0])
    for c in range(8):
        norm.chunk(c)
        norm.sums(0)

    def layer(l, norm, nxt_norm):
        arena["at"] = 0
        q0 = 0 if l == 0 else META
        qT, qiT = alloc(4, T), alloc(4, T)
        kT, kiT = alloc(T), alloc(T)
        V = alloc(3, 72)
        ga, gb = alloc(4, T), alloc(4, T)
        mg = alloc(16, T)
        L = alloc(8, T)
        bias, acc = alloc(T), alloc(T)
        rel = Ring([alloc(T) for _ in range(2)])
        PT = Ring([alloc(3, 128) for _ in range(2)])
        PM = L
        rope_a = Ring([alloc(T) for _ in range(2)])
        rope_g = Ring([alloc(T) for _ in range(2)])
        ubr = Ring([alloc(T) for _ in range(2)])
        pw = [alloc(T) for _ in range(2)]
        tmp = Ring([alloc(T) for _ in range(2)])
        m8 = alloc(8, 8)
        nm, sm, rs = alloc(8), alloc(8), alloc(8)
        rt3 = alloc(3)
        psh = alloc(4)
        r10 = alloc(T)
        qa = L[:, 0:5, :]
        Y = lambda i: (yh[:, i * T:(i + 1) * T], yl[:, i * T:(i + 1) * T])
        barrier()
        row = norm.row
        tr = norm.rstd(True, D.last())
        feed_all, feed_q = norm.feed(0), norm.feed(q0)
        nq = T - q0

        tiles3 = [(META, 128), (META + 128, 128), (0, 128)]
        k, bk, free = side.take()
        for i, (t0, n) in enumerate(tiles3):
            transposed(bk[:, 128 * i:128 * i + 128], row[:, t0:t0 + n], tr, *free)
        k_r3, bk_r3 = k, bk
        t_psh = D.do(lambda e: e.tensor_scalar(psh, prm[:, PARAMS[f"ps{l}"]:PARAMS[f"ps{l}"] + 4], 0.5, None, ALU.mult))

        ssq = {"n": 0}
        sk, sbank, sfree = side.take()

        def rope(ps, k, tok, c0, dst, gcol, b, done):
            n = T - c0
            ka, a, fa = rope_a.take() if gcol is None else (None, qa[:, b, :], [])
            a = a[:, 0:n]
            ta = D.do(lambda e: e.tensor_tensor(a, ps, row[:, c0:T], ALU.mult), tok, tr, *fa)
            main.give(k, ta)
            if gcol is None:
                ag, tg, kg = a, ta, None
            else:
                ks, sq, fs = sqb.take()
                sq = sq[:, 0:n]
                ts = A.do(lambda e: e.activation(sq, a, ACT.Square), ta, *fs)
                kg, ag, fg = rope_g.take()
                ag = ag[:, 0:n]
                tg = A.do(lambda e: e.activation(ag, a, ACT.Copy, scale=gcol), ta, *fg)
            yield
            if gcol is not None:
                first, last = ssq["n"] == 0, ssq["n"] == 4
                ssq["n"] += 1
                s10 = cst[:, C_S10 + 10 * b:C_S10 + 10 * b + 10]
                so = sbank[0:10, c0:T]
                if l == 1 and b == 4:
                    pass
                tp = P.do(lambda e: e.matmul(so, s10, sq, start=first, stop=last, skip_group_check=True), ts, *sfree)
                sqb.give(ks, tp)
                if last:
                    ssq["t"] = tp
            kr, rb, fr = side.take()
            ro = rb[:, 0:n]
            tp = P.do(lambda e: e.matmul(ro, cst[:, C_PERM:C_PERM + 128], ag, start=True, stop=True), tg, *fr)
            yield
            t2 = D.do(lambda e: e.tensor_tensor(dst, ro, cst[:, C_SIN + c0:C_SIN + T], ALU.mult), tp)
            side.give(kr, t2)
            t1 = D.do(lambda e: e.tensor_tensor(ag, ag, cst[:, C_COS + c0:C_COS + T], ALU.mult), tp)
            t3 = D.do(lambda e: e.tensor_tensor(dst, dst, ag, ALU.add), t1, t2)
            if kg is not None:
                rope_g.give(kg, t3)
            else:
                rope_a.give(ka, t3)
            done.append(t3)

        tq, tk, tqi, tki = [], [], [], []
        align()
        dup = lambda c: [(c, 64, 0), (c, 64, 64)]
        k, ps, tok = block("w_in", l, dup(512), feed_all, T)
        active.append(rope(ps, k, tok, 0, kT[:, :], pc(f"kn{l}"), 4, tk))
        k, ps, tok = block("w_in", l, dup(2688), feed_all, T)
        active.append(rope(ps, k, tok, 0, kiT[:, :], None, None, tki))
        tick()
        vt = [tile(("w_in", l, 128 * i, [(576, 64, 0), (2752, 8, 64)])) for i in range(8)]
        P.wait(*[t for f in feed_all for t in f[2]])
        tv = []
        t_r3 = D.do(lambda e: e.tensor_copy(rt3, bk_r3[:, 0:384:128]), P.do(
            lambda e: e.transpose(bk_r3[:, 384:512], row[:, 0:128], ident)))
        side.give(k_r3, t_r3)
        for i, (t0, n) in enumerate(tiles3):
            k, b, free = main.take()
            P.wait(*free)
            o = b[:, 0:72]
            for c in range(8):
                wh, wl, ends = vt[c]
                a = (norm.xh[:, c, t0:t0 + n], norm.xl[:, c, t0:t0 + n])
                tok = mm3(o, a, (wh[:, 0:72], wl[:, 0:72]), c == 0, c == 7, c == 7)
            t = D.do(lambda e, i=i, o=o: e.tensor_scalar(V[:, i, :], o, rt3[:, i:i + 1], None, ALU.mult), tok, t_r3)
            main.give(k, t)
            tv.append(t)
        pe_done[vt[7][2]] = tok
        tick()
        idx_scale = 8 ** -0.5 * 64 ** -0.5
        t_w = D.do(lambda e: e.tensor_scalar(V[:, 0:2, 64:72], V[:, 0:2, 64:72], idx_scale, None, ALU.mult), *tv)

        for b in range(4):
            k, ps, tok = block("w_in", l, 2176 + 128 * b, feed_q, nq)
            active.append(rope(ps, k, tok, q0, qiT[:, b, q0:T], None, None, tqi))
            tick()
        for b in range(4):
            k, ps, tok = block("w_in", l, 128 * b, feed_q, nq)
            active.append(rope(ps, k, tok, q0, qT[:, b, q0:T], pc(f"qn{l}"), b, tq))
            tick()

        def gate_a(b):
            k, ps, tok = block("w_in", l, 640 + 128 * b, feed_q, nq)
            kt, m, fm = tmp.take()
            m = m[:, 0:nq]
            g = ga[:, b, q0:T]
            t1 = D.do(lambda e: e.tensor_tensor(m, ps, row[:, q0:T], ALU.mult), tok, *fm)
            main.give(k, t1)
            t2 = A.do(lambda e: e.activation(g, m, ACT.Tanh, scale=0.5), t1)
            t3 = D.do(lambda e: e.scalar_tensor_tensor(g, g, 1.0, m, ALU.add, ALU.mult), t2)
            tmp.give(kt, t3)
            return t3

        def gate_b(b):
            k, ps, tok = block("w_in", l, 1664 + 128 * b, feed_q, nq)
            kt, m, fm = tmp.take()
            m = m[:, 0:nq]
            g = gb[:, b, q0:T]
            t1 = D.do(lambda e: e.tensor_tensor(m, ps, row[:, q0:T], ALU.mult), tok, *fm)
            main.give(k, t1)
            t2 = A.do(lambda e: e.activation(g, m, ACT.Tanh, scale=0.5), t1)
            t3 = D.do(lambda e: e.scalar_tensor_tensor(g, g, 1.0, m, ALU.add, ALU.mult), t2)
            tmp.give(kt, t3)
            return t3

        def merge(b):
            k, ps, tok = block("w_in", l, 2760 + 128 * b, feed_q, nq)
            kt, m, fm = tmp.take()
            m = m[:, 0:nq]
            t1 = D.do(lambda e: e.tensor_tensor(m, ps, row[:, q0:T], ALU.mult), tok, *fm)
            main.give(k, t1)
            t2 = A.do(lambda e: e.activation(mg[:, b, q0:T], m, ACT.Tanh, scale=0.5), t1)
            tmp.give(kt, t2)
            return t2

        def finish_q():
            so, ro, lo = sbank[0:10, 0:T], r10[0:10, 0:T], 0
            e10 = cst[0:10, C_EPS:C_EPS + 1]
            t = A.do(lambda e: e.activation(ro, so, ACT.Sqrt, scale=1.0 / 64, bias=e10), ssq["t"])
            rr = tens["rt"][0:10, 0:T]
            t = D.do(lambda e: e.reciprocal(rr, ro), t)
            side.give(sk, t)
            yield
            for b in (4, 0, 1, 2, 3):
                c0 = 0 if b == 4 else q0
                ks, sb_, fs = side.take()
                o = sb_[:, 0:T - c0]
                sel = cst[0:10, C_B10 + 128 * b:C_B10 + 128 * b + 128]
                tp = P.do(lambda e, o=o, c0=c0, sel=sel: e.matmul(o, sel, rr[:, c0:T], start=True, stop=True), t, *fs)
                dst = kT[:, :] if b == 4 else qT[:, b, q0:T]
                td = D.do(lambda e, o=o, dst=dst: e.tensor_tensor(dst, dst, o, ALU.mult), tp, *tq, *tk)
                side.give(ks, td)
                (tk if b == 4 else tq).append(td)
                if b in (0, 2):
                    yield

        def indexer(tile_no):
            c0, nk = ((META, 144), (META + 128, T))[tile_no]
            vis = cst[:, (C_VA, C_VB)[tile_no]:(C_VA, C_VB)[tile_no] + nk]
            ac = acc[:, 0:nk]
            t = None
            for hh in range(8):
                ks, sb_, fs = side.take()
                o = sb_[:, 0:nk]
                p0 = 64 * (hh % 2)
                tp = P.do(lambda e, o=o, p0=p0, hh=hh: e.matmul(
                    o, qiT[p0:p0 + 64, hh // 2, c0:c0 + 128], kiT[p0:p0 + 64, 0:nk], start=True, stop=True),
                    *tqi, *tki, *fs)
                kr, rl, fr = rel.take()
                rl = rl[:, 0:nk]
                ta = A.do(lambda e, rl=rl, o=o: e.activation(rl, o, ACT.Relu), tp, *fr)
                side.give(ks, ta)
                w = V[:, tile_no, 64 + hh:65 + hh]
                src = vis if hh == 0 else ac
                t = D.do(lambda e, rl=rl, w=w, src=src: e.scalar_tensor_tensor(
                    ac, rl, w, src, ALU.mult, ALU.add), ta, t, t_w)
                rel.give(kr, t)
                if hh % 2:
                    yield
            for r in range(8):
                mx = m8[:, r, :]
                tm = D.do(lambda e, mx=mx: e.max(mx, ac), t)
                t = D.do(lambda e, mx=mx: e.match_replace(ac, mx, ac, -3e38), tm)
                if r % 2:
                    yield
            bs = bias[:, 0:nk]
            t = D.do(lambda e: e.tensor_scalar(bs, ac, -2e38, NEG, ALU.is_gt, ALU.mult), t)
            sel_tok.append(t)

        def attend(tile_no):
            c0, nk = ((META, 144), (META + 128, T))[tile_no]
            kcs = [(2, 0, 16), (0, 16, 128)] + ([(1, 144, 128)] if tile_no else [])
            bs = bias[:, 0:nk]
            tb = sel_tok[-1]
            tl = None
            for hh in range(8):
                ks, sb_, fs = side.take()
                o = sb_[:, 0:nk]
                p0 = 64 * (hh % 2)
                tp = P.do(lambda e, o=o, p0=p0, hh=hh: e.matmul(
                    o, qT[p0:p0 + 64, hh // 2, c0:c0 + 128], kT[p0:p0 + 64, 0:nk], start=True, stop=True),
                    *tq, *tk, *fs)
                tl = D.do(lambda e, o=o, hh=hh: e.scalar_tensor_tensor(
                    L[:, hh, 0:nk], o, 0.125, bs, ALU.mult, ALU.add), tp, tb)
                side.give(ks, tl)
                if hh % 2:
                    yield
            t = D.do(lambda e: e.tensor_reduce(nm, L[:, :, 0:nk], AX, ALU.max, negate=True), tl)
            te = []
            for hh in range(8):
                te.append(A.do(lambda e, hh=hh: e.activation(
                    L[:, hh, 0:nk], L[:, hh, 0:nk], ACT.Exp, bias=nm[:, hh:hh + 1], accum_out=sm[:, hh:hh + 1]), t))
            yield
            t = D.do(lambda e: e.reciprocal(rs, sm), te[-1])
            tn = []
            for hh in range(8):
                tn.append(D.do(lambda e, hh=hh: e.tensor_scalar(
                    L[:, hh, 0:nk], L[:, hh, 0:nk], rs[:, hh:hh + 1], None, ALU.mult), t))
            yield
            ko, ob, fo = side.take()
            pend = []

            def pv(item):
                hh, kp, pt, toks = item
                half = 64 * (hh % 2)
                oo = ob[half:half + 64, 128 * (hh // 2):128 * (hh // 2) + 128]
                for i, (vi, _, kn) in enumerate(kcs):
                    f = lambda e, i=i, vi=vi, kn=kn: e.matmul(
                        oo, V[0:kn, vi, 0:64], pt[0:kn, i, :], start=(i == 0), stop=(i == len(kcs) - 1))
                    tt = P.do(f, *toks, *fo, *tv)
                PT.give(kp, tt)
                return tt

            for hh in range(8):
                ks, sb_, fs = side.take()
                P.wait(*fs, tn[hh])
                for i, (_, k0, kn) in enumerate(kcs):
                    f = lambda e, i=i, k0=k0, kn=kn: e.transpose(
                        sb_[0:kn, 128 * i:128 * i + 128], L[:, hh, k0:k0 + kn], ident)
                    tp = P.do(f)
                kp, pt, fp = PT.take()
                t1 = A.do(lambda e, pt=pt, sb_=sb_: e.activation(pt[0:16, 0, :], sb_[0:16, 0:128], ACT.Copy), tp, *fp)
                nn = len(kcs)
                t2 = A.do(lambda e, pt=pt, sb_=sb_, nn=nn: e.activation(
                    pt[:, 1:nn, :], sb_[:, 128:128 * nn].rearrange("p (a b) -> p a b", b=128), ACT.Copy), tp, *fp)
                side.give(ks, t1, t2)
                if pend:
                    pv(pend.pop(0))
                pend.append((hh, kp, pt, [t1, t2]))
                if hh % 2:
                    yield
            tt = pv(pend.pop(0))
            yield
            for b in range(4):
                kt, m, fm = tmp.take()
                m = m[:, 0:128]
                yhi, ylo = yh[:, b * T + c0:b * T + c0 + 128], yl[:, b * T + c0:b * T + c0 + 128]
                t1 = D.do(lambda e, b=b, m=m: e.scalar_tensor_tensor(
                    m, ob[:, 128 * b:128 * b + 128], 0.5, ga[:, b, c0:c0 + 128], ALU.mult, ALU.mult), tt, *fm, *t_ga)
                t2 = A.do(lambda e, m=m, yhi=yhi: e.activation(yhi, m, ACT.Copy), t1)
                t3 = D.do(lambda e, m=m, yhi=yhi, ylo=ylo: e.tensor_tensor(ylo, m, yhi.bitcast(F), ALU.subtract), t2)
                tmp.give(kt, t3)
                t_at[b] += [t2, t3]
            side.give(ko, t1)

        def attend_meta():
            pair = [side.take() for _ in range(2)]
            P.wait(*tq, *tk, *pair[0][2], *pair[1][2])
            tp = []
            for half in range(2):
                for j in range(4):
                    p0 = 64 * half
                    tp.append(P.do(lambda e, p0=p0, j=j, o=pair[half][1]: e.matmul(
                        o[0:16, 16 * j:16 * j + 16], qT[p0:p0 + 64, j, 0:16], kT[p0:p0 + 64, 0:16],
                        start=True, stop=True)))
            Lm = L[0:16, 0, 0:128].rearrange("p (h k) -> p h k", k=16)
            nmb = nm[0:16, :].unsqueeze(2).broadcast_to([16, 8, 16])
            rsb = rs[0:16, :].unsqueeze(2).broadcast_to([16, 8, 16])
            for half in range(2):
                t = A.do(lambda e, half=half: e.activation(
                    Lm[:, 4 * half:4 * half + 4, :], pair[half][1][0:16, 0:64].rearrange("p (h k) -> p h k", k=16),
                    ACT.Copy, scale=0.125), tp[-1])
                side.give(pair[half][0], t)
            yield
            t = D.do(lambda e: e.tensor_reduce(nm[0:16, :], Lm, AX, ALU.max, negate=True), t)
            t = D.do(lambda e: e.tensor_tensor(Lm, Lm, nmb, ALU.add), t)
            t = A.do(lambda e: e.activation(Lm, Lm, ACT.Exp), t)
            t = D.do(lambda e: e.tensor_reduce(sm[0:16, :], Lm, AX, ALU.add), t)
            t = D.do(lambda e: e.reciprocal(rs[0:16, :], sm[0:16, :]), t)
            t = D.do(lambda e: e.tensor_tensor(Lm, Lm, rsb, ALU.mult), t)
            yield
            ks, sb_, fs = side.take()
            P.wait(*fs, t)
            for hh in range(8):
                tp = P.do(lambda e, hh=hh: e.transpose(sb_[0:16, 16 * hh:16 * hh + 16], Lm[:, hh, :], ident[0:16, 0:16]))
            kp, pt, fp = PT.take()
            ptm = pt[0:16, 0, :]
            t = A.do(lambda e: e.activation(ptm, sb_[0:16, 0:128], ACT.Copy), tp, *fp)
            side.give(ks, t)
            ks, sb2, fs = side.take()
            P.wait(*fs, t, *tv)
            for half in range(2):
                rhs = ptm[:, 64 * half:64 * half + 64]
                tp = P.do(lambda e, half=half, rhs=rhs: e.matmul(
                    sb2[64 * half:64 * half + 64, 0:64], V[0:16, 2, 0:64], rhs, start=True, stop=True))
            PT.give(kp, tp)
            yield
            kt, m, fm = tmp.take()
            m = m[:, 0:64].rearrange("p (j q) -> p j q", q=16)
            yv = [y[:, 0:4 * T].rearrange("p (j t) -> p j t", t=T)[:, :, 0:16] for y in (yh, yl)]
            t1 = D.do(lambda e: e.scalar_tensor_tensor(
                m, sb2[:, 0:64].rearrange("p (j q) -> p j q", q=16), 0.5, ga[:, :, 0:16], ALU.mult, ALU.mult),
                tp, *fm, *t_ga)
            side.give(ks, t1)
            t2 = A.do(lambda e: e.activation(yv[0], m, ACT.Copy), t1)
            t3 = D.do(lambda e: e.tensor_tensor(yv[1], m, yv[0].bitcast(F), ALU.subtract), t2)
            tmp.give(kt, t3)
            for b in range(4):
                t_at[b] += [t2, t3]

        t_ga, sel_tok = [], []
        t_at = [[] for _ in range(4)]

        def attention():
            yield
            yield
            yield from finish_q()
            yield from indexer(0)
            if l == 0:
                yield from attend_meta()
            yield from attend(0)
            yield from indexer(1)
            yield from attend(1)

        def pool(g, ps, k, tok, done):
            ku, u, fu = ubr.take()
            t = D.do(lambda e: e.tensor_tensor(u, ps, row[:, 0:T], ALU.mult), tok, *fu)
            main.give(k, t)
            cur = u
            for i in range(g + 1):
                s, d = 1 << i, pw[i % 2]
                t = D.do(lambda e, s=s, d=d, cur=cur: e.tensor_tensor(
                    d[:, s:T], cur[:, s:T], cur[:, 0:T - s], ALU.add), t)
                t = D.do(lambda e, s=s, d=d, cur=cur: e.tensor_copy(d[:, 0:s], cur[:, 0:s]), t)
                cur = d
            rc = cst[:, C_RC + 16 * g:C_RC + 16 * g + 16]
            yhi, ylo = Y(4 + g)
            yhi, ylo = yhi[:, q0:T], ylo[:, q0:T]
            other = pw[(g + 1) % 2]
            t = D.do(lambda e: e.scalar_tensor_tensor(
                other[:, 16:T], cur[:, 16:T], 1.0 / (2 << g), u[:, 16:T], ALU.mult, ALU.subtract), t)
            if q0 == 0:
                t2 = D.do(lambda e: e.tensor_tensor(other[:, 0:16], cur[:, 0:16], rc, ALU.mult), t)
                t = D.do(lambda e: e.tensor_tensor(other[:, 0:16], other[:, 0:16], u[:, 0:16], ALU.subtract), t2)
            ubr.give(ku, t)
            t2 = A.do(lambda e: e.activation(yhi, other[:, q0:T], ACT.Copy), t)
            t3 = D.do(lambda e: e.tensor_tensor(ylo, other[:, q0:T], yhi.bitcast(F), ALU.subtract), t2)
            done[g] = [t2, t3]

        active.append(attention())
        for b in range(4):
            t_ga.append(gate_a(b))
            tick()
        t_pl = [None] * 4
        for g in range(4):
            k, ps, tok = block("w_in", l, 1152 + 128 * g, feed_all, T)
            pool(g, ps, k, tok, t_pl)
            tick()
        t_gb = []
        for b in range(4):
            t_gb.append(gate_b(b))
            tick()
        t_mg = [None] * 16
        for b in range(8, 16):
            t_mg[b] = merge(b)
            tick()
        t_mid = []
        for g in range(4):
            yhi, ylo = Y(4 + g)
            k, ps, tok = block("pool_w", 4 * l + g, 0, [(yhi[:, q0:T], ylo[:, q0:T], t_pl[g])], nq)
            kt, m, fm = tmp.take()
            m = m[:, 0:nq]
            zh, zl = Y(8 + g)
            zh, zl = zh[:, q0:T], zl[:, q0:T]
            t1 = D.do(lambda e, ps=ps, m=m, g=g: e.tensor_scalar(
                m, ps, pc(f"pb{l}", g), psh[:, g:g + 1], ALU.add, ALU.mult), tok, t_psh, *fm)
            main.give(k, t1)
            t2 = D.do(lambda e, m=m, g=g: e.tensor_tensor(m, m, gb[:, g, q0:T], ALU.mult), t1, t_gb[g])
            t3 = A.do(lambda e, m=m, zh=zh: e.activation(zh, m, ACT.Copy), t2)
            t4 = D.do(lambda e, m=m, zh=zh, zl=zl: e.tensor_tensor(zl, m, zh.bitcast(F), ALU.subtract), t3)
            tmp.give(kt, t4)
            t_mid.append([t3, t4])
        tick()
        src = [(Y(8 + g)[0][:, q0:T], Y(8 + g)[1][:, q0:T], t_mid[g]) for g in range(4)]
        for b in range(8):
            t_mg[b] = merge(b)
            tick()
        t_zb = []
        for b in range(8):
            k, ps, tok = block("w_b", l, 128 * b, src, nq)
            m = mg[:, 8 + b, q0:T]
            t = D.do(lambda e, ps=ps, m=m: e.scalar_tensor_tensor(m, m, 1.0, ps, ALU.add, ALU.mult), tok, t_mg[8 + b])
            main.give(k, t)
            t_zb.append(t)
            tick()
        drain()
        src = [(Y(g)[0][:, q0:T], Y(g)[1][:, q0:T], t_at[g]) for g in range(4)]
        t_z = []
        for b in range(8):
            k, ps, tok = block("w_a", l, 128 * b, src, nq)
            m, zb = mg[:, b, q0:T], mg[:, 8 + b, q0:T]
            t1 = D.do(lambda e, ps=ps, m=m: e.scalar_tensor_tensor(m, m, 1.0, ps, ALU.add, ALU.mult), tok, t_mg[b])
            main.give(k, t1)
            t2 = D.do(lambda e, zb=zb, m=m: e.tensor_tensor(m, m, zb, ALU.add), t1, t_zb[b])
            zh, zl = Y(12 + b)
            zh, zl = zh[:, q0:T], zl[:, q0:T]
            t3 = A.do(lambda e, m=m, zh=zh: e.activation(zh, m, ACT.Copy), t2)
            t4 = D.do(lambda e, m=m, zh=zh, zl=zl: e.tensor_tensor(zl, m, zh.bitcast(F), ALU.subtract), t3)
            t_z.append([t3, t4])
        src = [(Y(12 + b)[0][:, q0:T], Y(12 + b)[1][:, q0:T], t_z[b]) for b in range(8)]
        nxt = Norm(nxt_norm, rows[(l + 1) % 2], q0)
        for b in range(8):
            k, ps, tok = block("w_out", l, 128 * b, src, nq)
            residual(b, ps, k, tok, 0.5, nxt, q0)
        nxt.sums(0)
        return nxt

    norm = layer(0, norm, "ng1")
    norm = layer(1, norm, "f1n")

    Z = META
    Yc = lambda i: (yh[:, i * S:(i + 1) * S], yl[:, i * S:(i + 1) * S])

    def split_to(i, m, tok):
        a, b = Yc(i)
        t1 = A.do(lambda e: e.activation(a, m, ACT.Copy), tok)
        t2 = D.do(lambda e: e.tensor_tensor(b, m, a.bitcast(F), ALU.subtract), t1, tok)
        return [t1, t2]

    def ffn(name, norm, nxt):
        arena["at"] = 0
        tmp = Ring([alloc(2, S) for _ in range(3)])
        sil = Ring([alloc(S) for _ in range(3)])
        barrier()
        row = norm.row
        tr = norm.rstd(False, D.last())
        src = norm.feed()
        rb = row[:, Z:T].unsqueeze(1).broadcast_to([128, 2, S])
        ytok = []
        for j in range(22):
            k, b, free = main.take()
            block(name + "_gu", 0, 128 * j, src, S, b[:, 0:S], free)
            _, _, tok = block(name + "_gu", 0, 2816 + 128 * j, src, S, b[:, S:2 * S], [])
            kt, m, fm = tmp.take()
            t1 = D.do(lambda e, m=m, b=b: e.tensor_tensor(
                m, b[:, :].rearrange("p (a s) -> p a s", a=2), rb, ALU.mult), tok, tr, *fm)
            main.give(k, t1)
            kg, g, fg = sil.take()
            t2 = A.do(lambda e, m=m, g=g: e.activation(g, m[:, 0, :], ACT.Silu), t1, *fg)
            t3 = D.do(lambda e, m=m, g=g: e.tensor_tensor(g, g, m[:, 1, :], ALU.mult), t2)
            tmp.give(kt, t3)
            tt = split_to(j, g, t3)
            sil.give(kg, *tt)
            ytok.append(tt)
        src = [(*Yc(j), ytok[j]) for j in range(22)]
        nxt = nxt()
        for b in range(8):
            k, ps, tok = block(name + "_dn", 0, 128 * b, src, S)
            residual(b, ps, k, tok, 0.5, nxt, Z)
        nxt.sums(0)
        return nxt

    norm = ffn("f1", norm, lambda: Norm("mxn", rows[1], Z))

    def mixer(norm):
        arena["at"] = 0
        zacc = alloc(8, S)
        xsT = [alloc(4, S) for _ in range(2)]
        BC = [alloc(2, S) for _ in range(2)]
        zs = [alloc(4, S) for _ in range(2)]
        xdt = alloc(2, 512)
        btok = alloc(128)
        xw = alloc(512)
        cbm = alloc(2, 128)
        prev = alloc(512)
        M = alloc(8, 256)
        E8 = alloc(8, 128)
        cin = Ring([alloc(3 + S) for _ in range(3)])
        cv = Ring([alloc(S) for _ in range(3)])
        tmp = Ring([alloc(S) for _ in range(3)])
        dtT, acs, dq = alloc(S), alloc(S), alloc(S)
        dden = alloc(128)
        tokm = alloc(5, 32)
        negA = alloc(2, 32)
        acol = alloc(1)
        cwh, cbh, snh = alloc(96), alloc(24), alloc(16)
        grow = alloc(S)
        barrier()
        row = norm.row[:, Z:T]
        tr = norm.rstd(False, D.last())
        src = norm.feed()
        pr = lambda n, w: prm[:, PARAMS[n]:PARAMS[n] + w]
        t = D.do(lambda e: e.tensor_scalar(cwh, pr("cw", 96), 0.5, None, ALU.mult))
        t = D.do(lambda e: e.tensor_scalar(cbh, pr("cb", 24), 0.5, None, ALU.mult))
        t_half = D.do(lambda e: e.tensor_scalar(snh, pr("sn", 16), 0.5, None, ALU.mult))
        tc = [D.do(lambda e, b=b: e.memset(b[:, 0:3], 0.0)) for b in cin.bufs]

        k, ps, tok = block("w_in2", 0, [(8192, 32, 0)], src, S)
        d, ac, q = dtT[0:32, :], acs[0:32, :], dq[0:32, :]
        u = cin.bufs[0][0:32, 3:3 + S]
        v = cin.bufs[1][0:32, 3:3 + S]
        w = cin.bufs[2][0:32, 3:3 + S]
        t = D.do(lambda e: e.tensor_tensor(d, ps[0:32, :], row[0:32, :], ALU.mult), tok, tr)
        main.give(k, t)
        t = D.do(lambda e: e.tensor_scalar(d, d, pc("dtb", 0, 32), None, ALU.add), t)
        t1 = A.do(lambda e: e.activation(u, d, ACT.Abs), t)
        t1 = A.do(lambda e: e.activation(u, u, ACT.Exp, scale=-1.0), t1)
        t2 = A.do(lambda e: e.activation(acol[0:32, :], pc("alog", 0, 32), ACT.Exp))
        t = D.do(lambda e: e.tensor_scalar(d, d, 0.0, None, ALU.max), t1)
        t1 = D.do(lambda e: e.tensor_scalar(v, u, 1.0, None, ALU.add), t1)
        t3 = A.do(lambda e: e.activation(w, v, ACT.Ln), t1)
        t1 = D.do(lambda e: e.tensor_scalar(v, v, -1.0, None, ALU.add), t3)
        t4 = D.do(lambda e: e.tensor_scalar(ac, v, 0.0, None, ALU.is_equal), t1)
        t1 = D.do(lambda e: e.tensor_tensor(v, v, ac, ALU.add), t4)
        t1 = D.do(lambda e: e.reciprocal(q, v), t1)
        t1 = D.do(lambda e: e.tensor_tensor(w, w, q, ALU.mult), t1)
        t1 = D.do(lambda e: e.tensor_tensor(w, w, ac, ALU.add), t1)
        t1 = D.do(lambda e: e.tensor_tensor(w, w, u, ALU.mult), t1)
        t = D.do(lambda e: e.tensor_tensor(d, d, w, ALU.add), t1, t)
        t_dt = t
        t = D.do(lambda e: e.tensor_scalar(q, d, acol[0:32, :], -1.0, ALU.mult, ALU.mult), t2, t)
        for c in range(2):
            t = D.do(lambda e, c=c: e.tensor_tensor_scan(
                ac[:, 128 * c:128 * c + 128], ones[0:32, :], q[:, 128 * c:128 * c + 128], 0.0,
                ALU.mult, ALU.add), t)
        t_ac = t
        t_de = A.do(lambda e: e.activation(dden[0:32, :], ac[:, 0:128], ACT.Exp, scale=-1.0, bias=ac[:, 127:128]), t_ac)
        t_cin = t_ac

        def to_tokens():
            ks, sb_, fs = side.take()
            P.wait(*fs, t_dt, t_ac, t_de)
            for i, a in enumerate((d[:, 0:128], d[:, 128:256], ac[:, 0:128], ac[:, 128:256], dden[0:32, :])):
                tp = P.do(lambda e, i=i, a=a: e.transpose(sb_[:, 32 * i:32 * i + 32], a, ident[0:32, 0:32]))
            t = A.do(lambda e: e.activation(tokm, sb_[:, 0:160].rearrange("p (a b) -> p a b", b=32), ACT.Copy), tp)
            side.give(ks, t)
            return D.do(lambda e: e.tensor_scalar(negA, tokm[:, 2:4, :], -1.0, None, ALU.mult), t)

        cin.free = [(i, [t_cin]) for i in range(3)]

        yat = []
        for j in range(8):
            k1, p1, tok1 = block("w_in2", 0, 1024 + 128 * j, src, S)
            kt, m, fm = tmp.take()
            t1 = D.do(lambda e, m=m, p1=p1: e.tensor_tensor(m, p1, row, ALU.mult), tok1, *fm)
            main.give(k1, t1)
            t1 = D.do(lambda e, m=m: e.tensor_tensor(m, m, row, ALU.mult), t1)
            k2, p2, tok2 = block("w_in2", 0, 2048 + 128 * j, src, S)
            kc, ci, fc = cin.take()
            t2 = D.do(lambda e, ci=ci, m=m, p2=p2: e.tensor_tensor(ci[:, 3:3 + S], m, p2, ALU.mult), t1, tok2, *fc, *tc)
            main.give(k2, t2)
            wc = lambda i, j=j: pc("ca", 8 * i + j)
            t = D.do(lambda e, m=m, ci=ci, w=wc(2): e.tensor_scalar(m, ci[:, 3:3 + S], w, None, ALU.mult), t2)
            for i in (1, 0):
                t = D.do(lambda e, m=m, ci=ci, w=wc(i), i=i: e.scalar_tensor_tensor(
                    m, ci[:, 1 + i:1 + i + S], w, m, ALU.mult, ALU.add), t)
            cin.give(kc, t)
            t = D.do(lambda e, m=m: e.tensor_tensor(m, m, row, ALU.mult), t)
            k3, p3, tok3 = block("w_in2", 0, 128 * j, src, S)
            t = D.do(lambda e, m=m, p3=p3: e.tensor_tensor(m, m, p3, ALU.mult), t, tok3)
            main.give(k3, t)
            tt = split_to(16 + j, m, t)
            tmp.give(kt, *tt)
            yat.append(tt)
            if j == 1:
                t_tok = to_tokens()

        def sig(b, col, dst):
            k, ps, tok = block("w_in2", 0, col + 128 * b, src, S)
            kt, m, fm = tmp.take()
            t1 = D.do(lambda e: e.tensor_tensor(m, ps, row, ALU.mult), tok, *fm)
            main.give(k, t1)
            t2 = A.do(lambda e: e.activation(dst, m, ACT.Tanh, scale=0.5), t1)
            tmp.give(kt, t2)
            return t2

        tza = [sig(b, 8224, zacc[:, b, :]) for b in range(8)]
        srca = [(*Yc(16 + j), yat[j]) for j in range(8)]
        for b in range(8):
            k, ps, tok = block("w_oa", 0, 128 * b, srca, S)
            z = zacc[:, b, :]
            t = D.do(lambda e, z=z, ps=ps: e.scalar_tensor_tensor(z, z, 1.0, ps, ALU.add, ALU.mult), tok, tza[b])
            main.give(k, t)
            tza[b] = t

        def conv(cb, dst, *free):
            k, ps, tok = block("w_in2", 0, 5120 + 128 * cb, src, S)
            kc, ci, fc = cin.take()
            t = D.do(lambda e: e.tensor_tensor(ci[:, 3:3 + S], ps, row, ALU.mult), tok, *fc)
            main.give(k, t)
            kv, s, fv = cv.take()
            wc = lambda i: cwh[:, 24 * i + cb:24 * i + cb + 1]
            t = D.do(lambda e: e.tensor_scalar(s, ci[:, 3:3 + S], wc(3), cbh[:, cb:cb + 1], ALU.mult, ALU.add), t, *fv)
            for i in (2, 1, 0):
                t = D.do(lambda e, i=i: e.scalar_tensor_tensor(
                    s, ci[:, i:i + S], wc(i), s, ALU.mult, ALU.add), t)
            cin.give(kc, t)
            t2 = A.do(lambda e: e.activation(dst, s, ACT.Tanh), t, *free)
            t3 = D.do(lambda e: e.scalar_tensor_tensor(dst, dst, 1.0, s, ALU.add, ALU.mult), t2)
            cv.give(kv, t3)
            return t3

        grp_done = {}

        def ssd(g, tx, tbc, tz):
            x, (BT, CT), z = xsT[g % 2], (BC[g % 2][:, 0, :], BC[g % 2][:, 1, :]), zs[g % 2]
            hs = slice(8 * g, 8 * g + 8)
            prior = grp_done.get(g - 1, [])
            tk_ = []
            for c in range(2):
                ks, sb_, fs = side.take()
                P.wait(*fs, *tx)
                for b in range(4):
                    tp = P.do(lambda e, b=b, c=c, sb_=sb_: e.transpose(
                        sb_[:, 128 * b:128 * b + 128], x[:, b, 128 * c:128 * c + 128], ident))
                dtb = tokm[:, c, hs].unsqueeze(2).broadcast_to([128, 8, 64])
                t = D.do(lambda e, c=c, sb_=sb_, dtb=dtb: e.tensor_tensor(
                    xdt[:, c, :].rearrange("p (h q) -> p h q", q=64),
                    sb_[:, :].rearrange("p (h q) -> p h q", q=64), dtb, ALU.mult), tp, t_tok, *prior)
                side.give(ks, t)
                tk_.append(t)
            deb = tokm[:, 4, hs].unsqueeze(2).broadcast_to([128, 8, 64])
            t_xw = D.do(lambda e: e.tensor_tensor(
                xw.rearrange("p (h q) -> p h q", q=64), xdt[:, 0, :].rearrange("p (h q) -> p h q", q=64),
                deb, ALU.mult), tk_[0])
            ks, sb_, fs = side.take()
            P.wait(*fs, *tbc)
            P.put(lambda e, sb_=sb_: e.transpose(sb_[:, 256:384], BT[:, 0:128], ident))
            for c in range(2):
                cs = slice(128 * c, 128 * c + 128)
                tp = P.do(lambda e, sb_=sb_, cs=cs: e.matmul(sb_[:, cs], BT[:, cs], CT[:, cs], start=True, stop=True))
            t_bt = A.do(lambda e, sb_=sb_: e.activation(btok, sb_[:, 256:384], ACT.Copy), tp, *prior)
            t_cb = D.do(lambda e, sb_=sb_: e.tensor_tensor(
                cbm, sb_[:, 0:256].rearrange("p (a b) -> p a b", a=2),
                cst[:, C_CM:C_CM + 256].rearrange("p (a b) -> p a b", a=2), ALU.mult), tp, t_bt, *prior)
            side.give(ks, t_cb, t_bt)
            yield
            ks, sb_, fs = side.take()
            tp = P.do(lambda e, sb_=sb_: e.matmul(sb_[:, :], btok, xw, start=True, stop=True), t_bt, t_xw, *fs)
            t_pv = A.do(lambda e, sb_=sb_: e.activation(prev, sb_[:, :], ACT.Copy), tp, *prior)
            side.give(ks, t_pv)
            tM, tE = [], []
            for hp in range(4):
                ks, sb_, fs = side.take()
                P.wait(*fs, t_ac)
                tr_ = None
                for i in range(2):
                    hd = 8 * g + 2 * hp + i
                    sel = ident[0:32, hd:hd + 1].broadcast_to([32, 128])
                    tr_ = P.do(lambda e, sb_=sb_, i=i, sel=sel: e.matmul(
                        sb_[:, S * i:S * i + S], sel, acs[0:32, :], start=True, stop=True))
                t1 = A.do(lambda e, sb_=sb_, hp=hp: e.activation(
                    E8[:, 2 * hp:2 * hp + 2, :], sb_[:, :].rearrange("p (a s) -> p a s", a=2)[:, :, 128:256],
                    ACT.Exp), tr_, *prior)
                for i in range(2):
                    for c in range(2):
                        hd = 8 * g + 2 * hp + i
                        t2 = D.do(lambda e, sb_=sb_, hp=hp, i=i, c=c, hd=hd: e.tensor_scalar(
                            M[:, 2 * hp + i, 128 * c:128 * c + 128],
                            sb_[:, S * i + 128 * c:S * i + 128 * c + 128],
                            tokm[:, 2 + c, hd:hd + 1], 0.0, ALU.subtract, ALU.min), t1, t_tok, *prior)
                side.give(ks, t1, t2)
                tE.append(t1)
                t3 = A.do(lambda e, hp=hp: e.activation(
                    M[:, 2 * hp:2 * hp + 2, :], M[:, 2 * hp:2 * hp + 2, :], ACT.Exp), t2)
                cbb = cbm.rearrange("p a b -> p (a b)").unsqueeze(1).broadcast_to([128, 2, 256])
                t4 = D.do(lambda e, hp=hp, cbb=cbb: e.tensor_tensor(
                    M[:, 2 * hp:2 * hp + 2, :], M[:, 2 * hp:2 * hp + 2, :], cbb, ALU.mult), t3, t_cb)
                tM.append(t4)
                yield
            ctb = CT[:, 128:256].unsqueeze(1).broadcast_to([128, 8, 128])
            t_E = D.do(lambda e: e.tensor_tensor(E8, E8, ctb, ALU.mult), *tE)
            yield
            t_y = []
            for half in range(2):
                ks, sb_, fs = side.take()
                P.wait(*fs, *tk_, *tM, t_pv, t_E)
                for hp in range(2 * half, 2 * half + 2):
                    for c in range(2):
                        for i in range(2):
                            hd = 2 * hp + i
                            o = sb_[64 * i:64 * i + 64, S * (hp - 2 * half) + 128 * c:S * (hp - 2 * half) + 128 * c + 128]
                            tp = P.do(lambda e, o=o, c=c, hd=hd: e.matmul(
                                o, xdt[:, c, 64 * hd:64 * hd + 64], M[:, hd, 128 * c:128 * c + 128],
                                start=True, stop=(c == 0)))
                            if c == 1:
                                tp = P.do(lambda e, o=o, hd=hd: e.matmul(
                                    o, prev[:, 64 * hd:64 * hd + 64], E8[:, hd, :], start=False, stop=True))
                for b in range(2):
                    bb = 2 * half + b
                    yb = x[:, bb, :]
                    t1 = D.do(lambda e, sb_=sb_, b=b, bb=bb, yb=yb: e.scalar_tensor_tensor(
                        yb, x[:, bb, :], pc("sd", 4 * g + bb), sb_[:, S * b:S * b + S], ALU.mult, ALU.add), tp, *prior)
                    t2 = D.do(lambda e, bb=bb, yb=yb: e.tensor_tensor(yb, yb, z[:, bb, :], ALU.mult), t1, tz[bb])
                    t_y.append(t2)
                side.give(ks, t1)
                yield
            kq, qb, fq = side.take()
            for bb in range(4):
                k2, sq, f2 = sqb.take()
                t3 = A.do(lambda e, sq=sq, bb=bb: e.activation(sq[:, 0:S], x[:, bb, :], ACT.Square), t_y[bb], *f2)
                t5 = P.do(lambda e, sq=sq, bb=bb: e.matmul(
                    qb[:, 0:S], ones, sq[:, 0:S], start=(bb == 0), stop=(bb == 3)), t3, *fq)
                sqb.give(k2, t5)
            yield
            rt = tens["rt"][:, 0:S]
            t = A.do(lambda e: e.activation(rt, qb[:, 0:S], ACT.Sqrt, scale=1.0 / 2048, bias=eps), t5, *prior)
            side.give(kq, t)
            t = D.do(lambda e: e.reciprocal(grow, rt), t)
            last = []
            for bb in range(4):
                yb = x[:, bb, :]
                t1 = D.do(lambda e, yb=yb, bb=bb: e.scalar_tensor_tensor(
                    yb, yb, snh[:, 4 * g + bb:4 * g + bb + 1], grow, ALU.mult, ALU.mult), t)
                yt[4 * g + bb] = split_to(4 * g + bb, yb, t1)
                last += yt[4 * g + bb]
            grp_done[g] = last + [tp]

        yt = [None] * 16
        for g in range(4):
            old = grp_done.get(g - 2, [])
            bc = BC[g % 2]
            tbc = [conv(16 + g, bc[:, 0, :], *old), None]
            tick()
            tbc[1] = conv(20 + g, bc[:, 1, :], *old)
            tick()
            tx = []
            for b in range(4):
                tx.append(conv(4 * g + b, xsT[g % 2][:, b, :], *old))
                tick()
            tz = []
            for b in range(4):
                k, ps, tok = block("w_in2", 0, 3072 + 128 * (4 * g + b), src, S)
                kt, m, fm = tmp.take()
                t1 = D.do(lambda e, m=m, ps=ps: e.tensor_tensor(m, ps, row, ALU.mult), tok, *fm)
                main.give(k, t1)
                zb = zs[g % 2][:, b, :]
                t2 = A.do(lambda e, m=m, zb=zb: e.activation(zb, m, ACT.Tanh, scale=0.5), t1, *old)
                t3 = D.do(lambda e, m=m, zb=zb: e.scalar_tensor_tensor(zb, zb, 1.0, m, ALU.add, ALU.mult), t2)
                tmp.give(kt, t3)
                tz.append(t3)
                tick()
            drain()
            active.append(ssd(g, tx, tbc, tz))
        tsb = []
        sgb = [(xsT[0] if b < 4 else zs[0])[:, b % 4, :] for b in range(8)]
        D.wait(*grp_done[2])
        A.wait(*grp_done[2])
        for b in range(8):
            tsb.append(sig(b, 9248, sgb[b]))
            tick()
        drain()
        srcb = [(*Yc(j), yt[j]) for j in range(16)]
        tmg = []
        for b in range(8):
            k, ps, tok = block("w_os", 0, 128 * b, srcb, S)
            z, s = zacc[:, b, :], sgb[b]
            t = D.do(lambda e, s=s, ps=ps: e.scalar_tensor_tensor(s, s, 1.0, ps, ALU.add, ALU.mult), tok, tsb[b])
            main.give(k, t)
            t = D.do(lambda e, s=s, z=z: e.tensor_tensor(z, z, s, ALU.add), t, tza[b])
            tmg.append(split_to(16 + b, z, t))
        srcm = [(*Yc(16 + b), tmg[b]) for b in range(8)]
        nxt = Norm("xn", rows[0], Z)
        for b in range(8):
            k, ps, tok = block("w_mo", 0, 128 * b, srcm, S)
            residual(b, ps, k, tok, 0.5, nxt, Z)
        return nxt

    norm = mixer(norm)

    def cross(norm):
        arena["at"] = 0
        mem_sb = alloc(8, S)
        kTt, qTt = alloc(8, S), alloc(8, S)
        V = alloc(2, 1024)
        Pm = alloc(2, 2, S)
        PTx = Ring([alloc(2, S) for _ in range(2)])
        nm, sm, rs = alloc(2, 4), alloc(2, 4), alloc(2, 4)
        mrow = alloc(S)
        rt2 = alloc(2)
        barrier()
        SP.put(lambda e: e.dma_start(mem_sb, mem, sems["l_m"]), D.last(), A.last(), P.last())
        lm = (sems["l_m"], 16)
        norm.sums(0)
        tr = norm.rstd(False, D.last())
        row = norm.row[:, Z:T]
        mh = yh[:, 0:8 * S].rearrange("p (c s) -> p c s", c=8)
        ml = yl[:, 0:8 * S].rearrange("p (c s) -> p c s", c=8)
        mn = Norm("mn", mrow, 0, mem_sb, mh, ml)
        for c in range(8):
            mn.chunk(c, lm)
            mn.sums(0)
        tm = mn.rstd(False, D.last())
        srcm = mn.feed()
        tk = []
        for b in range(8):
            k, ps, tok = block("w_kv", 0, 128 * b, srcm, S)
            t = D.do(lambda e, b=b, ps=ps: e.tensor_tensor(kTt[:, b, :], ps, mrow, ALU.mult), tok, tm)
            main.give(k, t)
            tk.append(t)
        ks, sb_, fs = side.take()
        P.wait(*fs, tm)
        for i in range(2):
            tp = P.do(lambda e, i=i: e.transpose(sb_[:, 128 * i:128 * i + 128], mrow[:, 128 * i:128 * i + 128], ident))
        t_r2 = D.do(lambda e: e.tensor_copy(rt2, sb_[:, 0:256:128]), tp)
        side.give(ks, t_r2)
        tv = []
        for hf in range(2):
            pair = [main.take() for _ in range(2)]
            for c in range(8):
                ws = [tile(("w_kv", 0, 128 * c, [(1024 + 512 * hf + 128 * i, 128, 0)])) for i in range(4)]
                q = (len(plan) - 1) // TILES % NSPL
                j0 = (len(plan) - 4) % TILES
                wh, wl = (w[:, q, 128 * j0:128 * j0 + 512] for w in (whi, wlo))
                for mt in range(2):
                    k, b, free = pair[mt]
                    P.wait(*free)
                    a = (mh[:, c, 128 * mt:128 * mt + 128], ml[:, c, 128 * mt:128 * mt + 128])
                    tok = mm3(b[:, :], a, (wh, wl), c == 0, c == 7, True)
                if ws[3][2] is not None:
                    pe_done[ws[3][2]] = tok
            for mt in range(2):
                k, b, _ = pair[mt]
                t = D.do(lambda e, mt=mt, b=b: e.tensor_scalar(
                    V[:, mt, 512 * hf:512 * hf + 512], b[:, :], rt2[:, mt:mt + 1], None, ALU.mult), tok, t_r2)
                main.give(k, t)
                tv.append(t)
        src = norm.feed()
        tq = []
        t_o = [None] * 8

        def head(hd):
            tn = []
            for st in range(2):
                ks, sb_, fs = side.take()
                P.wait(*fs, *tq, *tk)
                for b in range(2):
                    tp = P.do(lambda e, b=b, st=st, sb_=sb_: e.matmul(
                        sb_[:, 0:S], qTt[:, 2 * hd + b, 128 * st:128 * st + 128], kTt[:, 2 * hd + b, :],
                        start=(b == 0), stop=(b == 1)))
                n1 = nm[:, st, hd:hd + 1]
                t = D.do(lambda e, sb_=sb_, n1=n1: e.tensor_reduce(n1, sb_[:, 0:S], AX, ALU.max, negate=True), tp)
                t = D.do(lambda e, n1=n1: e.tensor_scalar(n1, n1, 1.0 / 16, None, ALU.mult), t)
                te = A.do(lambda e, sb_=sb_, st=st, n1=n1: e.activation(
                    Pm[:, st, hd % 2, :], sb_[:, 0:S], ACT.Exp, scale=1.0 / 16, bias=n1,
                    accum_out=sm[:, st, hd:hd + 1]), t, *xdone.get(hd - 2, []))
                side.give(ks, te)
                t = D.do(lambda e, st=st: e.reciprocal(rs[:, st, hd:hd + 1], sm[:, st, hd:hd + 1]), te)
                tn.append(D.do(lambda e, st=st: e.tensor_scalar(
                    Pm[:, st, hd % 2, :], Pm[:, st, hd % 2, :], rs[:, st, hd:hd + 1], None, ALU.mult), t))
            yield
            ks, sb_, fs = side.take()
            P.wait(*fs, *tn)
            for mc in range(2):
                for st in range(2):
                    tp = P.do(lambda e, mc=mc, st=st: e.transpose(
                        sb_[:, 256 * mc + 128 * st:256 * mc + 128 * st + 128],
                        Pm[:, st, hd % 2, 128 * mc:128 * mc + 128], ident))
            xdone[hd] = [tp]
            kp, pt, fp = PTx.take()
            t = A.do(lambda e: e.activation(pt, sb_[:, :].rearrange("p (a b) -> p a b", a=2), ACT.Copy), tp, *fp)
            side.give(ks, t)
            yield
            ks, sb2, fs = side.take()
            P.wait(*fs, t, *tv)
            for db in range(2):
                for mc in range(2):
                    tp = P.do(lambda e, db=db, mc=mc: e.matmul(
                        sb2[:, S * db:S * db + S], V[:, mc, 256 * hd + 128 * db:256 * hd + 128 * db + 128],
                        pt[:, mc, :], start=(mc == 0), stop=(mc == 1)))
            PTx.give(kp, tp)
            yield
            a, b = (y[:, (8 + 2 * hd) * S:(10 + 2 * hd) * S] for y in (yh, yl))
            t1 = A.do(lambda e: e.activation(a, sb2[:, :], ACT.Copy), tp)
            t2 = D.do(lambda e: e.tensor_tensor(b, sb2[:, :], a.bitcast(F), ALU.subtract), t1)
            t_o[2 * hd] = t_o[2 * hd + 1] = [t1, t2]
            side.give(ks, t2)

        xdone = {}
        for b in range(8):
            k, ps, tok = block("w_q", 0, 128 * b, src, S)
            t = D.do(lambda e, b=b, ps=ps: e.tensor_tensor(qTt[:, b, :], ps, row, ALU.mult), tok, tr)
            main.give(k, t)
            tq.append(t)
            if b % 2:
                active.append(head(b // 2))
            tick()
        drain()
        srco = [(*Yc(8 + j), t_o[j]) for j in range(8)]
        nxt = Norm("f2n", rows[1], Z)
        for b in range(8):
            k, ps, tok = block("w_o", 0, 128 * b, srco, S)
            residual(b, ps, k, tok, 1.0, nxt, Z)
        nxt.sums(0)
        return nxt

    norm = cross(norm)
    norm = ffn("f2", norm, lambda: Norm("fn", rows[0], Z))
    norm.sums(0)
    tr = norm.rstd(False, D.last())
    for c in range(8):
        hc = h[:, c, Z:T]
        t = D.do(lambda e, hc=hc, c=c: e.scalar_tensor_tensor(
            hc, hc, pc("fn", c), norm.row[:, Z:T], ALU.mult, ALU.mult), tr, *norm.tok[c])
        if c % 4 == 3:
            c0 = c - 3
            SP.put(lambda e, c0=c0: e.dma_start(out[:, c0:c0 + 4, :], h[:, c0:c0 + 4, Z:T], sems["o"]), t)
    SP.wait((sems["o"], 32))
    return P, D, A, SP, arena["top"]


ARENA = 16800


def program(nc, wts_shape_decl, small, par, con, mem, out):
    with ExitStack() as ctx:
        def sb(name, shape, dt=F):
            return ctx.enter_context(nc.sbuf_tensor(name, shape, dt))

        names = ["pe", "dve", "act", "sp", "l_h", "l_c", "l_p", "l_m", "o"] + [f"w{i}" for i in range(NRAW)]
        sems = {n: ctx.enter_context(nc.semaphore(n)) for n in names}
        tens = {
            "raw": sb("raw", [128, NRAW, SLOT]), "whi": sb("whi", [128, NSPL, SLOT], R),
            "wlo": sb("wlo", [128, NSPL, SLOT], R), "h": sb("h", [128, 8, T]),
            "xh": sb("xh", [128, 8, T], R), "xl": sb("xl", [128, 8, T], R),
            "yh": sb("yh", [128, YCOLS], R), "yl": sb("yl", [128, YCOLS], R),
            "cst": sb("cst", [128, NCONST]), "prm": sb("prm", [128, NPARAM]), "ar": sb("ar", [128, ARENA]),
            "sq": sb("sq", [128, 2, T]), "rt": sb("rt", [128, T]), "rows": sb("rows", [128, 2, T]),
            "banks": [ctx.enter_context(nc.psum_tensor(f"bank{i}", [128, 512], F)) for i in range(8)],
        }
        plan = []
        build(nc, None, small, par, con, mem, out, 10 ** 6, plan, tens, sems)
        nslots = -(-len(plan) // TILES)
        wts = wts_shape_decl(nslots)
        again = []
        P, D, A, SP, top = build(nc, wts, small, par, con, mem, out, nslots, again, tens, sems)
        assert top <= ARENA, top
        assert len(again) == len(plan)
        block = ctx.enter_context(nc.Block())

        @block.sync
        def _(e):
            SP.run(e)

        @block.tensor
        def _(e):
            P.run(e)

        @block.vector
        def _(e):
            D.run(e)

        @block.scalar
        def _(e):
            A.run(e)
    return plan, nslots


def kernel(**inputs):
    import concourse.bacc as _bacc
    from concourse.bass_utils import run_bass_kernel_spmd as _run

    a = {n: np.asarray(v) for n, v in inputs.items()}
    nc = _bacc.Bacc("TRN2", target_bir_lowering=False, num_devices=1)

    def dram(name, shape, kind="ExternalInput"):
        return nc.dram_tensor(name, shape, F, kind=kind).ap()

    small, par, con = dram("x_dram", [128, 8, T]), dram("par_dram", [128, NPARAM]), dram("con_dram", [128, NCONST])
    mem, out = dram("mem_dram", [128, 8, S]), dram("out_dram", [128, 8, S], "ExternalOutput")
    plan, nslots = program(nc, lambda n: dram("w_dram", [n, 128, SLOT]), small, par, con, mem, out)

    mats = {
        "w_in": a["w_in"], "pool_w": a["pool_w"].reshape(8, 128, 128), "w_a": a["w_branch_a"],
        "w_b": a["w_branch_b"], "w_out": a["w_out"], "f1_gu": a["ffn1_w_gate_up_2"], "f1_dn": a["ffn1_w_down_2"],
        "w_in2": a["w_in_2"], "w_oa": a["w_out_a_2"], "w_os": a["w_out_ssm_2"], "w_mo": a["w_mix_out_2"],
        "w_q": a["w_q_2"], "w_kv": a["w_kv_2"], "w_o": a["w_o_x_2"], "f2_gu": a["ffn2_w_gate_up_2"],
        "f2_dn": a["ffn2_w_down_2"],
    }
    w = np.zeros((nslots, 128, SLOT), np.float32)
    for n, item in enumerate(plan):
        if item is None:
            continue
        name, l, r0, cols = item
        s, j = divmod(n, TILES)
        for c0, width, at in cols:
            w[s, :, 128 * j + at:128 * j + at + width] = mats[name][l, r0:r0 + 128, c0:c0 + width]

    def cols(v, n):
        return np.asarray(v).reshape(n, 128).T

    p = np.zeros((128, NPARAM), np.float32)

    def put(name, v):
        p[0:v.shape[0], PARAMS[name]:PARAMS[name] + v.shape[1]] = v

    for l in range(2):
        put(f"ng{l}", cols(a["norm_gain"][l], 8))
        put(f"qn{l}", np.concatenate([a["q_norm_gain"][l]] * 2)[:, None])
        put(f"kn{l}", np.concatenate([a["k_norm_gain"][l]] * 2)[:, None])
        put(f"pb{l}", cols(a["pool_b"][l], 4))
        put(f"ps{l}", cols(a["pool_scale"][l], 4))
    put("f1n", cols(a["ffn1_norm_2"][0], 8))
    put("mxn", cols(a["mix_norm_2"][0], 8))
    put("ca", np.concatenate([cols(a["conv_a_w_2"][0, i], 8) for i in range(3)], 1))
    put("cw", np.concatenate([cols(a["ssm_conv_w_2"][0, i], 24) for i in range(4)], 1))
    put("cb", cols(a["ssm_conv_b_2"][0], 24))
    put("sd", cols(np.repeat(a["ssm_d_2"][0], 64), 16))
    put("sn", cols(a["ssm_norm_2"][0], 16))
    put("xn", cols(a["xattn_norm_2"][0], 8))
    put("mn", cols(a["mem_norm_2"][0], 8))
    put("f2n", cols(a["ffn2_norm_2"][0], 8))
    put("fn", cols(a["final_norm_2"], 8))
    put("dtb", a["ssm_dt_bias_2"][0][:, None])
    put("alog", a["ssm_a_log_2"][0][:, None])

    def fm(x):
        return np.ascontiguousarray(x.reshape(x.shape[0], 8, 128).transpose(2, 1, 0))

    arrays = {
        "x_dram": fm(np.concatenate([a["meta_tokens"], a["x"][0]], 0)), "par_dram": p, "con_dram": constants(),
        "mem_dram": fm(a["mem_2"][0]), "w_dram": w,
    }
    r = _run(nc, [arrays], core_ids=[0])
    o = np.asarray(r.results[0]["out_dram"])
    return np.ascontiguousarray(o.transpose(2, 1, 0)).reshape(1, S, 1024)
```

```python
from contextlib import ExitStack

import numpy as np

import concourse.bass as bass
from concourse import mybir

F = mybir.dt.float32
R = mybir.dt.float32r
ALU = mybir.AluOpType
ACT = mybir.ActivationFunctionType
AX = mybir.AxisListType.X

T = 272
S = 256
META = 16
EPS = 1e-6
NEG = -1e30
TILES = 8
SLOT = TILES * 128
NRAW = 4
NSPL = 5
LOOK = 3
POOL_EVERY = 2
YCOLS = 24 * 256

C_ID, C_ONE, C_PERM = 0, 128, 256
C_COS, C_SIN = 384, 656
C_VA, C_VB = 928, 1072
C_CM = 1344
C_RC = 1600
C_S10 = 1664
C_EPS = 1714
C_B10 = 1716
C_R3 = 2356
NCONST = 2366

PARAMS = {}


def _param_table():
    at = 0
    for name, n in (("ng0", 8), ("ng1", 8), ("qn0", 1), ("qn1", 1), ("kn0", 1), ("kn1", 1),
                    ("pb0", 4), ("pb1", 4), ("ps0", 4), ("ps1", 4), ("f1n", 8), ("mxn", 8),
                    ("ca", 24), ("cw", 96), ("cb", 24), ("sd", 16), ("sn", 16), ("xn", 8),
                    ("mn", 8), ("f2n", 8), ("fn", 8), ("dtb", 1), ("alog", 1)):
        PARAMS[name] = at
        at += n
    return at


NPARAM = _param_table()


def constants():
    c = np.zeros((128, NCONST), np.float32)
    p = np.arange(128)
    c[p, C_ID + p] = 1.0
    c[:, C_ONE:C_ONE + 128] = 1.0
    for m in range(128):
        if m % 64 < 32:
            c[m + 32, C_PERM + m] = -1.0
        else:
            c[m - 32, C_PERM + m] = 1.0
    inv = (1.0 / (np.float32(10000.0) ** (np.arange(0, 64, 2, dtype=np.float32) / np.float32(64)))).astype(np.float32)
    ang = np.arange(T, dtype=np.float32)[:, None] * inv[None, :]
    ang = np.concatenate([ang, ang], -1).astype(np.float32)
    c[:, C_COS:C_COS + T] = np.tile(np.cos(ang).astype(np.float32).T, (2, 1))
    c[:, C_SIN:C_SIN + T] = np.tile(np.sin(ang).astype(np.float32).T, (2, 1))

    def chunk(x):
        return np.where(x < META, 0, 1 + (x - META) // 64)

    keys = np.arange(T)
    for base, q0, nk in ((C_VA, META, 144), (C_VB, META + 128, T)):
        vis = chunk(keys[:nk])[None, :] <= chunk(q0 + p)[:, None]
        c[:, base:base + nk] = np.where(vis, 0.0, NEG)
    causal = p[:, None] <= p[None, :]
    for half in range(2):
        c[:, C_CM + 128 * half:C_CM + 128 * half + 128] = causal
    for g in range(4):
        c[:, C_RC + 16 * g:C_RC + 16 * g + 16] = 1.0 / np.minimum(np.arange(1, 17), 2 << g)
    for b in range(5):
        c[0:64, C_S10 + 10 * b + 2 * b] = 1.0
        c[64:128, C_S10 + 10 * b + 2 * b + 1] = 1.0
        c[2 * b, C_B10 + 128 * b:C_B10 + 128 * b + 64] = 1.0
        c[2 * b + 1, C_B10 + 128 * b + 64:C_B10 + 128 * b + 128] = 1.0
    c[:, C_EPS] = EPS
    c[:, C_EPS + 1] = 1.0
    return c


class Later:

    def matmul(self, *a, **k):
        return lambda e: e.matmul(*a, **k)

    def transpose(self, *a, **k):
        return lambda e: e.transpose(*a, **k)

    def activation(self, *a, **k):
        return lambda e: e.activation(*a, **k)

    def tensor_tensor(self, *a, **k):
        return lambda e: e.tensor_tensor(*a, **k)

    def tensor_scalar(self, *a, **k):
        return lambda e: e.tensor_scalar(*a, **k)

    def scalar_tensor_tensor(self, *a, **k):
        return lambda e: e.scalar_tensor_tensor(*a, **k)

    def tensor_copy(self, *a, **k):
        return lambda e: e.tensor_copy(*a, **k)

    def reciprocal(self, *a, **k):
        return lambda e: e.reciprocal(*a, **k)

    def tensor_reduce(self, *a, **k):
        return lambda e: e.tensor_reduce(*a, **k)

    def max(self, *a, **k):
        return lambda e: e.max(*a, **k)

    def match_replace(self, *a, **k):
        return lambda e: e.match_replace(*a, **k)

    def memset(self, *a, **k):
        return lambda e: e.memset(*a, **k)

    def tensor_tensor_scan(self, *a, **k):
        return lambda e: e.tensor_tensor_scan(*a, **k)

    def dma_start(self, dst, src, sem):
        return lambda e: e.dma_start(dst, src).then_inc(sem, 16)


LATER = Later()


class Pending(list):

    def __init__(self, settle):
        self.issued, self.settle = False, settle


class Eng:

    def __init__(self, sem):
        self.sem, self.n, self.list, self.seen = sem, 0, [], {}

    def wait(self, *toks):
        for t in toks:
            if t is None:
                continue
            if isinstance(t, Pending) and not t.issued:
                t.settle()
            if isinstance(t, list):
                self.wait(*t)
                continue
            sem, v = t
            if self.seen.get(sem.name, 0) < v:
                self.seen[sem.name] = v
                self.list.append((0, sem, v))

    def add(self, ins, *toks):
        self.wait(*toks)
        self.n += 1
        self.list.append((1, ins, self.sem))
        return (self.sem, self.n)

    def do(self, fn, *toks):
        return self.add(fn(LATER), *toks)

    def put(self, fn, *toks):
        self.wait(*toks)
        self.list.append((1, fn(LATER), None))

    def last(self):
        return (self.sem, self.n) if self.n else None

    def run(self, e):
        for kind, a, b in self.list:
            if kind == 0:
                e.wait_ge(a, b)
            elif b is None:
                a(e)
            else:
                a(e).then_inc(b, 1)


class Ring:

    def __init__(self, bufs):
        self.bufs = bufs
        self.free = [(k, []) for k in range(len(bufs))]

    def take(self):
        k, toks = self.free.pop(0)
        return k, self.bufs[k], toks

    def give(self, k, *toks):
        self.free.append((k, list(toks)))


def build(nc, wts, small, par, con, mem, out, nslots, plan, tens, sems):
    P, D, A = Eng(sems["pe"]), Eng(sems["dve"]), Eng(sems["act"])
    SP, G = Eng(sems["sp"]), Eng(sems["pool"])
    waiting = []

    def later(eng, fn, *toks):
        p = Pending(flush)
        waiting.append((p, eng, fn(LATER), toks))
        return p

    def flush():
        while waiting:
            p, eng, ins, toks = waiting.pop(0)
            p.append(eng.add(ins, *toks))
            p.issued = True

    raw, whi, wlo = tens["raw"], tens["whi"], tens["wlo"]
    h, xh, xl, yh, yl = tens["h"], tens["xh"], tens["xl"], tens["yh"], tens["yl"]
    cst, prm, ar, banks = tens["cst"], tens["prm"], tens["ar"], tens["banks"]
    ident = cst[:, C_ID:C_ID + 128]
    ones = cst[:, C_ONE:C_ONE + 128]
    eps = cst[:, C_EPS:C_EPS + 1]

    def pc(name, i=0, rows=128):
        return prm[0:rows, PARAMS[name] + i:PARAMS[name] + i + 1]

    arena = {"at": 0, "top": 0}

    def alloc(*shape):
        n = int(np.prod(shape))
        a = ar[:, arena["at"]:arena["at"] + n]
        arena["at"] += n
        arena["top"] = max(arena["top"], arena["at"])
        if len(shape) == 2:
            a = a.rearrange("p (a b) -> p a b", a=shape[0])
        if len(shape) == 3:
            a = a.rearrange("p (a b c) -> p a b c", a=shape[0], b=shape[1])
        return a

    ld = {}

    def load(key, dst, src):
        sem = sems[key]
        SP.put(lambda e: e.dma_start(dst, src, sem))
        ld[key] = (sem, 16)

    load("l_h", h[:, :, :], small)
    load("l_c", cst[:, :], con)
    load("l_p", prm[:, :], par)

    split_tok, pe_done, state = {}, {}, {"loads": 0, "splits": 0}

    def issue_load():
        i = state["loads"]
        if i >= nslots:
            return
        state["loads"] += 1
        k = i % NRAW
        if i >= NRAW:
            SP.wait(*split_tok[i - NRAW])
        sem = sems[f"w{k}"]
        SP.put(lambda e: e.dma_start(raw[:, k, :], None if wts is None else wts[i], sem))

    def issue_split():
        i = state["splits"]
        if i >= nslots:
            return
        state["splits"] += 1
        k, q = i % NRAW, i % NSPL
        landed = (sems[f"w{k}"], 16 * (i // NRAW + 1))
        freed = pe_done[i - NSPL] if i >= NSPL else None
        th = A.do(lambda e: e.activation(whi[:, q, :], raw[:, k, :], ACT.Copy), landed, freed)
        if i % POOL_EVERY == POOL_EVERY - 1:
            tl = []
            for c in (0, SLOT // 2):
                cs = slice(c, c + SLOT // 2)
                tl.append(G.do(lambda e: e.tensor_tensor(
                    wlo[:, q, cs], raw[:, k, cs], whi[:, q, cs].bitcast(F), ALU.subtract), landed, freed, th))
        else:
            tl = D.do(lambda e: e.tensor_tensor(
                wlo[:, q, :], raw[:, k, :], whi[:, q, :].bitcast(F), ALU.subtract), landed, freed, th)
        split_tok[i] = [th, tl]
        issue_load()

    for _ in range(NRAW):
        issue_load()

    def tile(desc):
        n = len(plan)
        plan.append(desc)
        slot, j = divmod(n, TILES)
        if j == 0:
            while state["splits"] <= slot + LOOK and state["splits"] < nslots:
                issue_split()
        q = slot % NSPL
        P.wait(*split_tok.get(slot, []))
        return (whi[:, q, 128 * j:128 * j + 128], wlo[:, q, 128 * j:128 * j + 128], slot if j == TILES - 1 else None)

    def align():
        if len(plan) % TILES:
            pe_done[len(plan) // TILES] = P.last()
            plan.extend([None] * (-len(plan) % TILES))

    def mm3(o, a, b, first, last, inc):
        (ah, al), (bh, bl) = a, b
        P.put(lambda e: e.matmul(o, ah, bh, start=first, stop=False))
        P.put(lambda e: e.matmul(o, ah, bl, start=False, stop=False))
        f = lambda e: e.matmul(o, al, bh, start=False, stop=last)
        if inc:
            return P.do(f)
        P.put(f)
        return None

    main = Ring([banks[i] for i in range(4)])
    side = Ring([banks[i] for i in range(4, 8)])

    active = []

    def tick():
        for g in list(active):
            if next(g, "end") == "end":
                active.remove(g)

    def drain():
        while active:
            flush()
            tick()

    def block(name, l, col, src, n, o=None, free=None, wrap=None):
        flush()
        k, b = None, None
        if o is None:
            k, b, free = main.take()
            o = b[:, 0:n]
        P.wait(*(free or []))
        tok = None
        for i, (sh, sl, toks) in enumerate(src):
            cols = col if isinstance(col, list) else [(col, 128, 0)]
            wh, wl, ends = tile((name, l, 128 * i, cols))
            P.wait(*toks)
            lastk = i == len(src) - 1
            tok = mm3(o, (wh, wl), (sh, sl), i == 0, lastk, lastk or ends is not None)
            if ends is not None:
                pe_done[ends] = tok
        return k, o, tok

    rows = [tens["rows"][:, i, :] for i in range(2)]
    cols3 = [cst[:, C_R3 + 3 * i:C_R3 + 3 * i + 3] for i in range(3)]
    sqb = Ring([tens["sq"][:, i, :] for i in range(2)])
    xtok = [None] * 8

    class Norm:

        def __init__(self, gain, row, c0=0, src=None, xhi=None, xlo=None, late=False):
            self.gain, self.row, self.c0, self.late = gain, row, c0, late
            self.src = h if src is None else src
            self.xh = xh if xhi is None else xhi
            self.xl = xl if xlo is None else xlo
            self.k, self.bank, self.free = side.take()
            self.tok = [None] * 8
            self.pend = []
            n = self.src.shape[2]
            self.tiles = [(n - 256, 128), (n - 128, 128)] + ([(0, META)] if c0 == 0 and n > S else [])
            self.col = cols3[0 if row is rows[0] else 1]

        def chunk(self, c, *toks):
            n = self.src.shape[2]
            hc = self.src[:, c, self.c0:n]
            if not self.late:
                a, b = self.xh[:, c, self.c0:n], self.xl[:, c, self.c0:n]
                g = pc(self.gain, c)
                t1 = A.do(lambda e: e.activation(a, hc, ACT.Copy, scale=g), *toks)
                t2 = later(D, lambda e: e.scalar_tensor_tensor(b, hc, g, a.bitcast(F), ALU.mult, ALU.subtract),
                           t1, *toks)
                self.tok[c] = [t1, t2]
            k, sq, free = sqb.take()
            t3 = A.do(lambda e: e.activation(sq[:, self.c0:n], hc, ACT.Square), *toks, *free)
            self.pend.append((c, k, sq, t3))

        def sums(self):
            for c, k, sq, t3 in self.pend:
                for j, (t0, n) in enumerate(self.tiles):
                    self.t = P.do(lambda e: e.matmul(
                        self.bank[0:n, j:j + 1], sq[:, t0:t0 + n], ones[:, 0:1], start=(c == 0 and j == 0),
                        stop=(c == 7), skip_group_check=True), t3, *self.free)
                sqb.give(k, self.t)
            self.pend.clear()

        def rstd(self, newton, *free):
            self.sums()
            c3, tmp3, row = self.col, cols3[2], self.row
            t = None
            for p, j0, j1 in ((128, 0, 2), (META, 2, 3)):
                if len(self.tiles) < j1:
                    break
                o, r, q = self.bank[0:p, j0:j1], c3[0:p, j0:j1], tmp3[0:p, j0:j1]
                t1 = A.do(lambda e: e.activation(q, o, ACT.Sqrt, scale=1.0 / 1024, bias=eps[0:p, :]), self.t, t,
                          D.last(), *free)
                t = D.do(lambda e: e.reciprocal(r, q), t1, *free)
                if newton:
                    t = D.do(lambda e: e.tensor_scalar(q, o, -0.5 / 1024, -0.5 * EPS, ALU.mult, ALU.add), t)
                    t = D.do(lambda e: e.tensor_tensor(q, q, r, ALU.mult), t)
                    t = D.do(lambda e: e.tensor_tensor(q, q, r, ALU.mult), t)
                    t = D.do(lambda e: e.scalar_tensor_tensor(r, q, 1.5, r, ALU.add, ALU.mult), t)
            side.give(self.k, t, t1)
            self.ctok = t
            k, b, fs = side.take()
            for j, (t0, n) in enumerate(self.tiles):
                tp = P.do(lambda e: e.matmul(b[:, t0:t0 + n], c3[0:n, j:j + 1].broadcast_to([n, 128]),
                                             ident[0:n, 0:n], start=True, stop=True), t, *fs)
            c0, n = self.c0, self.src.shape[2]
            self.rtok = A.do(lambda e: e.activation(row[:, c0:n], b[:, c0:n], ACT.Copy), tp, D.last())
            side.give(k, self.rtok)
            return self.rtok

        def apply(self, ring):
            n, row = self.src.shape[2], self.row
            for c in range(8):
                hc, g = self.src[:, c, self.c0:n], pc(self.gain, c)
                a, b = self.xh[:, c, self.c0:n], self.xl[:, c, self.c0:n]
                k, m, fm = ring.take()
                t = D.do(lambda e: e.scalar_tensor_tensor(m, hc, g, row[:, self.c0:n], ALU.mult, ALU.mult),
                         self.rtok, *fm)
                t1 = A.do(lambda e: e.activation(a, m, ACT.Copy), t)
                flush()
                t2 = later(D, lambda e: e.tensor_tensor(b, m, a.bitcast(F), ALU.subtract), t1)
                ring.give(k, t2)
                self.tok[c] = [t1, t2]
            flush()

        def feed(self, c0=None):
            n = self.src.shape[2]
            c0 = self.c0 if c0 is None else c0
            return [(self.xh[:, c, c0:n], self.xl[:, c, c0:n], self.tok[c]) for c in range(8)]

    def residual(c, ps, k, tok, scale, nxt, c0):
        n = T - c0
        hc = h[:, c, c0:T]
        t = D.do(lambda e: e.scalar_tensor_tensor(hc, ps, scale, hc, ALU.mult, ALU.add), tok)
        main.give(k, t)
        nxt.sums()
        nxt.chunk(c, t)

    def barrier():
        flush()
        toks = [P.last(), D.last(), A.last(), G.last()]
        for e in (D, A, G):
            e.wait(*toks)

    def transposed(dst, src, tok=None, *free):
        k = src.shape[0]
        P.put(lambda e: e.transpose(dst, src, ident[0:k, 0:k]), tok, *free)

    SP_in = ld["l_h"]
    for e in (A, D, P, G):
        e.wait(ld["l_h"], ld["l_c"], ld["l_p"])

    identb, maskb = tens["cnb"][:, 0:128], tens["cnb"][:, 128:384]
    D.do(lambda e: e.tensor_copy(identb, ident))
    D.do(lambda e: e.tensor_scalar(maskb, cst[:, C_CM:C_CM + 256], 1.0, -NEG, ALU.subtract, ALU.mult))

    norm = Norm("ng0", rows[0])
    for c in range(8):
        norm.chunk(c)
        norm.sums()

    def layer(l, norm, nxt_norm):
        arena["at"] = 0
        q0 = 0 if l == 0 else META
        qT, qiT = alloc(4, T), alloc(4, T)
        kT, kiT = alloc(T), alloc(T)
        V = alloc(3, 72)
        ga, gb = alloc(4, T), alloc(4, T)
        mg = alloc(16, T)
        L = alloc(8, T)
        scr = [alloc(T) for _ in range(2)]
        PT = Ring([alloc(3, 128) for _ in range(2)])
        PM = L
        rope_a = Ring([alloc(T) for _ in range(2)])
        rope_g = Ring([alloc(T) for _ in range(2)])
        rel = Ring([alloc(T), alloc(T), rope_g.bufs[0], rope_g.bufs[1]])
        ubr = Ring([alloc(16 + T)])
        pw = rope_a.bufs[0]
        tmp = Ring([alloc(T) for _ in range(3)])
        m8 = alloc(8, 8)
        nm, sm, rs = alloc(8), alloc(8), alloc(8)
        psh = alloc(4)
        r10 = scr[1]
        qa = L[:, 0:5, :]
        Y = lambda i: (yh[:, i * T:(i + 1) * T], yl[:, i * T:(i + 1) * T])
        barrier()
        row = norm.row
        tr = norm.rstd(True, D.last())
        feed_all, feed_q = norm.feed(0), norm.feed(q0)
        nq = T - q0

        tiles3 = [(META, 128), (META + 128, 128), (0, 128)]
        rt3 = norm.col
        t_psh = D.do(lambda e: e.tensor_scalar(psh, prm[:, PARAMS[f"ps{l}"]:PARAMS[f"ps{l}"] + 4], 0.5, None, ALU.mult))

        t_pad = D.do(lambda e: e.memset(ubr.bufs[0][:, 0:16], 0.0))
        ssq = {"n": 0}
        sk, sbank, sfree = side.take()

        def rope(ps, k, tok, c0, dst, gcol, b, done):
            n = T - c0
            ka, a, fa = rope_a.take() if gcol is None else (None, qa[:, b, :], [])
            a = a[:, 0:n]
            ta = D.do(lambda e: e.tensor_tensor(a, ps, row[:, c0:T], ALU.mult), tok, tr, *fa)
            main.give(k, ta)
            if gcol is None:
                ag, tg, kg = a, ta, None
            else:
                ks, sq, fs = sqb.take()
                sq = sq[:, 0:n]
                ts = A.do(lambda e: e.activation(sq, a, ACT.Square), ta, *fs)
                kg, ag, fg = rope_g.take()
                ag = ag[:, 0:n]
                tg = A.do(lambda e: e.activation(ag, a, ACT.Copy, scale=gcol), ta, *fg)
            yield
            if gcol is not None:
                first, last = ssq["n"] == 0, ssq["n"] == 4
                ssq["n"] += 1
                s10 = cst[:, C_S10 + 10 * b:C_S10 + 10 * b + 10]
                so = sbank[0:10, c0:T]
                if l == 1 and b == 4:
                    pass
                tp = P.do(lambda e: e.matmul(so, s10, sq, start=first, stop=last, skip_group_check=True), ts, *sfree)
                sqb.give(ks, tp)
                if last:
                    ssq["t"] = tp
            kr, rb, fr = side.take()
            ro = rb[:, 0:n]
            tp = P.do(lambda e: e.matmul(ro, cst[:, C_PERM:C_PERM + 128], ag, start=True, stop=True), tg, *fr)
            yield
            t2 = D.do(lambda e: e.tensor_tensor(dst, ro, cst[:, C_SIN + c0:C_SIN + T], ALU.mult), tp)
            side.give(kr, t2)
            t1 = G.do(lambda e: e.tensor_tensor(ag, ag, cst[:, C_COS + c0:C_COS + T], ALU.mult), tp)
            t3 = later(D, lambda e: e.tensor_tensor(dst, dst, ag, ALU.add), t1, t2)
            if kg is not None:
                rope_g.give(kg, t3)
            else:
                rope_a.give(ka, t3)
            done.append(t3)

        tq, tk, tqi, tki = [], [], [], []
        align()
        dup = lambda c: [(c, 64, 0), (c, 64, 64)]
        k, ps, tok = block("w_in", l, dup(512), feed_all, T)
        active.append(rope(ps, k, tok, 0, kT[:, :], pc(f"kn{l}"), 4, tk))
        k, ps, tok = block("w_in", l, dup(2688), feed_all, T)
        active.append(rope(ps, k, tok, 0, kiT[:, :], None, None, tki))
        tick()
        vt = [tile(("w_in", l, 128 * i, [(576, 64, 0), (2752, 8, 64)])) for i in range(8)]
        P.wait(*[t for f in feed_all for t in f[2]])
        tv = []
        flush()
        for i, (t0, n) in enumerate(tiles3):
            k, b, free = main.take()
            P.wait(*free)
            o = b[:, 0:72]
            for c in range(8):
                wh, wl, ends = vt[c]
                a = (norm.xh[:, c, t0:t0 + n], norm.xl[:, c, t0:t0 + n])
                tok = mm3(o, a, (wh[:, 0:72], wl[:, 0:72]), c == 0, c == 7, c == 7)
            r = 128 if i < 2 else META
            t = D.do(lambda e: e.tensor_scalar(V[0:r, i, :], o[0:r, :], rt3[0:r, i:i + 1], None, ALU.mult), tok,
                     norm.ctok)
            main.give(k, t)
            tv.append(t)
        pe_done[vt[7][2]] = tok
        tick()
        idx_scale = 8 ** -0.5 * 64 ** -0.5
        t_w = D.do(lambda e: e.tensor_scalar(V[:, 0:2, 64:72], V[:, 0:2, 64:72], idx_scale, None, ALU.mult), *tv)

        for b in range(4):
            k, ps, tok = block("w_in", l, 2176 + 128 * b, feed_q, nq)
            active.append(rope(ps, k, tok, q0, qiT[:, b, q0:T], None, None, tqi))
            tick()
        for b in range(4):
            k, ps, tok = block("w_in", l, 128 * b, feed_q, nq)
            active.append(rope(ps, k, tok, q0, qT[:, b, q0:T], pc(f"qn{l}"), b, tq))
            tick()

        def gate_a(b):
            k, ps, tok = block("w_in", l, 640 + 128 * b, feed_q, nq)
            kt, m, fm = tmp.take()
            m = m[:, 0:nq]
            g = ga[:, b, q0:T]
            t1 = D.do(lambda e: e.tensor_tensor(m, ps, row[:, q0:T], ALU.mult), tok, *fm)
            main.give(k, t1)
            t2 = A.do(lambda e: e.activation(g, m, ACT.Tanh, scale=0.5), t1)
            t3 = later(D, lambda e: e.scalar_tensor_tensor(g, g, 1.0, m, ALU.add, ALU.mult), t2)
            tmp.give(kt, t3)
            return t3

        def gate_b(b):
            k, ps, tok = block("w_in", l, 1664 + 128 * b, feed_q, nq)
            kt, m, fm = tmp.take()
            m = m[:, 0:nq]
            g = gb[:, b, q0:T]
            t1 = D.do(lambda e: e.tensor_tensor(m, ps, row[:, q0:T], ALU.mult), tok, *fm)
            main.give(k, t1)
            t2 = A.do(lambda e: e.activation(g, m, ACT.Tanh, scale=0.5), t1)
            t3 = later(D, lambda e: e.scalar_tensor_tensor(g, g, 1.0, m, ALU.add, ALU.mult), t2)
            tmp.give(kt, t3)
            return t3

        def merge(b):
            k, ps, tok = block("w_in", l, 2760 + 128 * b, feed_q, nq)
            kt, m, fm = tmp.take()
            m = m[:, 0:nq]
            t1 = D.do(lambda e: e.tensor_tensor(m, ps, row[:, q0:T], ALU.mult), tok, *fm)
            main.give(k, t1)
            t2 = A.do(lambda e: e.activation(mg[:, b, q0:T], m, ACT.Tanh, scale=0.5), t1)
            tmp.give(kt, t2)
            return t2

        def finish_q():
            so, ro, lo = sbank[0:10, 0:T], r10[0:10, 0:T], 0
            e10 = cst[0:10, C_EPS:C_EPS + 1]
            t = A.do(lambda e: e.activation(ro, so, ACT.Sqrt, scale=1.0 / 64, bias=e10), ssq["t"])
            rr = PT.bufs[0][0:10, :, :].rearrange("p a b -> p (a b)")[:, 0:T]
            t = D.do(lambda e: e.reciprocal(rr, ro), t)
            side.give(sk, t)
            yield
            for b in (4, 0, 1, 2, 3):
                c0 = 0 if b == 4 else q0
                ks, sb_, fs = side.take()
                o = sb_[:, 0:T - c0]
                sel = cst[0:10, C_B10 + 128 * b:C_B10 + 128 * b + 128]
                tp = P.do(lambda e, o=o, c0=c0, sel=sel: e.matmul(o, sel, rr[:, c0:T], start=True, stop=True), t, *fs)
                dst = kT[:, :] if b == 4 else qT[:, b, q0:T]
                td = D.do(lambda e, o=o, dst=dst: e.tensor_tensor(dst, dst, o, ALU.mult), tp, *tq, *tk)
                side.give(ks, td)
                (tk if b == 4 else tq).append(td)
                if b in (0, 2):
                    yield

        def indexer(tile_no):
            c0, nk = ((META, 144), (META + 128, T))[tile_no]
            vis = cst[:, (C_VA, C_VB)[tile_no]:(C_VA, C_VB)[tile_no] + nk]
            ac = scr[tile_no][:, 0:nk]
            t = None
            for hh in range(8):
                ks, sb_, fs = side.take()
                o = sb_[:, 0:nk]
                p0 = 64 * (hh % 2)
                tp = P.do(lambda e, o=o, p0=p0, hh=hh: e.matmul(
                    o, qiT[p0:p0 + 64, hh // 2, c0:c0 + 128], kiT[p0:p0 + 64, 0:nk], start=True, stop=True),
                    *tqi, *tki, *fs)
                kr, rl, fr = rel.take()
                rl = rl[:, 0:nk]
                ta = A.do(lambda e, rl=rl, o=o: e.activation(rl, o, ACT.Relu), tp, *fr)
                side.give(ks, ta)
                w = V[:, tile_no, 64 + hh:65 + hh]
                src = vis if hh == 0 else ac
                t = later(D, lambda e: e.scalar_tensor_tensor(
                    ac, rl, w, src, ALU.mult, ALU.add), ta, t, t_w)
                rel.give(kr, t)
                if hh % (2, 4)[1 - tile_no] == (2, 4)[1 - tile_no] - 1:
                    yield
            for r in range(8):
                mx = m8[:, r, :]
                tm = D.do(lambda e, mx=mx: e.max(mx, ac), t)
                t = D.do(lambda e, mx=mx: e.match_replace(ac, mx, ac, -3e38), tm)
                if r % (2, 4)[1 - tile_no] == (2, 4)[1 - tile_no] - 1:
                    yield
            sel_tok[tile_no] = D.do(lambda e: e.tensor_scalar(ac, ac, -2e38, NEG, ALU.is_gt, ALU.mult), t)

        def attend(tile_no):
            c0, nk = ((META, 144), (META + 128, T))[tile_no]
            kcs = [(2, 0, 16), (0, 16, 128)] + ([(1, 144, 128)] if tile_no else [])
            bs = scr[tile_no][:, 0:nk]
            tb = sel_tok[tile_no]
            tl = None
            for hh in range(8):
                ks, sb_, fs = side.take()
                o = sb_[:, 0:nk]
                p0 = 64 * (hh % 2)
                tp = P.do(lambda e, o=o, p0=p0, hh=hh: e.matmul(
                    o, qT[p0:p0 + 64, hh // 2, c0:c0 + 128], kT[p0:p0 + 64, 0:nk], start=True, stop=True),
                    *tq, *tk, *fs)
                tl = later(D, lambda e: e.scalar_tensor_tensor(
                    L[:, hh, 0:nk], o, 0.125, bs, ALU.mult, ALU.add), tp, tb)
                side.give(ks, tl)
                if hh % (2, 4)[1 - tile_no] == (2, 4)[1 - tile_no] - 1:
                    yield
            t = D.do(lambda e: e.tensor_reduce(nm, L[:, :, 0:nk], AX, ALU.max, negate=True), tl)
            te = []
            for hh in range(8):
                te.append(A.do(lambda e, hh=hh: e.activation(
                    L[:, hh, 0:nk], L[:, hh, 0:nk], ACT.Exp, bias=nm[:, hh:hh + 1], accum_out=sm[:, hh:hh + 1]), t))
            yield
            t = D.do(lambda e: e.reciprocal(rs, sm), te[-1])
            tn = []
            for hh in range(8):
                tn.append(D.do(lambda e, hh=hh: e.tensor_scalar(
                    L[:, hh, 0:nk], L[:, hh, 0:nk], rs[:, hh:hh + 1], None, ALU.mult), t))
            yield
            ko, ob, fo = side.take()
            pend = []

            def pv(item):
                hh, kp, pt, toks = item
                half = 64 * (hh % 2)
                oo = ob[half:half + 64, 128 * (hh // 2):128 * (hh // 2) + 128]
                for i, (vi, _, kn) in enumerate(kcs):
                    f = lambda e, i=i, vi=vi, kn=kn: e.matmul(
                        oo, V[0:kn, vi, 0:64], pt[0:kn, i, :], start=(i == 0), stop=(i == len(kcs) - 1))
                    tt = P.do(f, *toks, *fo, *tv)
                PT.give(kp, tt)
                return tt

            for hh in range(8):
                ks, sb_, fs = side.take()
                P.wait(*fs, tn[hh])
                for i, (_, k0, kn) in enumerate(kcs):
                    f = lambda e, i=i, k0=k0, kn=kn: e.transpose(
                        sb_[0:kn, 128 * i:128 * i + 128], L[:, hh, k0:k0 + kn], ident)
                    tp = P.do(f)
                kp, pt, fp = PT.take()
                t1 = A.do(lambda e, pt=pt, sb_=sb_: e.activation(pt[0:16, 0, :], sb_[0:16, 0:128], ACT.Copy), tp, *fp)
                nn = len(kcs)
                t2 = A.do(lambda e, pt=pt, sb_=sb_, nn=nn: e.activation(
                    pt[:, 1:nn, :], sb_[:, 128:128 * nn].rearrange("p (a b) -> p a b", b=128), ACT.Copy), tp, *fp)
                side.give(ks, t1, t2)
                if pend:
                    pv(pend.pop(0))
                pend.append((hh, kp, pt, [t1, t2]))
                if hh % 2:
                    yield
            tt = pv(pend.pop(0))
            yield
            for b in range(4):
                kt, m, fm = tmp.take()
                m = m[:, 0:128]
                yhi, ylo = yh[:, b * T + c0:b * T + c0 + 128], yl[:, b * T + c0:b * T + c0 + 128]
                t1 = D.do(lambda e, b=b, m=m: e.scalar_tensor_tensor(
                    m, ob[:, 128 * b:128 * b + 128], 0.5, ga[:, b, c0:c0 + 128], ALU.mult, ALU.mult), tt, *fm, *t_ga)
                t2 = A.do(lambda e, m=m, yhi=yhi: e.activation(yhi, m, ACT.Copy), t1)
                t3 = later(D, lambda e: e.tensor_tensor(ylo, m, yhi.bitcast(F), ALU.subtract), t2)
                tmp.give(kt, t3)
                t_at[b] += [t2, t3]
            side.give(ko, t1)

        def attend_meta():
            pair = [side.take() for _ in range(2)]
            P.wait(*tq, *tk, *pair[0][2], *pair[1][2])
            tp = []
            for half in range(2):
                for j in range(4):
                    p0 = 64 * half
                    tp.append(P.do(lambda e, p0=p0, j=j, o=pair[half][1]: e.matmul(
                        o[0:16, 16 * j:16 * j + 16], qT[p0:p0 + 64, j, 0:16], kT[p0:p0 + 64, 0:16],
                        start=True, stop=True)))
            Lm = L[0:16, 0, 0:128].rearrange("p (h k) -> p h k", k=16)
            nmb = nm[0:16, :].unsqueeze(2).broadcast_to([16, 8, 16])
            rsb = rs[0:16, :].unsqueeze(2).broadcast_to([16, 8, 16])
            for half in range(2):
                t = A.do(lambda e, half=half: e.activation(
                    Lm[:, 4 * half:4 * half + 4, :], pair[half][1][0:16, 0:64].rearrange("p (h k) -> p h k", k=16),
                    ACT.Copy, scale=0.125), tp[-1])
                side.give(pair[half][0], t)
            yield
            t = D.do(lambda e: e.tensor_reduce(nm[0:16, :], Lm, AX, ALU.max, negate=True), t)
            t = D.do(lambda e: e.tensor_tensor(Lm, Lm, nmb, ALU.add), t)
            t = A.do(lambda e: e.activation(Lm, Lm, ACT.Exp), t)
            t = D.do(lambda e: e.tensor_reduce(sm[0:16, :], Lm, AX, ALU.add), t)
            t = D.do(lambda e: e.reciprocal(rs[0:16, :], sm[0:16, :]), t)
            t = D.do(lambda e: e.tensor_tensor(Lm, Lm, rsb, ALU.mult), t)
            yield
            ks, sb_, fs = side.take()
            P.wait(*fs, t)
            for hh in range(8):
                tp = P.do(lambda e, hh=hh: e.transpose(sb_[0:16, 16 * hh:16 * hh + 16], Lm[:, hh, :], ident[0:16, 0:16]))
            kp, pt, fp = PT.take()
            ptm = pt[0:16, 0, :]
            t = A.do(lambda e: e.activation(ptm, sb_[0:16, 0:128], ACT.Copy), tp, *fp)
            side.give(ks, t)
            ks, sb2, fs = side.take()
            P.wait(*fs, t, *tv)
            for half in range(2):
                rhs = ptm[:, 64 * half:64 * half + 64]
                tp = P.do(lambda e, half=half, rhs=rhs: e.matmul(
                    sb2[64 * half:64 * half + 64, 0:64], V[0:16, 2, 0:64], rhs, start=True, stop=True))
            PT.give(kp, tp)
            yield
            kt, m, fm = tmp.take()
            m = m[:, 0:64].rearrange("p (j q) -> p j q", q=16)
            yv = [y[:, 0:4 * T].rearrange("p (j t) -> p j t", t=T)[:, :, 0:16] for y in (yh, yl)]
            t1 = D.do(lambda e: e.scalar_tensor_tensor(
                m, sb2[:, 0:64].rearrange("p (j q) -> p j q", q=16), 0.5, ga[:, :, 0:16], ALU.mult, ALU.mult),
                tp, *fm, *t_ga)
            side.give(ks, t1)
            t2 = A.do(lambda e: e.activation(yv[0], m, ACT.Copy), t1)
            t3 = D.do(lambda e: e.tensor_tensor(yv[1], m, yv[0].bitcast(F), ALU.subtract), t2)
            tmp.give(kt, t3)
            for b in range(4):
                t_at[b] += [t2, t3]

        t_ga, sel_tok = [], {}
        t_at = [[] for _ in range(4)]

        def attention():
            yield
            yield
            yield from finish_q()
            rel.free = [(i, [*tq, *tk]) for i in range(4)]
            yield from indexer(0)
            active.append(indexer(1))
            if l == 0:
                yield from attend_meta()
            yield from attend(0)
            while 1 not in sel_tok:
                yield
            yield from attend(1)

        def pool(g, ps, k, tok, done):
            ku, ub, fu = ubr.take()
            u, w = ub[:, 16:16 + T], 2 << g
            t = D.do(lambda e: e.tensor_tensor(u, ps, row[:, 0:T], ALU.mult), tok, t_pad, *fu)
            main.give(k, t)
            t = D.do(lambda e: e.tensor_tensor_scan(pw, u, ub[:, 16 - w:16 - w + T], 0.0, ALU.add, ALU.subtract), t,
                     *tq, *tki, *tk, *tqi)
            yhi, ylo = Y(4 + g)
            yhi, ylo = yhi[:, q0:T], ylo[:, q0:T]
            kt, m, fm = tmp.take()
            t2 = D.do(lambda e: e.scalar_tensor_tensor(
                m[:, 16:T], pw[:, 16:T], 1.0 / w, u[:, 16:T], ALU.mult, ALU.subtract), t, *fm)
            if q0 == 0:
                rc = cst[:, C_RC + 16 * g:C_RC + 16 * g + 16]
                t = D.do(lambda e: e.tensor_tensor(m[:, 0:16], pw[:, 0:16], rc, ALU.mult), t, *fm)
                t = D.do(lambda e: e.tensor_tensor(m[:, 0:16], m[:, 0:16], u[:, 0:16], ALU.subtract), t)
            ubr.give(ku, t, t2)
            t3 = A.do(lambda e: e.activation(yhi, m[:, q0:T], ACT.Copy), t, t2)
            t4 = later(D, lambda e: e.tensor_tensor(ylo, m[:, q0:T], yhi.bitcast(F), ALU.subtract), t3)
            tmp.give(kt, t4)
            done[g] = [t3, t4]

        active.append(attention())
        for b in range(4):
            t_ga.append(gate_a(b))
            tick()
        t_pl = [None] * 4
        for g in range(4):
            k, ps, tok = block("w_in", l, 1152 + 128 * g, feed_all, T)
            pool(g, ps, k, tok, t_pl)
            tick()
        t_gb = []
        for b in range(4):
            t_gb.append(gate_b(b))
            tick()
        t_mg = [None] * 16
        for b in range(8, 16):
            t_mg[b] = merge(b)
            tick()
        t_mid = []
        for g in range(4):
            yhi, ylo = Y(4 + g)
            k, ps, tok = block("pool_w", 4 * l + g, 0, [(yhi[:, q0:T], ylo[:, q0:T], t_pl[g])], nq)
            kt, m, fm = tmp.take()
            m = m[:, 0:nq]
            zh, zl = Y(8 + g)
            zh, zl = zh[:, q0:T], zl[:, q0:T]
            t1 = D.do(lambda e, ps=ps, m=m, g=g: e.tensor_scalar(
                m, ps, pc(f"pb{l}", g), psh[:, g:g + 1], ALU.add, ALU.mult), tok, t_psh, *fm)
            main.give(k, t1)
            t2 = D.do(lambda e, m=m, g=g: e.tensor_tensor(m, m, gb[:, g, q0:T], ALU.mult), t1, t_gb[g])
            t3 = A.do(lambda e, m=m, zh=zh: e.activation(zh, m, ACT.Copy), t2)
            t4 = later(D, lambda e: e.tensor_tensor(zl, m, zh.bitcast(F), ALU.subtract), t3)
            tmp.give(kt, t4)
            t_mid.append([t3, t4])
        tick()
        src = [(Y(8 + g)[0][:, q0:T], Y(8 + g)[1][:, q0:T], t_mid[g]) for g in range(4)]
        for b in range(8):
            t_mg[b] = merge(b)
            tick()
        t_zb = []
        for b in range(8):
            k, ps, tok = block("w_b", l, 128 * b, src, nq)
            m = mg[:, 8 + b, q0:T]
            t = D.do(lambda e, ps=ps, m=m: e.scalar_tensor_tensor(m, m, 1.0, ps, ALU.add, ALU.mult), tok, t_mg[8 + b])
            main.give(k, t)
            t_zb.append(t)
            tick()
        drain()
        src = [(Y(g)[0][:, q0:T], Y(g)[1][:, q0:T], t_at[g]) for g in range(4)]
        t_z = []
        for b in range(8):
            k, ps, tok = block("w_a", l, 128 * b, src, nq)
            m, zb = mg[:, b, q0:T], mg[:, 8 + b, q0:T]
            t1 = D.do(lambda e, ps=ps, m=m: e.scalar_tensor_tensor(m, m, 1.0, ps, ALU.add, ALU.mult), tok, t_mg[b])
            main.give(k, t1)
            t2 = D.do(lambda e, zb=zb, m=m: e.tensor_tensor(m, m, zb, ALU.add), t1, t_zb[b])
            zh, zl = Y(12 + b)
            zh, zl = zh[:, q0:T], zl[:, q0:T]
            t3 = A.do(lambda e, m=m, zh=zh: e.activation(zh, m, ACT.Copy), t2)
            t4 = later(D, lambda e: e.tensor_tensor(zl, m, zh.bitcast(F), ALU.subtract), t3)
            t_z.append([t3, t4])
        src = [(Y(12 + b)[0][:, q0:T], Y(12 + b)[1][:, q0:T], t_z[b]) for b in range(8)]
        nxt = Norm(nxt_norm, rows[(l + 1) % 2], q0)
        for b in range(8):
            k, ps, tok = block("w_out", l, 128 * b, src, nq)
            residual(b, ps, k, tok, 0.5, nxt, q0)
        nxt.sums()
        return nxt

    norm = layer(0, norm, "ng1")
    norm = layer(1, norm, "f1n")

    Z = META
    Yc = lambda i: (yh[:, i * S:(i + 1) * S], yl[:, i * S:(i + 1) * S])

    def split_to(i, m, tok):
        a, b = Yc(i)
        t1 = A.do(lambda e: e.activation(a, m, ACT.Copy), tok)
        t2 = later(D, lambda e: e.tensor_tensor(b, m, a.bitcast(F), ALU.subtract), t1, tok)
        return [t1, t2]

    def ffn(name, norm, nxt):
        arena["at"] = 0
        tmp = Ring([alloc(2, S) for _ in range(3)])
        sil = Ring([alloc(S) for _ in range(3)])
        barrier()
        row = norm.row
        tr = norm.rstd(False, D.last())
        src = norm.feed()
        rb = row[:, Z:T].unsqueeze(1).broadcast_to([128, 2, S])
        ytok, hid = [], []

        def hidden():
            j, kt, kg, g, m, t2 = hid.pop(0)
            t3 = D.do(lambda e: e.tensor_tensor(g, g, m[:, 1, :], ALU.mult), t2)
            tmp.give(kt, t3)
            tt = split_to(j, g, t3)
            sil.give(kg, *tt)
            ytok.append(tt)

        for j in range(22):
            k, b, free = main.take()
            block(name + "_gu", 0, 128 * j, src, S, b[:, 0:S], free)
            _, _, tok = block(name + "_gu", 0, 2816 + 128 * j, src, S, b[:, S:2 * S], [])
            kt, m, fm = tmp.take()
            t1 = D.do(lambda e, m=m, b=b: e.tensor_tensor(
                m, b[:, :].rearrange("p (a s) -> p a s", a=2), rb, ALU.mult), tok, tr, *fm)
            main.give(k, t1)
            kg, g, fg = sil.take()
            t2 = A.do(lambda e, m=m, g=g: e.activation(g, m[:, 0, :], ACT.Silu), t1, *fg)
            hid.append((j, kt, kg, g, m, t2))
            if j:
                hidden()
        hidden()
        src = [(*Yc(j), ytok[j]) for j in range(22)]
        nxt = nxt()
        for b in range(8):
            k, ps, tok = block(name + "_dn", 0, 128 * b, src, S)
            residual(b, ps, k, tok, 0.5, nxt, Z)
        nxt.sums()
        return nxt

    norm = ffn("f1", norm, lambda: Norm("mxn", rows[1], Z, late=True))

    def mixer(norm):
        arena["at"] = 0
        zacc = alloc(8, S)
        xsT = [alloc(4, S) for _ in range(2)]
        BC = [alloc(2, S) for _ in range(2)]
        zs = [alloc(4, S) for _ in range(2)]
        xdt = alloc(2, 512)
        btok = alloc(128)
        xw = alloc(512)
        cbm = alloc(2, 128)
        prev = alloc(512)
        M = alloc(8, 256)
        E8 = alloc(8, 128)
        cin = Ring([alloc(3 + S) for _ in range(3)])
        cv = Ring([alloc(S) for _ in range(3)])
        tmp = Ring([alloc(S) for _ in range(3)])
        dtT, acs, dq = alloc(S), alloc(S), alloc(S)
        dden = dq[:, 0:128]
        tokm = alloc(5, 32)
        negA = alloc(2, 32)
        identb, maskb = tens["cnb"][:, 0:128], tens["cnb"][:, 128:384]
        acol = alloc(1)
        grow = rows[0][:, 0:S]
        barrier()
        norm.rstd(False, D.last())
        norm.apply(tmp)
        src = norm.feed()
        cwh, cbh, snh = (prm[:, PARAMS[n]:PARAMS[n] + w] for n, w in (("cw", 96), ("cb", 24), ("sn", 16)))
        t = D.do(lambda e: e.tensor_scalar(cwh, cwh, 0.5, None, ALU.mult))
        t = D.do(lambda e: e.tensor_scalar(cbh, cbh, 0.5, None, ALU.mult))
        t_half = D.do(lambda e: e.tensor_scalar(snh, snh, 0.5, None, ALU.mult))
        tc = [D.do(lambda e, b=b: e.memset(b[:, 0:3], 0.0)) for b in cin.bufs]

        k, ps, tok = block("w_in2", 0, [(8192, 32, 0)], src, S)
        d, ac, q = dtT[0:32, :], acs[0:32, :], dq[0:32, :]
        u = cin.bufs[0][0:32, 3:3 + S]
        v = cin.bufs[1][0:32, 3:3 + S]
        w = cin.bufs[2][0:32, 3:3 + S]
        t = D.do(lambda e: e.tensor_scalar(d, ps[0:32, :], pc("dtb", 0, 32), None, ALU.add), tok)
        main.give(k, t)
        t1 = A.do(lambda e: e.activation(u, d, ACT.Abs), t)
        t1 = A.do(lambda e: e.activation(u, u, ACT.Exp, scale=-1.0), t1)
        t2 = A.do(lambda e: e.activation(acol[0:32, :], pc("alog", 0, 32), ACT.Exp))
        t = D.do(lambda e: e.tensor_scalar(d, d, 0.0, None, ALU.max), t1)
        t1 = D.do(lambda e: e.tensor_scalar(v, u, 1.0, None, ALU.add), t1)
        t3 = A.do(lambda e: e.activation(w, v, ACT.Ln), t1)
        t1 = D.do(lambda e: e.tensor_scalar(v, v, -1.0, None, ALU.add), t3)
        t4 = D.do(lambda e: e.tensor_scalar(ac, v, 0.0, None, ALU.is_equal), t1)
        t1 = D.do(lambda e: e.tensor_tensor(v, v, ac, ALU.add), t4)
        t1 = D.do(lambda e: e.reciprocal(q, v), t1)
        t1 = D.do(lambda e: e.tensor_tensor(w, w, q, ALU.mult), t1)
        t1 = D.do(lambda e: e.tensor_tensor(w, w, ac, ALU.add), t1)
        t1 = D.do(lambda e: e.tensor_tensor(w, w, u, ALU.mult), t1)
        t = D.do(lambda e: e.tensor_tensor(d, d, w, ALU.add), t1, t)
        t_dt = t
        t = D.do(lambda e: e.tensor_scalar(q, d, acol[0:32, :], -1.0, ALU.mult, ALU.mult), t2, t)
        for c in range(2):
            t = D.do(lambda e, c=c: e.tensor_tensor_scan(
                ac[:, 128 * c:128 * c + 128], ones[0:32, :], q[:, 128 * c:128 * c + 128], 0.0,
                ALU.mult, ALU.add), t)
        t_ac = t
        t_de = A.do(lambda e: e.activation(dden[0:32, :], ac[:, 0:128], ACT.Exp, scale=-1.0, bias=ac[:, 127:128]), t_ac)
        t_cin = t_ac

        def to_tokens():
            ks, sb_, fs = side.take()
            P.wait(*fs, t_dt, t_ac, t_de)
            for i, a in enumerate((d[:, 0:128], d[:, 128:256], ac[:, 0:128], ac[:, 128:256], dden[0:32, :])):
                tp = P.do(lambda e, i=i, a=a: e.transpose(sb_[:, 32 * i:32 * i + 32], a, ident[0:32, 0:32]))
            t = A.do(lambda e: e.activation(tokm, sb_[:, 0:160].rearrange("p (a b) -> p a b", b=32), ACT.Copy), tp)
            side.give(ks, t)
            return D.do(lambda e: e.tensor_scalar(negA, tokm[:, 2:4, :], -1.0, None, ALU.mult), t)

        cin.free = [(i, [t_cin]) for i in range(3)]

        yat = []
        for j in range(8):
            k1, p1, tok1 = block("w_in2", 0, 1024 + 128 * j, src, S)
            kt, m, fm = tmp.take()
            t1 = A.do(lambda e: e.activation(m, p1, ACT.Copy), tok1, *fm)
            main.give(k1, t1)
            k2, p2, tok2 = block("w_in2", 0, 2048 + 128 * j, src, S)
            kc, ci, fc = cin.take()
            t2 = D.do(lambda e, ci=ci, m=m, p2=p2: e.tensor_tensor(ci[:, 3:3 + S], m, p2, ALU.mult), t1, tok2, *fc, *tc)
            main.give(k2, t2)
            wc = lambda i, j=j: pc("ca", 8 * i + j)
            t = D.do(lambda e, m=m, ci=ci, w=wc(2): e.tensor_scalar(m, ci[:, 3:3 + S], w, None, ALU.mult), t2)
            for i in (1, 0):
                t = D.do(lambda e, m=m, ci=ci, w=wc(i), i=i: e.scalar_tensor_tensor(
                    m, ci[:, 1 + i:1 + i + S], w, m, ALU.mult, ALU.add), t)
            cin.give(kc, t)
            k3, p3, tok3 = block("w_in2", 0, 128 * j, src, S)
            t = D.do(lambda e, m=m, p3=p3: e.tensor_tensor(m, m, p3, ALU.mult), t, tok3)
            main.give(k3, t)
            tt = split_to(16 + j, m, t)
            tmp.give(kt, *tt)
            yat.append(tt)
            if j == 1:
                t_tok = to_tokens()

        def sig(b, col, dst):
            k, ps, tok = block("w_in2", 0, col + 128 * b, src, S)
            t2 = A.do(lambda e: e.activation(dst, ps, ACT.Tanh, scale=0.5), tok)
            main.give(k, t2)
            return t2

        tza = [sig(b, 8224, zacc[:, b, :]) for b in range(8)]
        srca = [(*Yc(16 + j), yat[j]) for j in range(8)]
        for b in range(8):
            k, ps, tok = block("w_oa", 0, 128 * b, srca, S)
            z = zacc[:, b, :]
            t = D.do(lambda e, z=z, ps=ps: e.scalar_tensor_tensor(z, z, 1.0, ps, ALU.add, ALU.mult), tok, tza[b])
            main.give(k, t)
            tza[b] = t

        def conv(cb, dst, *free):
            k, ps, tok = block("w_in2", 0, 5120 + 128 * cb, src, S)
            kc, ci, fc = cin.take()
            t = A.do(lambda e: e.activation(ci[:, 3:3 + S], ps, ACT.Copy), tok, *fc)
            main.give(k, t)
            return [cb, kc, ci, dst, t, free]

        def taps(items):
            out = []
            for it in items:
                cb, kc, ci, dst, t, free = it
                kv, s, fv = cv.take()
                it[5] = (kv, s, free)
                w, b_ = cwh[:, 72 + cb:73 + cb], cbh[:, cb:cb + 1]
                it[4] = D.do(lambda e: e.tensor_scalar(s, ci[:, 3:3 + S], w, b_, ALU.mult, ALU.add), t, *fv, t_half)
            for i in (2, 1, 0):
                for it in items:
                    cb, kc, ci, dst, t, (kv, s, free) = it
                    w = cwh[:, 24 * i + cb:24 * i + cb + 1]
                    it[4] = D.do(lambda e: e.scalar_tensor_tensor(s, ci[:, i:i + S], w, s, ALU.mult, ALU.add), t)
            for cb, kc, ci, dst, t, (kv, s, free) in items:
                cin.give(kc, t)
                t2 = A.do(lambda e: e.activation(dst, s, ACT.Tanh), t, *free)
                t3 = later(D, lambda e: e.scalar_tensor_tensor(dst, dst, 1.0, s, ALU.add, ALU.mult), t2)
                cv.give(kv, t3)
                out.append(t3)
            return out

        grp_done = {}

        def ssd(g, tx, tbc, tz):
            x, (BT, CT), z = xsT[g % 2], (BC[g % 2][:, 0, :], BC[g % 2][:, 1, :]), zs[g % 2]
            hs = slice(8 * g, 8 * g + 8)
            prior = grp_done.get(g - 1, [])
            tk_ = []
            for c in range(2):
                ks, sb_, fs = side.take()
                P.wait(*fs, *tx)
                for b in range(4):
                    tp = P.do(lambda e, b=b, c=c, sb_=sb_: e.transpose(
                        sb_[:, 128 * b:128 * b + 128], x[:, b, 128 * c:128 * c + 128], ident))
                dtb = tokm[:, c, hs].unsqueeze(2).broadcast_to([128, 8, 64])
                t = D.do(lambda e, c=c, sb_=sb_, dtb=dtb: e.tensor_tensor(
                    xdt[:, c, :].rearrange("p (h q) -> p h q", q=64),
                    sb_[:, :].rearrange("p (h q) -> p h q", q=64), dtb, ALU.mult), tp, t_tok, *prior)
                side.give(ks, t)
                tk_.append(t)
            deb = tokm[:, 4, hs].unsqueeze(2).broadcast_to([128, 8, 64])
            t_xw = D.do(lambda e: e.tensor_tensor(
                xw.rearrange("p (h q) -> p h q", q=64), xdt[:, 0, :].rearrange("p (h q) -> p h q", q=64),
                deb, ALU.mult), tk_[0])
            ks, sb_, fs = side.take()
            P.wait(*fs, *tbc)
            P.put(lambda e, sb_=sb_: e.transpose(sb_[:, 256:384], BT[:, 0:128], ident))
            for c in range(2):
                cs = slice(128 * c, 128 * c + 128)
                tp = P.do(lambda e, sb_=sb_, cs=cs: e.matmul(sb_[:, cs], BT[:, cs], CT[:, cs], start=True, stop=True))
            t_bt = A.do(lambda e, sb_=sb_: e.activation(btok, sb_[:, 256:384], ACT.Copy), tp, *prior)
            t_cb = D.do(lambda e, sb_=sb_: e.tensor_tensor(
                cbm, sb_[:, 0:256].rearrange("p (a b) -> p a b", a=2),
                cst[:, C_CM:C_CM + 256].rearrange("p (a b) -> p a b", a=2), ALU.mult), tp, t_bt, *prior)
            side.give(ks, t_cb, t_bt)
            yield
            ks, sb_, fs = side.take()
            tp = P.do(lambda e, sb_=sb_: e.matmul(sb_[:, :], btok, xw, start=True, stop=True), t_bt, t_xw, *fs)
            t_pv = A.do(lambda e, sb_=sb_: e.activation(prev, sb_[:, :], ACT.Copy), tp, *prior)
            side.give(ks, t_pv)
            tM, tE = [], []
            for hp in range(4):
                ks, sb_, fs = side.take()
                P.wait(*fs, t_ac)
                for i in range(2):
                    hd = 8 * g + 2 * hp + i
                    sel, o = ident[0:32, hd:hd + 1].broadcast_to([32, 128]), sb_[:, S * i:S * i + S]
                    tr_ = P.do(lambda e: e.matmul(o, sel, acs[0:32, :], start=(i == 0), stop=False,
                                                  skip_group_check=True))
                t1 = A.do(lambda e: e.activation(
                    E8[:, 2 * hp:2 * hp + 2, :], sb_[:, :].rearrange("p (a s) -> p a s", a=2)[:, :, 128:256],
                    ACT.Exp), tr_, *prior)
                P.wait(t1)
                for i in range(2):
                    o = sb_[:, S * i:S * i + S]
                    tr_ = P.do(lambda e: e.matmul(o, identb, maskb, start=False, stop=True, skip_group_check=True))
                for i in range(2):
                    for c in range(2):
                        hd = 8 * g + 2 * hp + i
                        cs = slice(128 * c, 128 * c + 128)
                        bi = negA[:, c, hd:hd + 1]
                        t2 = A.do(lambda e: e.activation(
                            M[:, 2 * hp + i, cs], sb_[:, S * i + 128 * c:S * i + 128 * c + 128], ACT.Exp,
                            bias=bi), tr_, t_tok, *prior)
                side.give(ks, t1, t2)
                tE.append(t1)
                cbb = cbm.rearrange("p a b -> p (a b)").unsqueeze(1).broadcast_to([128, 2, 256])
                t4 = G.do(lambda e: e.tensor_tensor(
                    M[:, 2 * hp:2 * hp + 2, :], M[:, 2 * hp:2 * hp + 2, :], cbb, ALU.mult), t2, t_cb)
                tM.append(t4)
                yield
            ctb = CT[:, 128:256].unsqueeze(1).broadcast_to([128, 8, 128])
            t_E = D.do(lambda e: e.tensor_tensor(E8, E8, ctb, ALU.mult), *tE)
            yield
            t_y = []
            for half in range(2):
                ks, sb_, fs = side.take()
                P.wait(*fs, *tk_, *tM, t_pv, t_E)
                for hp in range(2 * half, 2 * half + 2):
                    for c in range(2):
                        for i in range(2):
                            hd = 2 * hp + i
                            o = sb_[64 * i:64 * i + 64, S * (hp - 2 * half) + 128 * c:S * (hp - 2 * half) + 128 * c + 128]
                            tp = P.do(lambda e, o=o, c=c, hd=hd: e.matmul(
                                o, xdt[:, c, 64 * hd:64 * hd + 64], M[:, hd, 128 * c:128 * c + 128],
                                start=True, stop=(c == 0)))
                            if c == 1:
                                tp = P.do(lambda e, o=o, hd=hd: e.matmul(
                                    o, prev[:, 64 * hd:64 * hd + 64], E8[:, hd, :], start=False, stop=True))
                for b in range(2):
                    bb = 2 * half + b
                    yb = x[:, bb, :]
                    t1 = D.do(lambda e, sb_=sb_, b=b, bb=bb, yb=yb: e.scalar_tensor_tensor(
                        yb, x[:, bb, :], pc("sd", 4 * g + bb), sb_[:, S * b:S * b + S], ALU.mult, ALU.add), tp, *prior)
                    t_y.append(t1)
                side.give(ks, t1)
                for bb in (2 * half, 2 * half + 1):
                    yb = x[:, bb, :]
                    t_y[bb] = D.do(lambda e: e.tensor_tensor(yb, yb, z[:, bb, :], ALU.mult), t_y[bb], tz[bb])
                yield
            kq, qb, fq = side.take()
            for bb in range(4):
                k2, sq, f2 = sqb.take()
                t3 = A.do(lambda e: e.activation(sq[:, 0:S], x[:, bb, :], ACT.Square), t_y[bb], *f2)
                for j in range(2):
                    t5 = P.do(lambda e: e.matmul(
                        qb[:, j:j + 1], sq[:, 128 * j:128 * j + 128], ones[:, 0:1], start=(bb == 0 and j == 0),
                        stop=(bb == 3), skip_group_check=True), t3, *fq)
                sqb.give(k2, t5)
            yield
            c3, q3 = cols3[0][:, 0:2], cols3[2][:, 0:2]
            t = A.do(lambda e: e.activation(q3, qb[:, 0:2], ACT.Sqrt, scale=1.0 / 2048, bias=eps), t5, D.last())
            t = D.do(lambda e: e.reciprocal(c3, q3), t)
            side.give(kq, t)
            yield
            kq, qb, fq = side.take()
            for j in range(2):
                t5 = P.do(lambda e: e.matmul(qb[:, 128 * j:128 * j + 128], c3[:, j:j + 1].broadcast_to([128, 128]),
                                             ident, start=True, stop=True), t, *fq)
            t = A.do(lambda e: e.activation(grow, qb[:, 0:S], ACT.Copy), t5, *prior)
            side.give(kq, t)
            yield
            last = []
            for bb in range(4):
                yb = x[:, bb, :]
                t1 = D.do(lambda e, yb=yb, bb=bb: e.scalar_tensor_tensor(
                    yb, yb, snh[:, 4 * g + bb:4 * g + bb + 1], grow, ALU.mult, ALU.mult), t)
                yt[4 * g + bb] = split_to(4 * g + bb, yb, t1)
                last += yt[4 * g + bb]
            flush()
            grp_done[g] = last + [tp]

        yt = [None] * 16
        for g in range(4):
            old = grp_done.get(g - 2, [])
            bc = BC[g % 2]
            dsts = [(16 + g, bc[:, 0, :]), (20 + g, bc[:, 1, :])] + [
                (4 * g + b, xsT[g % 2][:, b, :]) for b in range(4)]
            tt = []
            for p in range(3):
                items = []
                for cb, dst in dsts[2 * p:2 * p + 2]:
                    items.append(conv(cb, dst, *old))
                    if len(items) == 2:
                        tt += taps(items)
                    tick()
            tbc, tx = tt[0:2], tt[2:6]
            tz = []
            for b in range(4):
                k, ps, tok = block("w_in2", 0, 3072 + 128 * (4 * g + b), src, S)
                zb = zs[g % 2][:, b, :]
                t2 = A.do(lambda e: e.activation(zb, ps, ACT.Tanh, scale=0.5), tok, *old)
                t3 = later(D, lambda e: e.scalar_tensor_tensor(zb, zb, 1.0, ps, ALU.add, ALU.mult), t2)
                main.give(k, t3)
                tz.append(t3)
                tick()
            drain()
            active.append(ssd(g, tx, tbc, tz))
        tsb = []
        sgb = [(xsT[0] if b < 4 else zs[0])[:, b % 4, :] for b in range(8)]
        D.wait(*grp_done[2])
        A.wait(*grp_done[2])
        for b in range(8):
            tsb.append(sig(b, 9248, sgb[b]))
            tick()
        drain()
        srcb = [(*Yc(j), yt[j]) for j in range(16)]
        tmg = []
        for b in range(8):
            k, ps, tok = block("w_os", 0, 128 * b, srcb, S)
            z, s = zacc[:, b, :], sgb[b]
            t = D.do(lambda e, s=s, ps=ps: e.scalar_tensor_tensor(s, s, 1.0, ps, ALU.add, ALU.mult), tok, tsb[b])
            main.give(k, t)
            t = D.do(lambda e, s=s, z=z: e.tensor_tensor(z, z, s, ALU.add), t, tza[b])
            tmg.append(split_to(16 + b, z, t))
        srcm = [(*Yc(16 + b), tmg[b]) for b in range(8)]
        nxt = Norm("xn", rows[0], Z)
        for b in range(8):
            k, ps, tok = block("w_mo", 0, 128 * b, srcm, S)
            residual(b, ps, k, tok, 0.5, nxt, Z)
        return nxt

    norm = mixer(norm)

    def cross(norm):
        arena["at"] = 0
        mem_sb = alloc(8, S)
        kTt, qTt = alloc(8, S), alloc(8, S)
        V = alloc(2, 1024)
        Pm = alloc(2, 2, S)
        PTx = Ring([alloc(2, S) for _ in range(2)])
        nm, sm, rs = alloc(2, 4), alloc(2, 4), alloc(2, 4)
        mrow = rows[1][:, 0:S]
        barrier()
        SP.put(lambda e: e.dma_start(mem_sb, mem, sems["l_m"]), D.last(), A.last(), P.last())
        lm = (sems["l_m"], 16)
        tr = norm.rstd(False, D.last())
        row = norm.row[:, Z:T]
        mh = yh[:, 0:8 * S].rearrange("p (c s) -> p c s", c=8)
        ml = yl[:, 0:8 * S].rearrange("p (c s) -> p c s", c=8)
        mn = Norm("mn", mrow, 0, mem_sb, mh, ml)
        for c in range(8):
            mn.chunk(c, lm)
            mn.sums()
        tm = mn.rstd(False, D.last())
        srcm = mn.feed()
        tk = []
        for b in range(8):
            k, ps, tok = block("w_kv", 0, 128 * b, srcm, S)
            t = D.do(lambda e, b=b, ps=ps: e.tensor_tensor(kTt[:, b, :], ps, mrow, ALU.mult), tok, tm)
            main.give(k, t)
            tk.append(t)
        rt2, t_r2 = mn.col, mn.ctok
        flush()
        tv = []
        for hf in range(2):
            pair = [main.take() for _ in range(2)]
            for c in range(8):
                ws = [tile(("w_kv", 0, 128 * c, [(1024 + 512 * hf + 128 * i, 128, 0)])) for i in range(4)]
                q = (len(plan) - 1) // TILES % NSPL
                j0 = (len(plan) - 4) % TILES
                wh, wl = (w[:, q, 128 * j0:128 * j0 + 512] for w in (whi, wlo))
                for mt in range(2):
                    k, b, free = pair[mt]
                    P.wait(*free)
                    a = (mh[:, c, 128 * mt:128 * mt + 128], ml[:, c, 128 * mt:128 * mt + 128])
                    tok = mm3(b[:, :], a, (wh, wl), c == 0, c == 7, True)
                if ws[3][2] is not None:
                    pe_done[ws[3][2]] = tok
            for mt in range(2):
                k, b, _ = pair[mt]
                t = D.do(lambda e, mt=mt, b=b: e.tensor_scalar(
                    V[:, mt, 512 * hf:512 * hf + 512], b[:, :], rt2[:, mt:mt + 1], None, ALU.mult), tok, t_r2)
                main.give(k, t)
                tv.append(t)
        src = norm.feed()
        tq = []
        t_o = [None] * 8

        def head(hd):
            tn = []
            for st in range(2):
                ks, sb_, fs = side.take()
                P.wait(*fs, *tq, *tk)
                for b in range(2):
                    tp = P.do(lambda e, b=b, st=st, sb_=sb_: e.matmul(
                        sb_[:, 0:S], qTt[:, 2 * hd + b, 128 * st:128 * st + 128], kTt[:, 2 * hd + b, :],
                        start=(b == 0), stop=(b == 1)))
                n1 = nm[:, st, hd:hd + 1]
                t = D.do(lambda e, sb_=sb_, n1=n1: e.tensor_reduce(n1, sb_[:, 0:S], AX, ALU.max, negate=True), tp)
                t = D.do(lambda e, n1=n1: e.tensor_scalar(n1, n1, 1.0 / 16, None, ALU.mult), t)
                te = A.do(lambda e, sb_=sb_, st=st, n1=n1: e.activation(
                    Pm[:, st, hd % 2, :], sb_[:, 0:S], ACT.Exp, scale=1.0 / 16, bias=n1,
                    accum_out=sm[:, st, hd:hd + 1]), t, *xdone.get(hd - 2, []))
                side.give(ks, te)
                t = D.do(lambda e, st=st: e.reciprocal(rs[:, st, hd:hd + 1], sm[:, st, hd:hd + 1]), te)
                tn.append(D.do(lambda e, st=st: e.tensor_scalar(
                    Pm[:, st, hd % 2, :], Pm[:, st, hd % 2, :], rs[:, st, hd:hd + 1], None, ALU.mult), t))
            yield
            ks, sb_, fs = side.take()
            P.wait(*fs, *tn)
            for mc in range(2):
                for st in range(2):
                    tp = P.do(lambda e, mc=mc, st=st: e.transpose(
                        sb_[:, 256 * mc + 128 * st:256 * mc + 128 * st + 128],
                        Pm[:, st, hd % 2, 128 * mc:128 * mc + 128], ident))
            xdone[hd] = [tp]
            kp, pt, fp = PTx.take()
            t = A.do(lambda e: e.activation(pt, sb_[:, :].rearrange("p (a b) -> p a b", a=2), ACT.Copy), tp, *fp)
            side.give(ks, t)
            yield
            ks, sb2, fs = side.take()
            P.wait(*fs, t, *tv)
            for db in range(2):
                for mc in range(2):
                    tp = P.do(lambda e, db=db, mc=mc: e.matmul(
                        sb2[:, S * db:S * db + S], V[:, mc, 256 * hd + 128 * db:256 * hd + 128 * db + 128],
                        pt[:, mc, :], start=(mc == 0), stop=(mc == 1)))
            PTx.give(kp, tp)
            yield
            a, b = (y[:, (8 + 2 * hd) * S:(10 + 2 * hd) * S] for y in (yh, yl))
            t1 = A.do(lambda e: e.activation(a, sb2[:, :], ACT.Copy), tp)
            t2 = D.do(lambda e: e.tensor_tensor(b, sb2[:, :], a.bitcast(F), ALU.subtract), t1)
            t_o[2 * hd] = t_o[2 * hd + 1] = [t1, t2]
            side.give(ks, t2)

        xdone = {}
        for b in range(8):
            k, ps, tok = block("w_q", 0, 128 * b, src, S)
            t = D.do(lambda e, b=b, ps=ps: e.tensor_tensor(qTt[:, b, :], ps, row, ALU.mult), tok, tr)
            main.give(k, t)
            tq.append(t)
            if b % 2:
                active.append(head(b // 2))
            tick()
        drain()
        srco = [(*Yc(8 + j), t_o[j]) for j in range(8)]
        nxt = Norm("f2n", rows[1], Z)
        for b in range(8):
            k, ps, tok = block("w_o", 0, 128 * b, srco, S)
            residual(b, ps, k, tok, 1.0, nxt, Z)
        nxt.sums()
        return nxt

    norm = cross(norm)
    norm = ffn("f2", norm, lambda: Norm("fn", rows[0], Z))
    norm.sums()
    tr = norm.rstd(False, D.last())
    for c in range(8):
        hc = h[:, c, Z:T]
        t = D.do(lambda e, hc=hc, c=c: e.scalar_tensor_tensor(
            hc, hc, pc("fn", c), norm.row[:, Z:T], ALU.mult, ALU.mult), tr, *norm.tok[c])
        if c % 4 == 3:
            c0 = c - 3
            SP.put(lambda e, c0=c0: e.dma_start(out[:, c0:c0 + 4, :], h[:, c0:c0 + 4, Z:T], sems["o"]), t)
    SP.wait((sems["o"], 32))
    return P, D, A, SP, G, arena["top"]


ARENA = 16072


def program(nc, wts_shape_decl, small, par, con, mem, out):
    with ExitStack() as ctx:
        def sb(name, shape, dt=F):
            return ctx.enter_context(nc.sbuf_tensor(name, shape, dt))

        names = ["pe", "dve", "act", "sp", "pool", "l_h", "l_c", "l_p", "l_m", "o"] + [f"w{i}" for i in range(NRAW)]
        sems = {n: ctx.enter_context(nc.semaphore(n)) for n in names}
        tens = {
            "raw": sb("raw", [128, NRAW, SLOT]), "whi": sb("whi", [128, NSPL, SLOT], R),
            "wlo": sb("wlo", [128, NSPL, SLOT], R), "h": sb("h", [128, 8, T]),
            "xh": sb("xh", [128, 8, T], R), "xl": sb("xl", [128, 8, T], R),
            "yh": sb("yh", [128, YCOLS], R), "yl": sb("yl", [128, YCOLS], R),
            "cst": sb("cst", [128, NCONST]), "prm": sb("prm", [128, NPARAM]), "ar": sb("ar", [128, ARENA]),
            "cnb": sb("cnb", [128, 384], mybir.dt.bfloat16),
            "sq": sb("sq", [128, 2, T]), "rows": sb("rows", [128, 2, T]),
            "banks": [ctx.enter_context(nc.psum_tensor(f"bank{i}", [128, 512], F)) for i in range(8)],
        }
        plan = []
        build(nc, None, small, par, con, mem, out, 10 ** 6, plan, tens, sems)
        nslots = -(-len(plan) // TILES)
        wts = wts_shape_decl(nslots)
        again = []
        P, D, A, SP, G, top = build(nc, wts, small, par, con, mem, out, nslots, again, tens, sems)
        assert top <= ARENA, top
        assert len(again) == len(plan)
        block = ctx.enter_context(nc.Block())

        @block.sync
        def _(e):
            SP.run(e)

        @block.tensor
        def _(e):
            P.run(e)

        @block.gpsimd
        def _(e):
            G.run(e)

        @block.vector
        def _(e):
            D.run(e)

        @block.scalar
        def _(e):
            A.run(e)
    return plan, nslots


def kernel(**inputs):
    import concourse.bacc as _bacc
    from concourse.bass_utils import run_bass_kernel_spmd as _run

    a = {n: np.asarray(v) for n, v in inputs.items()}
    nc = _bacc.Bacc("TRN2", target_bir_lowering=False, num_devices=1)

    def dram(name, shape, kind="ExternalInput"):
        return nc.dram_tensor(name, shape, F, kind=kind).ap()

    small, par, con = dram("x_dram", [128, 8, T]), dram("par_dram", [128, NPARAM]), dram("con_dram", [128, NCONST])
    mem, out = dram("mem_dram", [128, 8, S]), dram("out_dram", [128, 8, S], "ExternalOutput")
    plan, nslots = program(nc, lambda n: dram("w_dram", [n, 128, SLOT]), small, par, con, mem, out)

    mats = {
        "w_in": a["w_in"], "pool_w": a["pool_w"].reshape(8, 128, 128), "w_a": a["w_branch_a"],
        "w_b": a["w_branch_b"], "w_out": a["w_out"], "f1_gu": a["ffn1_w_gate_up_2"], "f1_dn": a["ffn1_w_down_2"],
        "w_in2": a["w_in_2"], "w_oa": a["w_out_a_2"], "w_os": a["w_out_ssm_2"], "w_mo": a["w_mix_out_2"],
        "w_q": a["w_q_2"], "w_kv": a["w_kv_2"], "w_o": a["w_o_x_2"], "f2_gu": a["ffn2_w_gate_up_2"],
        "f2_dn": a["ffn2_w_down_2"],
    }
    w = np.zeros((nslots, 128, SLOT), np.float32)
    for n, item in enumerate(plan):
        if item is None:
            continue
        name, l, r0, cols = item
        s, j = divmod(n, TILES)
        for c0, width, at in cols:
            w[s, :, 128 * j + at:128 * j + at + width] = mats[name][l, r0:r0 + 128, c0:c0 + width]

    def cols(v, n):
        return np.asarray(v).reshape(n, 128).T

    p = np.zeros((128, NPARAM), np.float32)

    def put(name, v):
        p[0:v.shape[0], PARAMS[name]:PARAMS[name] + v.shape[1]] = v

    for l in range(2):
        put(f"ng{l}", cols(a["norm_gain"][l], 8))
        put(f"qn{l}", np.concatenate([a["q_norm_gain"][l]] * 2)[:, None])
        put(f"kn{l}", np.concatenate([a["k_norm_gain"][l]] * 2)[:, None])
        put(f"pb{l}", cols(a["pool_b"][l], 4))
        put(f"ps{l}", cols(a["pool_scale"][l], 4))
    put("f1n", cols(a["ffn1_norm_2"][0], 8))
    put("mxn", cols(a["mix_norm_2"][0], 8))
    put("ca", np.concatenate([cols(a["conv_a_w_2"][0, i], 8) for i in range(3)], 1))
    put("cw", np.concatenate([cols(a["ssm_conv_w_2"][0, i], 24) for i in range(4)], 1))
    put("cb", cols(a["ssm_conv_b_2"][0], 24))
    put("sd", cols(np.repeat(a["ssm_d_2"][0], 64), 16))
    put("sn", cols(a["ssm_norm_2"][0], 16))
    put("xn", cols(a["xattn_norm_2"][0], 8))
    put("mn", cols(a["mem_norm_2"][0], 8))
    put("f2n", cols(a["ffn2_norm_2"][0], 8))
    put("fn", cols(a["final_norm_2"], 8))
    put("dtb", a["ssm_dt_bias_2"][0][:, None])
    put("alog", a["ssm_a_log_2"][0][:, None])

    def fm(x):
        return np.ascontiguousarray(x.reshape(x.shape[0], 8, 128).transpose(2, 1, 0))

    arrays = {
        "x_dram": fm(np.concatenate([a["meta_tokens"], a["x"][0]], 0)), "par_dram": p, "con_dram": constants(),
        "mem_dram": fm(a["mem_2"][0]), "w_dram": w,
    }
    r = _run(nc, [arrays], core_ids=[0])
    o = np.asarray(r.results[0]["out_dram"])
    return np.ascontiguousarray(o.transpose(2, 1, 0)).reshape(1, S, 1024)
```

```python
from contextlib import ExitStack

import numpy as np

import concourse.bass as bass
from concourse import mybir

F = mybir.dt.float32
R = mybir.dt.float32r
ALU = mybir.AluOpType
ACT = mybir.ActivationFunctionType
AX = mybir.AxisListType.X

T = 272
S = 256
META = 16
EPS = 1e-6
NEG = -1e30
TILES = 8
SLOT = TILES * 128
NRAW = 4
NSPL = 5
LOOK = 3
YCOLS = 24 * 256

C_ID, C_ONE, C_EPS = 0, 128, 256
C_R3 = 258
C_PERM = 268
C_COS, C_SIN = 396, 668
C_VA, C_VB = 940, 1084
C_CM = 1356
C_RC = 1612
C_S10 = 1676
C_B10 = 1726
NCONST = 2366

PARAMS = {}


def _param_table():
    at = 0
    for name, n in (("ng0", 8), ("ng1", 8), ("qn0", 1), ("qn1", 1), ("kn0", 1), ("kn1", 1),
                    ("pb0", 4), ("pb1", 4), ("ps0", 4), ("ps1", 4), ("f1n", 8), ("mxn", 8),
                    ("ca", 24), ("cw", 96), ("cb", 24), ("sd", 16), ("sn", 16), ("xn", 8),
                    ("mn", 8), ("f2n", 8), ("fn", 8), ("dtb", 1), ("alog", 1)):
        PARAMS[name] = at
        at += n
    return at


NPARAM = _param_table()


def constants():
    c = np.zeros((128, NCONST), np.float32)
    p = np.arange(128)
    c[p, C_ID + p] = 1.0
    c[:, C_ONE:C_ONE + 128] = 1.0
    for m in range(128):
        if m % 64 < 32:
            c[m + 32, C_PERM + m] = -1.0
        else:
            c[m - 32, C_PERM + m] = 1.0
    inv = (1.0 / (np.float32(10000.0) ** (np.arange(0, 64, 2, dtype=np.float32) / np.float32(64)))).astype(np.float32)
    ang = np.arange(T, dtype=np.float32)[:, None] * inv[None, :]
    ang = np.concatenate([ang, ang], -1).astype(np.float32)
    c[:, C_COS:C_COS + T] = np.tile(np.cos(ang).astype(np.float32).T, (2, 1))
    c[:, C_SIN:C_SIN + T] = np.tile(np.sin(ang).astype(np.float32).T, (2, 1))

    def chunk(x):
        return np.where(x < META, 0, 1 + (x - META) // 64)

    keys = np.arange(T)
    for base, q0, nk in ((C_VA, META, 144), (C_VB, META + 128, T)):
        vis = chunk(keys[:nk])[None, :] <= chunk(q0 + p)[:, None]
        c[:, base:base + nk] = np.where(vis, 0.0, NEG)
    causal = p[:, None] <= p[None, :]
    for half in range(2):
        c[:, C_CM + 128 * half:C_CM + 128 * half + 128] = causal
    for g in range(4):
        c[:, C_RC + 16 * g:C_RC + 16 * g + 16] = 1.0 / np.minimum(np.arange(1, 17), 2 << g)
    for b in range(5):
        c[0:64, C_S10 + 10 * b + 2 * b] = 1.0
        c[64:128, C_S10 + 10 * b + 2 * b + 1] = 1.0
        c[2 * b, C_B10 + 128 * b:C_B10 + 128 * b + 64] = 1.0
        c[2 * b + 1, C_B10 + 128 * b + 64:C_B10 + 128 * b + 128] = 1.0
    c[:, C_EPS] = EPS
    c[:, C_EPS + 1] = 1.0
    return c


class Later:

    def matmul(self, *a, **k):
        return lambda e: e.matmul(*a, **k)

    def transpose(self, *a, **k):
        return lambda e: e.transpose(*a, **k)

    def activation(self, *a, **k):
        return lambda e: e.activation(*a, **k)

    def tensor_tensor(self, *a, **k):
        return lambda e: e.tensor_tensor(*a, **k)

    def tensor_scalar(self, *a, **k):
        return lambda e: e.tensor_scalar(*a, **k)

    def scalar_tensor_tensor(self, *a, **k):
        return lambda e: e.scalar_tensor_tensor(*a, **k)

    def tensor_copy(self, *a, **k):
        return lambda e: e.tensor_copy(*a, **k)

    def reciprocal(self, *a, **k):
        return lambda e: e.reciprocal(*a, **k)

    def tensor_reduce(self, *a, **k):
        return lambda e: e.tensor_reduce(*a, **k)

    def max(self, *a, **k):
        return lambda e: e.max(*a, **k)

    def match_replace(self, *a, **k):
        return lambda e: e.match_replace(*a, **k)

    def memset(self, *a, **k):
        return lambda e: e.memset(*a, **k)

    def tensor_tensor_scan(self, *a, **k):
        return lambda e: e.tensor_tensor_scan(*a, **k)

    def dma_start(self, dst, src, sem):
        return lambda e: e.dma_start(dst, src).then_inc(sem, 16)


LATER = Later()


class Pending(list):

    def __init__(self, settle):
        self.issued, self.settle = False, settle


class Eng:

    def __init__(self, sem):
        self.sem, self.n, self.list, self.seen = sem, 0, [], {}

    def wait(self, *toks):
        for t in toks:
            if t is None:
                continue
            if isinstance(t, Pending) and not t.issued:
                t.settle()
            if isinstance(t, list):
                self.wait(*t)
                continue
            sem, v = t
            if self.seen.get(sem.name, 0) < v:
                self.seen[sem.name] = v
                self.list.append((0, sem, v))

    def add(self, ins, *toks):
        self.wait(*toks)
        self.n += 1
        self.list.append((1, ins, self.sem))
        return (self.sem, self.n)

    def do(self, fn, *toks):
        return self.add(fn(LATER), *toks)

    def put(self, fn, *toks):
        self.wait(*toks)
        self.list.append((1, fn(LATER), None))

    def last(self):
        return (self.sem, self.n) if self.n else None

    def run(self, e):
        for kind, a, b in self.list:
            if kind == 0:
                e.wait_ge(a, b)
            elif b is None:
                a(e)
            else:
                a(e).then_inc(b, 1)


class Ring:

    def __init__(self, bufs):
        self.bufs = bufs
        self.free = [(k, []) for k in range(len(bufs))]

    def take(self):
        k, toks = self.free.pop(0)
        return k, self.bufs[k], toks

    def give(self, k, *toks):
        self.free.append((k, list(toks)))


def build(nc, wts, small, par, con, mem, out, nslots, plan, tens, sems):
    P, D, A = Eng(sems["pe"]), Eng(sems["dve"]), Eng(sems["act"])
    SP, G = Eng(sems["sp"]), Eng(sems["pool"])
    waiting = []

    def later(eng, fn, *toks):
        p = Pending(flush)
        waiting.append((p, eng, fn(LATER), toks))
        return p

    def flush():
        while waiting:
            p, eng, ins, toks = waiting.pop(0)
            p.append(eng.add(ins, *toks))
            p.issued = True

    raw, whi, wlo = tens["raw"], tens["whi"], tens["wlo"]
    h, xh, xl, yh, yl = tens["h"], tens["xh"], tens["xl"], tens["yh"], tens["yl"]
    cst, prm, ar, banks = tens["cst"], tens["prm"], tens["ar"], tens["banks"]
    ident = cst[:, C_ID:C_ID + 128]
    ones = cst[:, C_ONE:C_ONE + 128]
    eps = cst[:, C_EPS:C_EPS + 1]

    def pc(name, i=0, rows=128):
        return prm[0:rows, PARAMS[name] + i:PARAMS[name] + i + 1]

    arena = {"at": 0, "top": 0}

    def alloc(*shape):
        n = int(np.prod(shape))
        a = ar[:, arena["at"]:arena["at"] + n]
        arena["at"] += n
        arena["top"] = max(arena["top"], arena["at"])
        if len(shape) == 2:
            a = a.rearrange("p (a b) -> p a b", a=shape[0])
        if len(shape) == 3:
            a = a.rearrange("p (a b c) -> p a b c", a=shape[0], b=shape[1])
        return a

    ld = {}

    def load(key, dst, src):
        sem = sems[key]
        SP.put(lambda e: e.dma_start(dst, src, sem))
        ld[key] = (sem, 16)


    split_tok, pe_done, state = {}, {}, {"loads": 0, "splits": 0}

    def issue_load():
        i = state["loads"]
        if i >= nslots:
            return
        state["loads"] += 1
        k = i % NRAW
        if i >= NRAW:
            SP.wait(*split_tok[i - NRAW])
        sem = sems[f"w{k}"]
        SP.put(lambda e: e.dma_start(raw[:, k, :], None if wts is None else wts[i], sem))

    def issue_split():
        i = state["splits"]
        if i >= nslots:
            return
        state["splits"] += 1
        k, q = i % NRAW, i % NSPL
        landed = (sems[f"w{k}"], 16 * (i // NRAW + 1))
        freed = pe_done[i - NSPL] if i >= NSPL else None
        th = A.do(lambda e: e.activation(whi[:, q, :], raw[:, k, :], ACT.Copy), landed, freed)
        parts = [(G, 0, SLOT)] if i >= 4 else [(G, 0, SLOT // 2), (D, SLOT // 2, SLOT)]
        tl = [eng.do(lambda e: e.tensor_tensor(
            wlo[:, q, c0:c1], raw[:, k, c0:c1], whi[:, q, c0:c1].bitcast(F), ALU.subtract), landed, freed, th)
            for eng, c0, c1 in parts]
        split_tok[i] = [th, tl]
        issue_load()

    for i in range(NRAW):
        issue_load()
        if i == 0:
            load("l_c1", cst[:, 0:C_PERM], con[:, 0:C_PERM])
            load("l_p", prm[:, :], par)
            load("l_h", h[:, 0:4, :], small[:, 0:4, :])
            load("l_h2", h[:, 4:8, :], small[:, 4:8, :])
        if i == 2:
            load("l_c", cst[:, C_PERM:NCONST], con[:, C_PERM:NCONST])

    def tile(desc):
        n = len(plan)
        plan.append(desc)
        slot, j = divmod(n, TILES)
        if j == 0:
            while state["splits"] <= slot + LOOK and state["splits"] < nslots:
                issue_split()
        q = slot % NSPL
        P.wait(*split_tok.get(slot, []))
        return (whi[:, q, 128 * j:128 * j + 128], wlo[:, q, 128 * j:128 * j + 128], slot if j == TILES - 1 else None)

    def align():
        if len(plan) % TILES:
            pe_done[len(plan) // TILES] = P.last()
            plan.extend([None] * (-len(plan) % TILES))

    def mm3(o, a, b, first, last, inc):
        (ah, al), (bh, bl) = a, b
        P.put(lambda e: e.matmul(o, ah, bh, start=first, stop=False))
        P.put(lambda e: e.matmul(o, ah, bl, start=False, stop=False))
        f = lambda e: e.matmul(o, al, bh, start=False, stop=last)
        if inc:
            return P.do(f)
        P.put(f)
        return None

    main = Ring([banks[i] for i in range(4)])
    side = Ring([banks[i] for i in range(4, 8)])

    active = []

    def tick():
        for g in list(active):
            if next(g, "end") == "end":
                active.remove(g)

    def drain():
        while active:
            flush()
            tick()

    def block(name, l, col, src, n, o=None, free=None, wrap=None):
        flush()
        k, b = None, None
        if o is None:
            k, b, free = main.take()
            o = b[:, 0:n]
        P.wait(*(free or []))
        tok = None
        for i, (sh, sl, toks) in enumerate(src):
            cols = col if isinstance(col, list) else [(col, 128, 0)]
            wh, wl, ends = tile((name, l, 128 * i, cols))
            P.wait(*toks)
            lastk = i == len(src) - 1
            tok = mm3(o, (wh, wl), (sh, sl), i == 0, lastk, lastk or ends is not None)
            if ends is not None:
                pe_done[ends] = tok
        return k, o, tok

    rows = [tens["rows"][:, i, :] for i in range(2)]
    cols3 = [cst[:, C_R3 + 3 * i:C_R3 + 3 * i + 3] for i in range(3)]
    sqb = Ring([tens["sq"][:, i, :] for i in range(2)])
    xtok = [None] * 8

    class Norm:

        def __init__(self, gain, row, c0=0, src=None, xhi=None, xlo=None, late=False):
            self.gain, self.row, self.c0, self.late = gain, row, c0, late
            self.src = h if src is None else src
            self.xh = xh if xhi is None else xhi
            self.xl = xl if xlo is None else xlo
            self.k, self.bank, self.free = side.take()
            self.tok = [None] * 8
            n = self.src.shape[2]
            self.tiles = [(n - 256, 128), (n - 128, 128)] + ([(0, META)] if c0 == 0 and n > S else [])
            self.col = cols3[0 if row is rows[0] else 1]

        def chunk(self, c, *toks):
            self.split(c, *toks)
            self.square(c, *toks)

        def split(self, c, *toks):
            n = self.src.shape[2]
            hc = self.src[:, c, self.c0:n]
            if not self.late:
                a, b = self.xh[:, c, self.c0:n], self.xl[:, c, self.c0:n]
                g = pc(self.gain, c)
                t1 = A.do(lambda e: e.activation(a, hc, ACT.Copy, scale=g), *toks)
                t2 = later(D, lambda e: e.scalar_tensor_tensor(b, hc, g, a.bitcast(F), ALU.mult, ALU.subtract),
                           t1, *toks)
                self.tok[c] = [t1, t2]

        def square(self, c, *toks):
            n = self.src.shape[2]
            hc = self.src[:, c, self.c0:n]
            if c == 0:
                self.acc = self.row[:, self.c0:n]
                self.ta = A.do(lambda e: e.activation(self.acc, hc, ACT.Square), D.last(), *toks)
                return
            k, sq, free = sqb.take()
            sq = sq[:, self.c0:n]
            t3 = A.do(lambda e: e.activation(sq, hc, ACT.Square), *toks, *free)
            if c < 7:
                self.ta = later(D, lambda e: e.tensor_tensor(self.acc, self.acc, sq, ALU.add), t3, self.ta)
                sqb.give(k, self.ta)
            else:
                self.end = (k, sq, t3)

        def rstd_sums(self, newton, *free):
            flush()
            ks, sq, t3 = self.end
            for i, (x, tx) in enumerate(((self.acc, self.ta), (sq, t3))):
                for j, (t0, n) in enumerate(self.tiles):
                    t0 -= self.c0
                    self.t = P.do(lambda e: e.matmul(
                        self.bank[0:n, j:j + 1], x[:, t0:t0 + n], ones[:, 0:1], start=(i == 0 and j == 0),
                        stop=(i == 1), skip_group_check=True), tx, *self.free)
            sqb.give(ks, self.t)
            c3, tmp3 = self.col, cols3[2]
            t = None
            for p, j0, j1 in ((128, 0, 2), (META, 2, 3)):
                if len(self.tiles) < j1:
                    break
                o, r, q = self.bank[0:p, j0:j1], c3[0:p, j0:j1], tmp3[0:p, j0:j1]
                t1 = A.do(lambda e: e.activation(q, o, ACT.Sqrt, scale=1.0 / 1024, bias=eps[0:p, :]), self.t, t,
                          D.last(), *free)
                t = D.do(lambda e: e.reciprocal(r, q), t1, *free)
                if newton:
                    t = D.do(lambda e: e.tensor_scalar(q, o, -0.5 / 1024, -0.5 * EPS, ALU.mult, ALU.add), t)
                    t = D.do(lambda e: e.tensor_tensor(q, q, r, ALU.mult), t)
                    t = D.do(lambda e: e.tensor_tensor(q, q, r, ALU.mult), t)
                    t = D.do(lambda e: e.scalar_tensor_tensor(r, q, 1.5, r, ALU.add, ALU.mult), t)
            side.give(self.k, t, t1)
            self.ctok = t

        def rstd_row(self):
            c3, row, t = self.col, self.row, self.ctok
            k, b, fs = side.take()
            for j, (t0, n) in enumerate(self.tiles):
                tp = P.do(lambda e: e.matmul(b[:, t0:t0 + n], c3[0:n, j:j + 1].broadcast_to([n, 128]),
                                             ident[0:n, 0:n], start=True, stop=True), t, *fs)
            c0, n = self.c0, self.src.shape[2]
            self.rtok = A.do(lambda e: e.activation(row[:, c0:n], b[:, c0:n], ACT.Copy), tp, D.last())
            side.give(k, self.rtok)
            return self.rtok

        def rstd(self, newton, *free):
            self.rstd_sums(newton, *free)
            return self.rstd_row()

        def apply(self, ring):
            n, row = self.src.shape[2], self.row
            for c in range(8):
                hc, g = self.src[:, c, self.c0:n], pc(self.gain, c)
                a, b = self.xh[:, c, self.c0:n], self.xl[:, c, self.c0:n]
                k, m, fm = ring.take()
                t = D.do(lambda e: e.scalar_tensor_tensor(m, hc, g, row[:, self.c0:n], ALU.mult, ALU.mult),
                         self.rtok, *fm)
                t1 = A.do(lambda e: e.activation(a, m, ACT.Copy), t)
                flush()
                t2 = later(D, lambda e: e.tensor_tensor(b, m, a.bitcast(F), ALU.subtract), t1)
                ring.give(k, t2)
                self.tok[c] = [t1, t2]
            flush()

        def feed(self, c0=None):
            n = self.src.shape[2]
            c0 = self.c0 if c0 is None else c0
            return [(self.xh[:, c, c0:n], self.xl[:, c, c0:n], self.tok[c]) for c in range(8)]

    def load_sqrt():
        A.do(lambda e: e.activation(cst[:, C_R3 + 9:C_R3 + 10], eps, ACT.Sqrt), A.last())

    def residual(c, ps, k, tok, scale, nxt, c0):
        n = T - c0
        hc = h[:, c, c0:T]
        t = D.do(lambda e: e.scalar_tensor_tensor(hc, ps, scale, hc, ALU.mult, ALU.add), tok)
        main.give(k, t)
        if c == 5:
            load_sqrt()
        nxt.chunk(c, t)

    def barrier():
        flush()
        toks = [P.last(), D.last(), A.last(), G.last()]
        for e in (D, A, G):
            e.wait(*toks)

    def transposed(dst, src, tok=None, *free):
        k = src.shape[0]
        P.put(lambda e: e.transpose(dst, src, ident[0:k, 0:k]), tok, *free)

    identb, maskb = tens["cnb"][:, 0:128], tens["cnb"][:, 128:384]
    issue_split()
    for e in (A, D, P):
        e.wait(ld["l_c1"], ld["l_p"])
    norm = Norm("ng0", rows[0])
    load_sqrt()
    for c in range(8):
        norm.split(c, ld["l_h"] if c < 4 else ld["l_h2"])
        flush()
        if c == 5:
            issue_split()
    for c in range(8):
        norm.square(c)
        flush()
        if c == 3:
            issue_split()

    def layer(l, norm, nxt_norm):
        arena["at"] = 0
        q0 = 0 if l == 0 else META
        qT, qiT = alloc(4, T), alloc(4, T)
        kT, kiT = alloc(T), alloc(T)
        V = alloc(3, 72)
        ga, gb = alloc(4, T), alloc(4, T)
        mg = alloc(16, T)
        L = alloc(8, T)
        scr = [alloc(T) for _ in range(2)]
        PT = Ring([alloc(3, 128) for _ in range(2)])
        rope_a = Ring([alloc(T) for _ in range(2)])
        rope_g = Ring([alloc(T) for _ in range(2)])
        rel = Ring([alloc(T), alloc(T), rope_g.bufs[0], rope_g.bufs[1]])
        ubr = Ring([alloc(16 + T)])
        pw = rope_a.bufs[0]
        tmp = Ring([alloc(T) for _ in range(2)])
        m8 = alloc(8, 8)
        nm, sm, rs = alloc(8), alloc(8), alloc(8)
        psh = alloc(4)
        r10 = scr[1]
        qa = L[:, 0:5, :]
        Y = lambda i: (yh[:, i * T:(i + 1) * T], yl[:, i * T:(i + 1) * T])
        barrier()
        row = norm.row
        feed_all, feed_q = norm.feed(0), norm.feed(q0)
        nq = T - q0

        tiles3 = [(META, 128), (META + 128, 128), (0, 128)]
        align()
        first = [block("w_in", l, [(512, 64, 0), (2688, 64, 64)], feed_all, T)]
        if l:
            norm.rstd_sums(True)
        first.append(block("w_in", l, [(576, 64, 0), (2752, 8, 64)], feed_all, T))
        if l == 0:
            norm.rstd_sums(True)
            first.append(block("w_in", l, 2176, feed_q, nq))
        tr = norm.rstd_row()
        if l == 0:
            for e in (D, P):
                e.wait(ld["l_c"])
            D.do(lambda e: e.tensor_copy(identb, ident))
            D.do(lambda e: e.tensor_scalar(maskb, cst[:, C_CM:C_CM + 256], 1.0, -NEG, ALU.subtract, ALU.mult))
        t_psh = D.do(lambda e: e.tensor_scalar(psh, prm[:, PARAMS[f"ps{l}"]:PARAMS[f"ps{l}"] + 4], 0.5, None, ALU.mult))

        t_pad = D.do(lambda e: e.memset(ubr.bufs[0][:, 0:16], 0.0))
        ssq = {"n": 0}
        sk, sbank, sfree = side.take()

        def rope(ps, k, tok, c0, dst, gcol, b, done):
            n = T - c0
            ka, a, fa = rope_a.take() if gcol is None else (None, qa[:, b, :], [])
            a = a[:, 0:n]
            ta = D.do(lambda e: e.tensor_tensor(a, ps, row[:, c0:T], ALU.mult), tok, tr, *fa)
            main.give(k, ta)
            if gcol is None:
                ag, tg, kg = a, ta, None
            else:
                ks, sq, fs = sqb.take()
                sq = sq[:, 0:n]
                ts = A.do(lambda e: e.activation(sq, a, ACT.Square), ta, *fs)
                kg, ag, fg = rope_g.take()
                ag = ag[:, 0:n]
                tg = A.do(lambda e: e.activation(ag, a, ACT.Copy, scale=gcol), ta, *fg)
            yield
            if gcol is not None:
                first, last = ssq["n"] == 0, ssq["n"] == 4
                ssq["n"] += 1
                s10 = cst[:, C_S10 + 10 * b:C_S10 + 10 * b + 10]
                so = sbank[0:10, c0:T]
                if l == 1 and b == 4:
                    pass
                tp = P.do(lambda e: e.matmul(so, s10, sq, start=first, stop=last, skip_group_check=True), ts, *sfree)
                sqb.give(ks, tp)
                if last:
                    ssq["t"] = tp
            kr, rb, fr = side.take()
            ro = rb[:, 0:n]
            tp = P.do(lambda e: e.matmul(ro, cst[:, C_PERM:C_PERM + 128], ag, start=True, stop=True), tg, *fr)
            yield
            t2 = D.do(lambda e: e.tensor_tensor(dst, ro, cst[:, C_SIN + c0:C_SIN + T], ALU.mult), tp)
            side.give(kr, t2)
            t1 = D.do(lambda e: e.tensor_tensor(ag, ag, cst[:, C_COS + c0:C_COS + T], ALU.mult), tp)
            t3 = later(D, lambda e: e.tensor_tensor(dst, dst, ag, ALU.add), t1, t2)
            if kg is not None:
                rope_g.give(kg, t3)
            else:
                rope_a.give(ka, t3)
            done.append(t3)

        tq, tk, tqi, tki = [], [], [], []
        k, ps, tok = first[0]
        active.append(rope(ps, k, tok, 0, kiT[:, :], pc(f"kn{l}"), 4, tk))
        tv, t_w = [], []

        def values(k, ps, tok):
            kt, m, fm = tmp.take()
            t = D.do(lambda e: e.tensor_tensor(m[0:72, :], ps[0:72, :], row[0:72, :], ALU.mult), tok, tr, *fm)
            main.give(k, t)
            yield
            ks, sb_, fs = side.take()
            for i, (t0, n) in enumerate(tiles3):
                tp = P.do(lambda e: e.transpose(sb_[0:n, 72 * i:72 * i + 72], m[0:72, t0:t0 + n], ident[0:72, 0:72]),
                          t, *fs)
            tmp.give(kt, tp)
            t = A.do(lambda e: e.activation(V[:, 0:2, :], sb_[:, 0:144].rearrange("p (a b) -> p a b", b=72), ACT.Copy), tp)
            t1 = A.do(lambda e: e.activation(V[0:META, 2, :], sb_[0:META, 144:216], ACT.Copy), tp)
            side.give(ks, t1)
            t = D.do(lambda e: e.tensor_scalar(V[:, 0:2, 64:72], V[:, 0:2, 64:72], 8 ** -0.5 * 64 ** -0.5, None,
                                               ALU.mult), t)
            tv.extend([t1, t])
            t_w.append(t)

        active.append(values(*first[1]))
        if len(first) == 2:
            tick()
        for b in range(4):
            k, ps, tok = first[2] if b < len(first) - 2 else block("w_in", l, 2176 + 128 * b, feed_q, nq)
            active.append(rope(ps, k, tok, q0, qiT[:, b, q0:T], None, None, tqi))
            tick()
        for b in range(4):
            k, ps, tok = block("w_in", l, 128 * b, feed_q, nq)
            active.append(rope(ps, k, tok, q0, qT[:, b, q0:T], pc(f"qn{l}"), b, tq))
            tick()

        def gate_a(b):
            k, ps, tok = block("w_in", l, 640 + 128 * b, feed_q, nq)
            kt, m, fm = tmp.take()
            m = m[:, 0:nq]
            g = ga[:, b, q0:T]
            t1 = D.do(lambda e: e.tensor_tensor(m, ps, row[:, q0:T], ALU.mult), tok, *fm)
            main.give(k, t1)
            t2 = A.do(lambda e: e.activation(g, m, ACT.Tanh, scale=0.5), t1)
            t3 = later(D, lambda e: e.scalar_tensor_tensor(g, g, 1.0, m, ALU.add, ALU.mult), t2)
            tmp.give(kt, t3)
            return t3

        def gate_b(b):
            k, ps, tok = block("w_in", l, 1664 + 128 * b, feed_q, nq)
            kt, m, fm = tmp.take()
            m = m[:, 0:nq]
            g = gb[:, b, q0:T]
            t1 = D.do(lambda e: e.tensor_tensor(m, ps, row[:, q0:T], ALU.mult), tok, *fm)
            main.give(k, t1)
            t2 = A.do(lambda e: e.activation(g, m, ACT.Tanh, scale=0.5), t1)
            t3 = later(D, lambda e: e.scalar_tensor_tensor(g, g, 1.0, m, ALU.add, ALU.mult), t2)
            tmp.give(kt, t3)
            return t3

        def merge(b):
            k, ps, tok = block("w_in", l, 2760 + 128 * b, feed_q, nq)
            kt, m, fm = tmp.take()
            m = m[:, 0:nq]
            t1 = D.do(lambda e: e.tensor_tensor(m, ps, row[:, q0:T], ALU.mult), tok, *fm)
            main.give(k, t1)
            t2 = A.do(lambda e: e.activation(mg[:, b, q0:T], m, ACT.Tanh, scale=0.5), t1)
            tmp.give(kt, t2)
            return t2

        def finish_q():
            so, ro, lo = sbank[0:10, 0:T], r10[0:10, 0:T], 0
            e10 = cst[0:10, C_EPS:C_EPS + 1]
            t = A.do(lambda e: e.activation(ro, so, ACT.Sqrt, scale=1.0 / 64, bias=e10), ssq["t"])
            rr = PT.bufs[0][0:10, :, :].rearrange("p a b -> p (a b)")[:, 0:T]
            t = D.do(lambda e: e.reciprocal(rr, ro), t)
            side.give(sk, t)
            yield
            yield
            for b in (4, 0, 1, 2, 3):
                c0 = 0 if b == 4 else q0
                ks, sb_, fs = side.take()
                o = sb_[:, 0:T - c0]
                sel = cst[0:10, C_B10 + 128 * b:C_B10 + 128 * b + 128]
                tp = P.do(lambda e, o=o, c0=c0, sel=sel: e.matmul(o, sel, rr[:, c0:T], start=True, stop=True), t, *fs)
                if b == 4:
                    td = D.do(lambda e: e.tensor_tensor(kT[0:64, :], kiT[0:64, :], o[0:64, :], ALU.mult), tp, *tk)
                    side.give(ks, td)
                    t1 = A.do(lambda e: e.activation(kT[64:128, :], kT[0:64, :], ACT.Copy), td)
                    t2 = A.do(lambda e: e.activation(kiT[0:64, :], kiT[64:128, :], ACT.Copy), td)
                    tk.extend([td, t1])
                    tki.append(t2)
                else:
                    dst = qT[:, b, q0:T]
                    td = D.do(lambda e: e.tensor_tensor(dst, dst, o, ALU.mult), tp, *tq)
                    side.give(ks, td)
                    tq.append(td)
                if b in (0, 2, 3):
                    yield

        def indexer(tile_no):
            c0, nk = ((META, 144), (META + 128, T))[tile_no]
            vis = cst[:, (C_VA, C_VB)[tile_no]:(C_VA, C_VB)[tile_no] + nk]
            ac = scr[tile_no][:, 0:nk]
            t = None
            for hh in range(8):
                ks, sb_, fs = side.take()
                o = sb_[:, 0:nk]
                p0 = 64 * (hh % 2)
                tp = P.do(lambda e, o=o, p0=p0, hh=hh: e.matmul(
                    o, qiT[p0:p0 + 64, hh // 2, c0:c0 + 128], kiT[p0:p0 + 64, 0:nk], start=True, stop=True),
                    *tqi, *tki, *fs)
                kr, rl, fr = rel.take()
                rl = rl[:, 0:nk]
                ta = A.do(lambda e, rl=rl, o=o: e.activation(rl, o, ACT.Relu), tp, *fr)
                side.give(ks, ta)
                w = V[:, tile_no, 64 + hh:65 + hh]
                src = vis if hh == 0 else ac
                t = later(D, lambda e: e.scalar_tensor_tensor(
                    ac, rl, w, src, ALU.mult, ALU.add), ta, t, *t_w)
                rel.give(kr, t)
                if hh % (2, 4)[1 - tile_no] == (2, 4)[1 - tile_no] - 1:
                    yield
            for r in range(8):
                mx = m8[:, r, :]
                tm = D.do(lambda e, mx=mx: e.max(mx, ac), t)
                t = D.do(lambda e, mx=mx: e.match_replace(ac, mx, ac, -3e38), tm)
                if r % (2, 4)[1 - tile_no] == (2, 4)[1 - tile_no] - 1:
                    yield
            sel_tok[tile_no] = D.do(lambda e: e.tensor_scalar(ac, ac, -2e38, NEG, ALU.is_gt, ALU.mult), t)

        def attend(tile_no):
            c0, nk = ((META, 144), (META + 128, T))[tile_no]
            kcs = [(2, 0, 16), (0, 16, 128)] + ([(1, 144, 128)] if tile_no else [])
            bs = scr[tile_no][:, 0:nk]
            tb = sel_tok[tile_no]
            nn = len(kcs)
            tl, te, tn, copied, ob = {}, {}, {}, {}, None
            for s in range(8):
                if s == 4:
                    ko, ob, fo = side.take()
                for hh in (range(2 * s - 8, 2 * s - 6) if s >= 4 else ()):
                    kp, pt, toks = copied[hh]
                    half = 64 * (hh % 2)
                    oo = ob[half:half + 64, 128 * (hh // 2):128 * (hh // 2) + 128]
                    for i, (vi, _, kn) in enumerate(kcs):
                        tt = P.do(lambda e: e.matmul(
                            oo, V[0:kn, vi, 0:64], pt[0:kn, i, :], start=(i == 0), stop=(i == nn - 1)),
                            *toks, *fo, *tv)
                    PT.give(kp, tt)
                g = s - 1
                if 0 <= g < 4:
                    hs = slice(2 * g, 2 * g + 2)
                    t = D.do(lambda e: e.tensor_reduce(nm[:, hs], L[:, hs, 0:nk], AX, ALU.max, negate=True),
                             tl[2 * g + 1])
                    for hh in (2 * g, 2 * g + 1):
                        te[g] = A.do(lambda e: e.activation(
                            L[:, hh, 0:nk], L[:, hh, 0:nk], ACT.Exp, bias=nm[:, hh:hh + 1],
                            accum_out=sm[:, hh:hh + 1]), t)
                g = s - 3
                if 0 <= g < 4:
                    for hh in (2 * g, 2 * g + 1):
                        ks, sb_, fs = side.take()
                        P.wait(*fs, tn[hh])
                        for i, (_, k0, kn) in enumerate(kcs):
                            tp = P.do(lambda e: e.transpose(
                                sb_[0:kn, 128 * i:128 * i + 128], L[:, hh, k0:k0 + kn], ident))
                        kp, pt, fp = PT.take()
                        t1 = A.do(lambda e: e.activation(pt[0:16, 0, :], sb_[0:16, 0:128], ACT.Copy), tp, *fp)
                        t2 = A.do(lambda e: e.activation(
                            pt[:, 1:nn, :], sb_[:, 128:128 * nn].rearrange("p (a b) -> p a b", b=128), ACT.Copy),
                            tp, *fp)
                        side.give(ks, t1, t2)
                        copied[hh] = (kp, pt, [t1, t2])
                if s < 4:
                    for hh in (2 * s, 2 * s + 1):
                        ks, sb_, fs = side.take()
                        o, p0 = sb_[:, 0:nk], 64 * (hh % 2)
                        tp = P.do(lambda e: e.matmul(
                            o, qT[p0:p0 + 64, hh // 2, c0:c0 + 128], kT[p0:p0 + 64, 0:nk], start=True, stop=True),
                            *tq, *tk, *fs)
                        tl[hh] = later(D, lambda e: e.scalar_tensor_tensor(
                            L[:, hh, 0:nk], o, 0.125, bs, ALU.mult, ALU.add), tp, tb, *busy[hh])
                        side.give(ks, tl[hh])
                g = s - 2
                if 0 <= g < 4:
                    hs = slice(2 * g, 2 * g + 2)
                    t = D.do(lambda e: e.reciprocal(rs[:, hs], sm[:, hs]), te[g])
                    for hh in (2 * g, 2 * g + 1):
                        tn[hh] = D.do(lambda e: e.tensor_scalar(
                            L[:, hh, 0:nk], L[:, hh, 0:nk], rs[:, hh:hh + 1], None, ALU.mult), t)
                        busy[hh] = []
                yield
            for hh in range(8):
                busy[hh] = [copied[hh][2]]
            for b in range(4):
                kt, m, fm = tmp.take()
                m = m[:, 0:128]
                yhi, ylo = yh[:, b * T + c0:b * T + c0 + 128], yl[:, b * T + c0:b * T + c0 + 128]
                t1 = D.do(lambda e, b=b, m=m: e.scalar_tensor_tensor(
                    m, ob[:, 128 * b:128 * b + 128], 0.5, ga[:, b, c0:c0 + 128], ALU.mult, ALU.mult), tt, *fm, *t_ga)
                t2 = A.do(lambda e, m=m, yhi=yhi: e.activation(yhi, m, ACT.Copy), t1)
                t3 = later(D, lambda e: e.tensor_tensor(ylo, m, yhi.bitcast(F), ALU.subtract), t2)
                tmp.give(kt, t3)
                t_at[b] += [t2, t3]
            side.give(ko, t1)

        def attend_meta():
            pair = [side.take() for _ in range(2)]
            P.wait(*tq, *tk, *pair[0][2], *pair[1][2])
            tp = []
            for half in range(2):
                for j in range(4):
                    p0 = 64 * half
                    tp.append(P.do(lambda e, p0=p0, j=j, o=pair[half][1]: e.matmul(
                        o[0:16, 16 * j:16 * j + 16], qT[p0:p0 + 64, j, 0:16], kT[p0:p0 + 64, 0:16],
                        start=True, stop=True)))
            Lm = L[0:16, 0, 0:128].rearrange("p (h k) -> p h k", k=16)
            nmb = nm[0:16, :].unsqueeze(2).broadcast_to([16, 8, 16])
            rsb = rs[0:16, :].unsqueeze(2).broadcast_to([16, 8, 16])
            for half in range(2):
                t = A.do(lambda e, half=half: e.activation(
                    Lm[:, 4 * half:4 * half + 4, :], pair[half][1][0:16, 0:64].rearrange("p (h k) -> p h k", k=16),
                    ACT.Copy, scale=0.125), tp[-1])
                side.give(pair[half][0], t)
            yield
            t = D.do(lambda e: e.tensor_reduce(nm[0:16, :], Lm, AX, ALU.max, negate=True), t)
            t = D.do(lambda e: e.tensor_tensor(Lm, Lm, nmb, ALU.add), t)
            t = A.do(lambda e: e.activation(Lm, Lm, ACT.Exp), t)
            yield
            t = D.do(lambda e: e.tensor_reduce(sm[0:16, :], Lm, AX, ALU.add), t)
            t = D.do(lambda e: e.reciprocal(rs[0:16, :], sm[0:16, :]), t)
            t = D.do(lambda e: e.tensor_tensor(Lm, Lm, rsb, ALU.mult), t)
            yield
            yield
            ks, sb_, fs = side.take()
            P.wait(*fs, t)
            for hh in range(8):
                tp = P.do(lambda e, hh=hh: e.transpose(sb_[0:16, 16 * hh:16 * hh + 16], Lm[:, hh, :], ident[0:16, 0:16]))
            kp, pt, fp = PT.take()
            ptm = pt[0:16, 0, :]
            t = A.do(lambda e: e.activation(ptm, sb_[0:16, 0:128], ACT.Copy), tp, *fp)
            side.give(ks, t)
            yield
            ks, sb2, fs = side.take()
            P.wait(*fs, t, *tv)
            for half in range(2):
                rhs = ptm[:, 64 * half:64 * half + 64]
                tp = P.do(lambda e, half=half, rhs=rhs: e.matmul(
                    sb2[64 * half:64 * half + 64, 0:64], V[0:16, 2, 0:64], rhs, start=True, stop=True))
            PT.give(kp, tp)
            yield
            kt, m, fm = tmp.take()
            m = m[:, 0:64].rearrange("p (j q) -> p j q", q=16)
            yv = [y[:, 0:4 * T].rearrange("p (j t) -> p j t", t=T)[:, :, 0:16] for y in (yh, yl)]
            t1 = D.do(lambda e: e.scalar_tensor_tensor(
                m, sb2[:, 0:64].rearrange("p (j q) -> p j q", q=16), 0.5, ga[:, :, 0:16], ALU.mult, ALU.mult),
                tp, *fm, *t_ga)
            side.give(ks, t1)
            t2 = A.do(lambda e: e.activation(yv[0], m, ACT.Copy), t1)
            t3 = D.do(lambda e: e.tensor_tensor(yv[1], m, yv[0].bitcast(F), ALU.subtract), t2)
            tmp.give(kt, t3)
            for b in range(4):
                t_at[b] += [t2, t3]

        t_ga, sel_tok = [], {}
        busy = [[] for _ in range(8)]
        t_at = [[] for _ in range(4)]

        def attention():
            yield
            yield
            yield from finish_q()
            rel.free = [(i, [*tq, *tk]) for i in range(4)]
            if l == 0:
                active.append(attend_meta())
            yield from indexer(0)
            active.insert(0, indexer(1))
            if l == 0:
                yield
                yield
            yield from attend(0)
            while 1 not in sel_tok:
                yield
            yield from attend(1)

        def pool(g, ps, k, tok, done):
            ku, ub, fu = ubr.take()
            u, w = ub[:, 16:16 + T], 2 << g
            t = D.do(lambda e: e.tensor_tensor(u, ps, row[:, 0:T], ALU.mult), tok, t_pad, *fu)
            main.give(k, t)
            t = D.do(lambda e: e.tensor_tensor_scan(pw, u, ub[:, 16 - w:16 - w + T], 0.0, ALU.add, ALU.subtract), t,
                     *tq, *tki, *tk, *tqi)
            yhi, ylo = Y(4 + g)
            yhi, ylo = yhi[:, q0:T], ylo[:, q0:T]
            kt, m, fm = tmp.take()
            t2 = D.do(lambda e: e.scalar_tensor_tensor(
                m[:, 16:T], pw[:, 16:T], 1.0 / w, u[:, 16:T], ALU.mult, ALU.subtract), t, *fm)
            if q0 == 0:
                rc = cst[:, C_RC + 16 * g:C_RC + 16 * g + 16]
                t = D.do(lambda e: e.tensor_tensor(m[:, 0:16], pw[:, 0:16], rc, ALU.mult), t, *fm)
                t = D.do(lambda e: e.tensor_tensor(m[:, 0:16], m[:, 0:16], u[:, 0:16], ALU.subtract), t)
            ubr.give(ku, t, t2)
            t3 = A.do(lambda e: e.activation(yhi, m[:, q0:T], ACT.Copy), t, t2)
            t4 = later(D, lambda e: e.tensor_tensor(ylo, m[:, q0:T], yhi.bitcast(F), ALU.subtract), t3)
            tmp.give(kt, t4)
            done[g] = [t3, t4]

        active.append(attention())
        for b in range(4):
            t_ga.append(gate_a(b))
            tick()
        tmp.bufs.append(rope_a.bufs[1])
        tmp.give(2, *tq, *tqi, *tk, *tki)
        t_pl = [None] * 4
        for g in range(4):
            k, ps, tok = block("w_in", l, 1152 + 128 * g, feed_all, T)
            pool(g, ps, k, tok, t_pl)
            tick()
        t_gb = []
        for b in range(4):
            t_gb.append(gate_b(b))
            tick()
        t_mg = [None] * 16
        for b in range(8, 16):
            t_mg[b] = merge(b)
            tick()
        t_mid = []

        def mid(g):
            yhi, ylo = Y(4 + g)
            k, ps, tok = block("pool_w", 4 * l + g, 0, [(yhi[:, q0:T], ylo[:, q0:T], t_pl[g])], nq)
            kt, m, fm = tmp.take()
            m = m[:, 0:nq]
            zh, zl = Y(8 + g)
            zh, zl = zh[:, q0:T], zl[:, q0:T]
            t1 = D.do(lambda e: e.scalar_tensor_tensor(
                m, ps, pc(f"pb{l}", g), gb[:, g, q0:T], ALU.add, ALU.mult), tok, t_gb[g], *fm)
            main.give(k, t1)
            t3 = A.do(lambda e: e.activation(zh, m, ACT.Copy, scale=psh[:, g:g + 1]), t1, t_psh)
            t4 = later(D, lambda e: e.scalar_tensor_tensor(
                zl, m, psh[:, g:g + 1], zh.bitcast(F), ALU.mult, ALU.subtract), t3)
            tmp.give(kt, t4)
            t_mid.append([t3, t4])

        for b in range(8):
            t_mg[b] = merge(b)
            tick()
            if b < 4:
                mid(b)
        src = [(Y(8 + g)[0][:, q0:T], Y(8 + g)[1][:, q0:T], t_mid[g]) for g in range(4)]
        t_zb = []
        for b in range(8):
            k, ps, tok = block("w_b", l, 128 * b, src, nq)
            m = mg[:, 8 + b, q0:T]
            t = D.do(lambda e, ps=ps, m=m: e.scalar_tensor_tensor(m, m, 1.0, ps, ALU.add, ALU.mult), tok, t_mg[8 + b])
            main.give(k, t)
            t_zb.append(t)
            tick()
        drain()
        src = [(Y(g)[0][:, q0:T], Y(g)[1][:, q0:T], t_at[g]) for g in range(4)]
        t_z, lows = [], []

        def low(b, zl, m, zh, t3):
            t_z[b].append(D.do(lambda e: e.tensor_tensor(zl, m, zh.bitcast(F), ALU.subtract), t3))

        for b in range(8):
            k, ps, tok = block("w_a", l, 128 * b, src, nq)
            m, zb = mg[:, b, q0:T], mg[:, 8 + b, q0:T]
            t1 = D.do(lambda e, ps=ps, m=m: e.scalar_tensor_tensor(m, m, 1.0, ps, ALU.add, ALU.mult), tok, t_mg[b])
            main.give(k, t1)
            t2 = D.do(lambda e, zb=zb, m=m: e.tensor_tensor(m, m, zb, ALU.add), t1, t_zb[b])
            zh, zl = Y(12 + b)
            zh, zl = zh[:, q0:T], zl[:, q0:T]
            t3 = A.do(lambda e, m=m, zh=zh: e.activation(zh, m, ACT.Copy), t2)
            t_z.append([t3])
            lows.append((b, zl, m, zh, t3))
            if b:
                low(*lows.pop(0))
        low(*lows.pop(0))
        src = [(Y(12 + b)[0][:, q0:T], Y(12 + b)[1][:, q0:T], t_z[b]) for b in range(8)]
        nxt = Norm(nxt_norm, rows[(l + 1) % 2], q0)
        for b in range(8):
            k, ps, tok = block("w_out", l, 128 * b, src, nq)
            residual(b, ps, k, tok, 0.5, nxt, q0)
        return nxt

    norm = layer(0, norm, "ng1")
    norm = layer(1, norm, "f1n")

    Z = META
    Yc = lambda i: (yh[:, i * S:(i + 1) * S], yl[:, i * S:(i + 1) * S])

    def split_to(i, m, tok):
        a, b = Yc(i)
        t1 = A.do(lambda e: e.activation(a, m, ACT.Copy), tok)
        t2 = later(D, lambda e: e.tensor_tensor(b, m, a.bitcast(F), ALU.subtract), t1, tok)
        return [t1, t2]

    def split_later(i, m, tok):
        a, b = Yc(i)
        t1 = later(A, lambda e: e.activation(a, m, ACT.Copy), tok)
        t2 = later(D, lambda e: e.tensor_tensor(b, m, a.bitcast(F), ALU.subtract), t1, tok)
        return [t1, t2]

    def ffn(name, norm, nxt):
        arena["at"] = 0
        tmp = Ring([alloc(2, S) for _ in range(3)])
        sil = Ring([alloc(S) for _ in range(3)])
        barrier()
        row = norm.row
        src = norm.feed()
        rb = row[:, Z:T].unsqueeze(1).broadcast_to([128, 2, S])
        ytok, hid, up = [], [], []

        def hidden():
            j, kt, kg, g, m, t2 = hid.pop(0)
            t3 = D.do(lambda e: e.tensor_tensor(g, g, m[:, 1, :], ALU.mult), t2)
            tmp.give(kt, t3)
            tt = split_to(j, g, t3)
            sil.give(kg, *tt)
            ytok.append(tt)

        def gated(j, k, b, tok):
            kt, m, fm = tmp.take()
            t1 = D.do(lambda e: e.tensor_tensor(
                m, b[:, :].rearrange("p (a s) -> p a s", a=2), rb, ALU.mult), tok, norm.rtok, *fm)
            main.give(k, t1)
            kg, g, fg = sil.take()
            t2 = A.do(lambda e: e.activation(g, m[:, 0, :], ACT.Silu), t1, *fg)
            hid.append((j, kt, kg, g, m, t2))
            if j:
                hidden()

        for j in range(22):
            k, b, free = main.take()
            block(name + "_gu", 0, 128 * j, src, S, b[:, 0:S], free)
            _, _, tok = block(name + "_gu", 0, 2816 + 128 * j, src, S, b[:, S:2 * S], [])
            up.append((j, k, b, tok))
            if j == 0:
                norm.rstd_sums(False)
            if j == 1:
                norm.rstd_row()
            while j and up:
                gated(*up.pop(0))
        hidden()
        src = [(*Yc(j), ytok[j]) for j in range(22)]
        nxt = nxt()
        for b in range(8):
            k, ps, tok = block(name + "_dn", 0, 128 * b, src, S)
            residual(b, ps, k, tok, 0.5, nxt, Z)
        return nxt

    norm = ffn("f1", norm, lambda: Norm("mxn", rows[1], Z, late=True))

    def mixer(norm):
        arena["at"] = 0
        zacc = alloc(8, S)
        xsT = [alloc(4, S) for _ in range(2)]
        BC = [alloc(2, S) for _ in range(2)]
        zs = [alloc(4, S) for _ in range(2)]
        xdt = alloc(2, 512)
        btok = alloc(128)
        xw = alloc(512)
        cbm = alloc(2, 128)
        prev = alloc(512)
        M = alloc(8, 256)
        E8 = alloc(8, 128)
        cin = Ring([alloc(3 + S) for _ in range(3)])
        cv = Ring([alloc(S) for _ in range(3)])
        tmp = Ring([alloc(S) for _ in range(3)])
        dtT, acs, dq = (M[:, i, :] for i in (3, 4, 5))
        dden = dq[:, 0:128]
        tokm = alloc(5, 32)
        negA = alloc(2, 32)
        identb, maskb = tens["cnb"][:, 0:128], tens["cnb"][:, 128:384]
        acol = alloc(1)
        acr, idr = tens["acr"][:, 0:S], tens["acr"][:, S:S + 32]
        grow = rows[0][:, 0:S]
        barrier()
        norm.rstd(False, D.last())
        norm.apply(tmp)
        src = norm.feed()
        cwh, cbh, snh = (prm[:, PARAMS[n]:PARAMS[n] + w] for n, w in (("cw", 96), ("cb", 24), ("sn", 16)))
        t = D.do(lambda e: e.tensor_scalar(cwh, cwh, 0.5, None, ALU.mult))
        t = D.do(lambda e: e.tensor_scalar(cbh, cbh, 0.5, None, ALU.mult))
        t_half = D.do(lambda e: e.tensor_scalar(snh, snh, 0.5, None, ALU.mult))
        tc = [D.do(lambda e, b=b: e.memset(b[:, 0:3], 0.0)) for b in cin.bufs]

        d, ac, q = dtT[0:32, :], acs[0:32, :], dq[0:32, :]
        t_acs = []

        def steps(k, ps, tok):
            u, v, w = (M[0:32, i, :] for i in range(3))
            t = D.do(lambda e: e.tensor_scalar(d, ps[0:32, :], pc("dtb", 0, 32), None, ALU.add), tok)
            main.give(k, t)
            t1 = A.do(lambda e: e.activation(u, d, ACT.Abs), t)
            t1 = A.do(lambda e: e.activation(u, u, ACT.Exp, scale=-1.0), t1)
            t2 = A.do(lambda e: e.activation(acol[0:32, :], pc("alog", 0, 32), ACT.Exp))
            yield
            t = D.do(lambda e: e.tensor_scalar(d, d, 0.0, None, ALU.max), t1)
            t1 = D.do(lambda e: e.tensor_scalar(v, u, 1.0, None, ALU.add), t1)
            t3 = A.do(lambda e: e.activation(w, v, ACT.Ln), t1)
            yield
            t1 = D.do(lambda e: e.tensor_scalar(v, v, -1.0, None, ALU.add), t3)
            t4 = D.do(lambda e: e.tensor_scalar(ac, v, 0.0, None, ALU.is_equal), t1)
            t1 = D.do(lambda e: e.tensor_tensor(v, v, ac, ALU.add), t4)
            t1 = D.do(lambda e: e.reciprocal(q, v), t1)
            yield
            t1 = D.do(lambda e: e.tensor_tensor(w, w, q, ALU.mult), t1)
            t1 = D.do(lambda e: e.tensor_tensor(w, w, ac, ALU.add), t1)
            t1 = D.do(lambda e: e.tensor_tensor(w, w, u, ALU.mult), t1)
            t = D.do(lambda e: e.tensor_tensor(d, d, w, ALU.add), t1, t)
            t_dt = t
            yield
            t = D.do(lambda e: e.tensor_scalar(q, d, acol[0:32, :], -1.0, ALU.mult, ALU.mult), t2, t)
            for c in range(2):
                t = D.do(lambda e: e.tensor_tensor_scan(
                    ac[:, 128 * c:128 * c + 128], ones[0:32, :], q[:, 128 * c:128 * c + 128], 0.0,
                    ALU.mult, ALU.add), t)
            t_ac = t
            t_de = A.do(lambda e: e.activation(dden[0:32, :], ac[:, 0:128], ACT.Exp, scale=-1.0, bias=ac[:, 127:128]),
                        t_ac)
            yield
            ks, sb_, fs = side.take()
            P.wait(*fs, t_dt, t_ac, t_de)
            for i, a in enumerate((d[:, 0:128], d[:, 128:256], ac[:, 0:128], ac[:, 128:256], dden[0:32, :])):
                tp = P.do(lambda e: e.transpose(sb_[:, 32 * i:32 * i + 32], a, ident[0:32, 0:32]))
            t = A.do(lambda e: e.activation(tokm, sb_[:, 0:160].rearrange("p (a b) -> p a b", b=32), ACT.Copy), tp)
            th = A.do(lambda e: e.activation(acr[0:32, :], ac, ACT.Copy))
            ti = [A.do(lambda e: e.activation(idr[32 * i:32 * i + 32, :], ident[0:32, 0:32], ACT.Copy)) for i in (0, 1)]
            tl = D.do(lambda e: e.tensor_tensor(acr[32:64, :], ac, acr[0:32, :].bitcast(F), ALU.subtract), th)
            t_acs.extend([*ti, tl])
            t_tok.append(D.do(lambda e: e.tensor_scalar(negA, tokm[:, 2:4, :], -1.0, None, ALU.mult), t))

        t_tok = []
        active.append(steps(*block("w_in2", 0, [(8192, 32, 0)], src, S)))
        tick()
        yat = []
        for j in range(8):
            k1, p1, tok1 = block("w_in2", 0, 1024 + 128 * j, src, S)
            kt, m, fm = tmp.take()
            t1 = A.do(lambda e: e.activation(m, p1, ACT.Copy), tok1, *fm)
            main.give(k1, t1)
            k2, p2, tok2 = block("w_in2", 0, 2048 + 128 * j, src, S)
            kc, ci, fc = cin.take()
            t2 = D.do(lambda e, ci=ci, m=m, p2=p2: e.tensor_tensor(ci[:, 3:3 + S], m, p2, ALU.mult), t1, tok2, *fc, *tc)
            main.give(k2, t2)
            wc = lambda i, j=j: pc("ca", 8 * i + j)
            t = D.do(lambda e, m=m, ci=ci, w=wc(2): e.tensor_scalar(m, ci[:, 3:3 + S], w, None, ALU.mult), t2)
            for i in (1, 0):
                t = D.do(lambda e, m=m, ci=ci, w=wc(i), i=i: e.scalar_tensor_tensor(
                    m, ci[:, 1 + i:1 + i + S], w, m, ALU.mult, ALU.add), t)
            cin.give(kc, t)
            k3, p3, tok3 = block("w_in2", 0, 128 * j, src, S)
            t = D.do(lambda e, m=m, p3=p3: e.tensor_tensor(m, m, p3, ALU.mult), t, tok3)
            main.give(k3, t)
            tt = split_to(16 + j, m, t)
            tmp.give(kt, *tt)
            yat.append(tt)
            tick()

        def sig(b, col, dst):
            k, ps, tok = block("w_in2", 0, col + 128 * b, src, S)
            t2 = A.do(lambda e: e.activation(dst, ps, ACT.Tanh, scale=0.5), tok)
            main.give(k, t2)
            return t2

        def conv(cb, dst, free):
            k, ps, tok = block("w_in2", 0, 5120 + 128 * cb, src, S)
            return [cb, k, ps, dst, tok, free]

        def taps(items):
            out = []
            for it in items:
                cb, k, ps, dst, t, free = it
                kv, s, fv = cv.take()
                it[5] = (kv, s, free)
                w, b_ = cwh[:, 72 + cb:73 + cb], cbh[:, cb:cb + 1]
                it[4] = D.do(lambda e: e.tensor_scalar(s, ps, w, b_, ALU.mult, ALU.add), t, *fv, t_half)
            for i in (2, 1, 0):
                for it in items:
                    cb, k, ps, dst, t, (kv, s, free) = it
                    w, d = cwh[:, 24 * i + cb:24 * i + cb + 1], 3 - i
                    it[4] = D.do(lambda e: e.scalar_tensor_tensor(
                        s[:, d:S], ps[:, 0:S - d], w, s[:, d:S], ALU.mult, ALU.add), t)
            for cb, k, ps, dst, t, (kv, s, free) in items:
                main.give(k, t)
                out.append([])
                silus.append((dst, s, t, free, kv, out[-1]))
            return out

        silus = []

        def silu():
            while silus:
                dst, s, t, free, kv, done = silus.pop(0)
                t2 = A.do(lambda e: e.activation(dst, s, ACT.Tanh), t, *free())
                t3 = later(D, lambda e: e.scalar_tensor_tensor(dst, dst, 1.0, s, ALU.add, ALU.mult), t2)
                cv.give(kv, t3)
                done.append(t3)

        grp_done, core_done = {}, {}

        def ssd(g, tx, tbc, tz):
            x, (BT, CT), z = xsT[g % 2], (BC[g % 2][:, 0, :], BC[g % 2][:, 1, :]), zs[g % 2]
            hs = slice(8 * g, 8 * g + 8)
            prior = core_done.get(g - 1, [])
            tk_ = []
            for c in range(2):
                ks, sb_, fs = side.take()
                P.wait(*fs, *tx)
                for b in range(4):
                    tp = P.do(lambda e, b=b, c=c, sb_=sb_: e.transpose(
                        sb_[:, 128 * b:128 * b + 128], x[:, b, 128 * c:128 * c + 128], ident))
                dtb = tokm[:, c, hs].unsqueeze(2).broadcast_to([128, 8, 64])
                t = D.do(lambda e, c=c, sb_=sb_, dtb=dtb: e.tensor_tensor(
                    xdt[:, c, :].rearrange("p (h q) -> p h q", q=64),
                    sb_[:, :].rearrange("p (h q) -> p h q", q=64), dtb, ALU.mult), tp, *t_tok, *prior)
                side.give(ks, t)
                tk_.append(t)
            deb = tokm[:, 4, hs].unsqueeze(2).broadcast_to([128, 8, 64])
            t_xw = D.do(lambda e: e.tensor_tensor(
                xw.rearrange("p (h q) -> p h q", q=64), xdt[:, 0, :].rearrange("p (h q) -> p h q", q=64),
                deb, ALU.mult), tk_[0])
            ks, sb_, fs = side.take()
            P.wait(*fs, *tbc)
            P.put(lambda e, sb_=sb_: e.transpose(sb_[:, 256:384], BT[:, 0:128], ident))
            for c in range(2):
                cs = slice(128 * c, 128 * c + 128)
                tp = P.do(lambda e, sb_=sb_, cs=cs: e.matmul(sb_[:, cs], BT[:, cs], CT[:, cs], start=True, stop=True))
            t_bt = A.do(lambda e, sb_=sb_: e.activation(btok, sb_[:, 256:384], ACT.Copy), tp, *prior)
            t_cb = D.do(lambda e, sb_=sb_: e.tensor_tensor(
                cbm, sb_[:, 0:256].rearrange("p (a b) -> p a b", a=2),
                cst[:, C_CM:C_CM + 256].rearrange("p (a b) -> p a b", a=2), ALU.mult), tp, t_bt, *prior)
            side.give(ks, t_cb, t_bt)
            yield
            ks, sb_, fs = side.take()
            tp = P.do(lambda e, sb_=sb_: e.matmul(sb_[:, :], btok, xw, start=True, stop=True), t_bt, t_xw, *fs)
            t_pv = A.do(lambda e, sb_=sb_: e.activation(prev, sb_[:, :], ACT.Copy), tp, *prior)
            side.give(ks, t_pv)
            tM, tEC = [], []
            held = None
            for hp in range(5):
                if held:
                    ks, sb_, t1 = held
                    P.wait(t1)
                    for i in range(2):
                        o = sb_[:, S * i:S * i + S]
                        tr_ = P.do(lambda e: e.matmul(o, identb, maskb, start=False, stop=True, skip_group_check=True))
                    for i in range(2):
                        for c in range(2):
                            hd = 8 * g + 2 * (hp - 1) + i
                            bi = negA[:, c, hd:hd + 1]
                            t2 = A.do(lambda e: e.activation(
                                M[:, 2 * (hp - 1) + i, 128 * c:128 * c + 128],
                                sb_[:, S * i + 128 * c:S * i + 128 * c + 128], ACT.Exp, bias=bi), tr_, *t_tok, *prior)
                    side.give(ks, t1, t2)
                    cbb = cbm.rearrange("p a b -> p (a b)").unsqueeze(1).broadcast_to([128, 2, 256])
                    t4 = D.do(lambda e: e.tensor_tensor(
                        M[:, 2 * hp - 2:2 * hp, :], M[:, 2 * hp - 2:2 * hp, :], cbb, ALU.mult), t2, t_cb)
                    tM.append(t4)
                    ctb = CT[:, 128:256].unsqueeze(1).broadcast_to([128, 2, 128])
                    eh = E8[:, 2 * hp - 2:2 * hp, :]
                    tEC.append(D.do(lambda e: e.tensor_tensor(eh, eh, ctb, ALU.mult), t1))
                if hp < 4:
                    ks, sb_, fs = side.take()
                    P.wait(*fs, *t_acs)
                    for i in range(2):
                        hd = 8 * g + 2 * hp + i
                        sel, o = idr[:, hd:hd + 1].broadcast_to([64, 128]), sb_[:, S * i:S * i + S]
                        tr_ = P.do(lambda e: e.matmul(o, sel, acr, start=(i == 0), stop=False, skip_group_check=True))
                    t1 = A.do(lambda e: e.activation(
                        E8[:, 2 * hp:2 * hp + 2, :], sb_[:, :].rearrange("p (a s) -> p a s", a=2)[:, :, 128:256],
                        ACT.Exp), tr_, *prior)
                    held = (ks, sb_, t1)
                    yield
            yield
            t_y = []
            for half in range(2):
                ks, sb_, fs = side.take()
                P.wait(*fs, *tk_, *tM[0:2 * half + 2], t_pv, *tEC[0:2 * half + 2])
                for hp in range(2 * half, 2 * half + 2):
                    for c in range(2):
                        for i in range(2):
                            hd = 2 * hp + i
                            o = sb_[64 * i:64 * i + 64, S * (hp - 2 * half) + 128 * c:S * (hp - 2 * half) + 128 * c + 128]
                            tp = P.do(lambda e, o=o, c=c, hd=hd: e.matmul(
                                o, xdt[:, c, 64 * hd:64 * hd + 64], M[:, hd, 128 * c:128 * c + 128],
                                start=True, stop=(c == 0)))
                            if c == 1:
                                tp = P.do(lambda e, o=o, hd=hd: e.matmul(
                                    o, prev[:, 64 * hd:64 * hd + 64], E8[:, hd, :], start=False, stop=True))
                for b in range(2):
                    bb = 2 * half + b
                    yb = x[:, bb, :]
                    t1 = D.do(lambda e, sb_=sb_, b=b, bb=bb, yb=yb: e.scalar_tensor_tensor(
                        yb, x[:, bb, :], pc("sd", 4 * g + bb), sb_[:, S * b:S * b + S], ALU.mult, ALU.add), tp, *prior)
                    t_y.append(t1)
                side.give(ks, t1)
                if half == 1:
                    core_done[g] = [tp]
                    sq = [A.do(lambda e: e.activation(z[:, bb, :], x[:, bb, :], ACT.Square), t_y[bb]) for bb in (0, 1)]
                for bb in (2 * half, 2 * half + 1):
                    yb = x[:, bb, :]
                    t_y[bb] = D.do(lambda e: e.tensor_tensor(yb, yb, z[:, bb, :], ALU.mult), t_y[bb], tz[bb])
                yield
            sq += [A.do(lambda e: e.activation(z[:, bb, :], x[:, bb, :], ACT.Square), t_y[bb]) for bb in (2, 3)]
            t = later(D, lambda e: e.tensor_tensor(z[:, 0:2, :], z[:, 0:2, :], z[:, 2:4, :], ALU.add), *sq)
            t = later(D, lambda e: e.tensor_tensor(z[:, 0, :], z[:, 0, :], z[:, 1, :], ALU.add), t)
            yield
            kq, qb, fq = side.take()
            for j in range(2):
                t5 = P.do(lambda e: e.matmul(
                    qb[:, j:j + 1], z[:, 0, 128 * j:128 * j + 128], ones[:, 0:1], start=(j == 0),
                    stop=True, skip_group_check=True), t, *fq)
            c3, q3 = cols3[0][:, 0:2], cols3[2][:, 0:2]
            t = A.do(lambda e: e.activation(q3, qb[:, 0:2], ACT.Sqrt, scale=1.0 / 2048, bias=eps), t5, D.last())
            A.do(lambda e: e.activation(cst[:, C_R3 + 9:C_R3 + 10], eps, ACT.Exp), A.last())
            t = D.do(lambda e: e.reciprocal(c3, q3), t)
            side.give(kq, t)
            yield
            kq, qb, fq = side.take()
            for j in range(2):
                t5 = P.do(lambda e: e.matmul(qb[:, 128 * j:128 * j + 128], c3[:, j:j + 1].broadcast_to([128, 128]),
                                             ident, start=True, stop=True), t, *fq)
            t = A.do(lambda e: e.activation(grow, qb[:, 0:S], ACT.Copy), t5, D.last())
            side.give(kq, t)
            yield
            last = []
            for bb in range(4):
                if bb == 2:
                    yield
                yb = x[:, bb, :]
                t1 = D.do(lambda e, yb=yb, bb=bb: e.scalar_tensor_tensor(
                    yb, yb, snh[:, 4 * g + bb:4 * g + bb + 1], grow, ALU.mult, ALU.mult), t)
                yt[4 * g + bb] = split_later(4 * g + bb, yb, t1)
                last += yt[4 * g + bb]
            flush()
            grp_done[g] = last + [tp]

        yt = [None] * 16
        for g in range(4):
            core = lambda: core_done[g - 2] if g > 1 else []
            whole = lambda: grp_done[g - 2] if g > 1 else []
            bc = BC[g % 2]
            dsts = [(16 + g, bc[:, 0, :]), (20 + g, bc[:, 1, :])] + [
                (4 * g + b, xsT[g % 2][:, b, :]) for b in range(4)]
            tt = []
            for p in range(3):
                items = []
                for cb, dst in dsts[2 * p:2 * p + 2]:
                    items.append(conv(cb, dst, whole if p else core))
                    tick()
                    silu()
                    if len(items) == 2:
                        tt += taps(items)
            tbc, tx = tt[0:2], tt[2:6]
            tz = []
            for b in range(4):
                k, ps, tok = block("w_in2", 0, 3072 + 128 * (4 * g + b), src, S)
                zb = zs[g % 2][:, b, :]
                t2 = A.do(lambda e: e.activation(zb, ps, ACT.Tanh, scale=0.5), tok, *whole())
                t3 = later(D, lambda e: e.scalar_tensor_tensor(zb, zb, 1.0, ps, ALU.add, ALU.mult), t2)
                main.give(k, t3)
                tz.append(t3)
                tick()
                silu()
            active.append(ssd(g, tx, tbc, tz))
        tsb = []
        sgb = [(xsT[0] if b < 4 else zs[0])[:, b % 4, :] for b in range(8)]
        tza = []
        for b in range(8):
            tza.append(sig(b, 8224, zacc[:, b, :]))
            tick()
        srca = [(*Yc(16 + j), yat[j]) for j in range(8)]
        for b in range(8):
            k, ps, tok = block("w_oa", 0, 128 * b, srca, S)
            z = zacc[:, b, :]
            t = D.do(lambda e, z=z, ps=ps: e.scalar_tensor_tensor(z, z, 1.0, ps, ALU.add, ALU.mult), tok, tza[b])
            main.give(k, t)
            tza[b] = t
            tick()
        drain()
        D.wait(*grp_done[2])
        A.wait(*grp_done[2])
        for b in range(8):
            tsb.append(sig(b, 9248, sgb[b]))
        srcb = [(*Yc(j), yt[j]) for j in range(16)]
        tmg = []
        for b in range(8):
            k, ps, tok = block("w_os", 0, 128 * b, srcb, S)
            z, s = zacc[:, b, :], sgb[b]
            t = D.do(lambda e, s=s, ps=ps: e.scalar_tensor_tensor(s, s, 1.0, ps, ALU.add, ALU.mult), tok, tsb[b])
            main.give(k, t)
            t = D.do(lambda e, s=s, z=z: e.tensor_tensor(z, z, s, ALU.add), t, tza[b])
            tmg.append(split_to(16 + b, z, t))
        srcm = [(*Yc(16 + b), tmg[b]) for b in range(8)]
        nxt = Norm("xn", rows[0], Z)
        for b in range(8):
            k, ps, tok = block("w_mo", 0, 128 * b, srcm, S)
            residual(b, ps, k, tok, 0.5, nxt, Z)
        return nxt

    norm = mixer(norm)

    def cross(norm):
        arena["at"] = 0
        mem_sb = alloc(8, S)
        kTt, qTt = alloc(8, S), alloc(8, S)
        V = alloc(2, 1024)
        Pm = alloc(2, 2, S)
        PTx = Ring([alloc(2, S) for _ in range(2)])
        nm, sm, rs = alloc(2, 4), alloc(2, 4), alloc(2, 4)
        mrow = rows[1][:, 0:S]
        barrier()
        SP.put(lambda e: e.dma_start(mem_sb, mem, sems["l_m"]), D.last(), A.last(), P.last())
        lm = (sems["l_m"], 16)
        row = norm.row[:, Z:T]
        mh = yh[:, 0:8 * S].rearrange("p (c s) -> p c s", c=8)
        ml = yl[:, 0:8 * S].rearrange("p (c s) -> p c s", c=8)
        mn = Norm("mn", mrow, 0, mem_sb, mh, ml)
        src = norm.feed()
        tq, ready = [], []
        for b in range(8):
            ready.append(block("w_q", 0, 128 * b, src, S))
            if b == 0:
                norm.rstd_sums(False)
            if b == 1:
                norm.rstd_row()
            while b and ready:
                k, ps, tok = ready.pop(0)
                i = len(tq)
                t = D.do(lambda e: e.tensor_tensor(qTt[:, i, :], ps, row, ALU.mult), tok, norm.rtok)
                main.give(k, t)
                tq.append(t)
            if b == 3:
                for c in range(2):
                    mn.chunk(c, lm)
            if 4 <= b < 7:
                for c in (2 * b - 6, 2 * b - 5):
                    mn.chunk(c, lm)
        flush()
        mn.rstd_sums(False)
        srcm = mn.feed()
        rt2, t_r2 = mn.col, mn.ctok
        flush()
        tv = []
        def values(hf):
            pair = [main.take() for _ in range(2)]
            for c in range(8):
                ws = [tile(("w_kv", 0, 128 * c, [(1024 + 512 * hf + 128 * i, 128, 0)])) for i in range(4)]
                q = (len(plan) - 1) // TILES % NSPL
                j0 = (len(plan) - 4) % TILES
                wh, wl = (w[:, q, 128 * j0:128 * j0 + 512] for w in (whi, wlo))
                for mt in range(2):
                    k, b, free = pair[mt]
                    P.wait(*free)
                    a = (mh[:, c, 128 * mt:128 * mt + 128], ml[:, c, 128 * mt:128 * mt + 128])
                    tok = mm3(b[:, :], a, (wh, wl), c == 0, c == 7, True)
                if ws[3][2] is not None:
                    pe_done[ws[3][2]] = tok
                if hf and c % 2:
                    flush()
                    tick()
            for mt in range(2):
                k, b, _ = pair[mt]
                t = D.do(lambda e, mt=mt, b=b: e.tensor_scalar(
                    V[:, mt, 512 * hf:512 * hf + 512], b[:, :], rt2[:, mt:mt + 1], None, ALU.mult), tok, t_r2)
                main.give(k, t)
                tv.append(t)

        values(0)
        tm = mn.rstd_row()
        tk = []
        t_o = [None] * 8

        def head(hd):
            tn = []
            for st in range(2):
                ks, sb_, fs = side.take()
                P.wait(*fs, *tq, *tk)
                for b in range(2):
                    tp = P.do(lambda e, b=b, st=st, sb_=sb_: e.matmul(
                        sb_[:, 0:S], qTt[:, 2 * hd + b, 128 * st:128 * st + 128], kTt[:, 2 * hd + b, :],
                        start=(b == 0), stop=(b == 1)))
                n1 = nm[:, st, hd:hd + 1]
                t = D.do(lambda e, sb_=sb_, n1=n1: e.tensor_reduce(n1, sb_[:, 0:S], AX, ALU.max, negate=True), tp)
                t = D.do(lambda e, n1=n1: e.tensor_scalar(n1, n1, 1.0 / 16, None, ALU.mult), t)
                te = A.do(lambda e, sb_=sb_, st=st, n1=n1: e.activation(
                    Pm[:, st, hd % 2, :], sb_[:, 0:S], ACT.Exp, scale=1.0 / 16, bias=n1,
                    accum_out=sm[:, st, hd:hd + 1]), t, *xdone.get(hd - 2, []))
                side.give(ks, te)
                t = D.do(lambda e, st=st: e.reciprocal(rs[:, st, hd:hd + 1], sm[:, st, hd:hd + 1]), te)
                tn.append(D.do(lambda e, st=st: e.tensor_scalar(
                    Pm[:, st, hd % 2, :], Pm[:, st, hd % 2, :], rs[:, st, hd:hd + 1], None, ALU.mult), t))
            yield
            ks, sb_, fs = side.take()
            P.wait(*fs, *tn)
            for mc in range(2):
                for st in range(2):
                    tp = P.do(lambda e, mc=mc, st=st: e.transpose(
                        sb_[:, 256 * mc + 128 * st:256 * mc + 128 * st + 128],
                        Pm[:, st, hd % 2, 128 * mc:128 * mc + 128], ident))
            xdone[hd] = [tp]
            kp, pt, fp = PTx.take()
            t = A.do(lambda e: e.activation(pt, sb_[:, :].rearrange("p (a b) -> p a b", a=2), ACT.Copy), tp, *fp)
            side.give(ks, t)
            yield
            while hd > 1 and len(tv) < 4:
                yield
            ks, sb2, fs = side.take()
            P.wait(*fs, t, *(tv if hd > 1 else tv[0:2]))
            for db in range(2):
                for mc in range(2):
                    tp = P.do(lambda e, db=db, mc=mc: e.matmul(
                        sb2[:, S * db:S * db + S], V[:, mc, 256 * hd + 128 * db:256 * hd + 128 * db + 128],
                        pt[:, mc, :], start=(mc == 0), stop=(mc == 1)))
            PTx.give(kp, tp)
            yield
            a, b = (y[:, (8 + 2 * hd) * S:(10 + 2 * hd) * S] for y in (yh, yl))
            t1 = A.do(lambda e: e.activation(a, sb2[:, :], ACT.Copy), tp)
            t2 = D.do(lambda e: e.tensor_tensor(b, sb2[:, :], a.bitcast(F), ALU.subtract), t1)
            t_o[2 * hd] = t_o[2 * hd + 1] = [t1, t2]
            side.give(ks, t2)

        xdone = {}
        for b in range(8):
            k, ps, tok = block("w_kv", 0, 128 * b, srcm, S)
            t = D.do(lambda e, b=b, ps=ps: e.tensor_tensor(kTt[:, b, :], ps, mrow, ALU.mult), tok, tm)
            main.give(k, t)
            tk.append(t)
            if b % 2:
                active.append(head(b // 2))
            tick()
        values(1)
        drain()
        srco = [(*Yc(8 + j), t_o[j]) for j in range(8)]
        nxt = Norm("f2n", rows[1], Z)
        for b in range(8):
            k, ps, tok = block("w_o", 0, 128 * b, srco, S)
            residual(b, ps, k, tok, 1.0, nxt, Z)
        return nxt

    norm = cross(norm)
    norm = ffn("f2", norm, lambda: Norm("fn", rows[0], Z))
    tr = norm.rstd(False, D.last())
    for c in range(8):
        hc = h[:, c, Z:T]
        t = D.do(lambda e: e.scalar_tensor_tensor(
            hc, hc, pc("fn", c), norm.row[:, Z:T], ALU.mult, ALU.mult), tr, *norm.tok[c])
        if c % 2:
            SP.put(lambda e: e.dma_start(out[:, c - 1:c + 1, :], h[:, c - 1:c + 1, Z:T], sems["o"]), t)
    SP.wait((sems["o"], 64))
    return P, D, A, SP, G, arena["top"]


ARENA = 15710


def program(nc, wts_shape_decl, small, par, con, mem, out):
    with ExitStack() as ctx:
        def sb(name, shape, dt=F):
            return ctx.enter_context(nc.sbuf_tensor(name, shape, dt))

        names = ["pe", "dve", "act", "sp", "pool", "l_h", "l_h2", "l_c1", "l_c", "l_p", "l_m", "o"] + [f"w{i}" for i in range(NRAW)]
        sems = {n: ctx.enter_context(nc.semaphore(n)) for n in names}
        tens = {
            "raw": sb("raw", [128, NRAW, SLOT]), "whi": sb("whi", [128, NSPL, SLOT], R),
            "wlo": sb("wlo", [128, NSPL, SLOT], R), "h": sb("h", [128, 8, T]),
            "xh": sb("xh", [128, 8, T], R), "xl": sb("xl", [128, 8, T], R),
            "yh": sb("yh", [128, YCOLS], R), "yl": sb("yl", [128, YCOLS], R),
            "cst": sb("cst", [128, NCONST]), "prm": sb("prm", [128, NPARAM]), "ar": sb("ar", [128, ARENA]),
            "cnb": sb("cnb", [128, 384], mybir.dt.bfloat16),
            "acr": sb("acr", [64, S + 32], R), "sq": sb("sq", [128, 2, T]), "rows": sb("rows", [128, 2, T]),
            "banks": [ctx.enter_context(nc.psum_tensor(f"bank{i}", [128, 512], F)) for i in range(8)],
        }
        plan = []
        build(nc, None, small, par, con, mem, out, 10 ** 6, plan, tens, sems)
        nslots = -(-len(plan) // TILES)
        wts = wts_shape_decl(nslots)
        again = []
        P, D, A, SP, G, top = build(nc, wts, small, par, con, mem, out, nslots, again, tens, sems)
        assert top <= ARENA, top
        assert len(again) == len(plan)
        block = ctx.enter_context(nc.Block())

        @block.sync
        def _(e):
            SP.run(e)

        @block.tensor
        def _(e):
            P.run(e)

        @block.gpsimd
        def _(e):
            G.run(e)

        @block.vector
        def _(e):
            D.run(e)

        @block.scalar
        def _(e):
            A.run(e)
    return plan, nslots


def kernel(**inputs):
    import concourse.bacc as _bacc
    from concourse.bass_utils import run_bass_kernel_spmd as _run

    a = {n: np.asarray(v) for n, v in inputs.items()}
    nc = _bacc.Bacc("TRN2", target_bir_lowering=False, num_devices=1)

    def dram(name, shape, kind="ExternalInput"):
        return nc.dram_tensor(name, shape, F, kind=kind).ap()

    small, par, con = dram("x_dram", [128, 8, T]), dram("par_dram", [128, NPARAM]), dram("con_dram", [128, NCONST])
    mem, out = dram("mem_dram", [128, 8, S]), dram("out_dram", [128, 8, S], "ExternalOutput")
    plan, nslots = program(nc, lambda n: dram("w_dram", [n, 128, SLOT]), small, par, con, mem, out)

    mats = {
        "w_in": a["w_in"], "pool_w": a["pool_w"].reshape(8, 128, 128), "w_a": a["w_branch_a"],
        "w_b": a["w_branch_b"], "w_out": a["w_out"], "f1_gu": a["ffn1_w_gate_up_2"], "f1_dn": a["ffn1_w_down_2"],
        "w_in2": a["w_in_2"], "w_oa": a["w_out_a_2"], "w_os": a["w_out_ssm_2"], "w_mo": a["w_mix_out_2"],
        "w_q": a["w_q_2"], "w_kv": a["w_kv_2"], "w_o": a["w_o_x_2"], "f2_gu": a["ffn2_w_gate_up_2"],
        "f2_dn": a["ffn2_w_down_2"],
    }
    w = np.zeros((nslots, 128, SLOT), np.float32)
    for n, item in enumerate(plan):
        if item is None:
            continue
        name, l, r0, cols = item
        s, j = divmod(n, TILES)
        for c0, width, at in cols:
            w[s, :, 128 * j + at:128 * j + at + width] = mats[name][l, r0:r0 + 128, c0:c0 + width]

    def cols(v, n):
        return np.asarray(v).reshape(n, 128).T

    p = np.zeros((128, NPARAM), np.float32)

    def put(name, v):
        p[0:v.shape[0], PARAMS[name]:PARAMS[name] + v.shape[1]] = v

    for l in range(2):
        put(f"ng{l}", cols(a["norm_gain"][l], 8))
        put(f"qn{l}", np.concatenate([a["q_norm_gain"][l]] * 2)[:, None])
        put(f"kn{l}", np.concatenate([a["k_norm_gain"][l], np.ones(64, np.float32)])[:, None])
        put(f"pb{l}", cols(a["pool_b"][l], 4))
        put(f"ps{l}", cols(a["pool_scale"][l], 4))
    put("f1n", cols(a["ffn1_norm_2"][0], 8))
    put("mxn", cols(a["mix_norm_2"][0], 8))
    put("ca", np.concatenate([cols(a["conv_a_w_2"][0, i], 8) for i in range(3)], 1))
    put("cw", np.concatenate([cols(a["ssm_conv_w_2"][0, i], 24) for i in range(4)], 1))
    put("cb", cols(a["ssm_conv_b_2"][0], 24))
    put("sd", cols(np.repeat(a["ssm_d_2"][0], 64), 16))
    put("sn", cols(a["ssm_norm_2"][0], 16))
    put("xn", cols(a["xattn_norm_2"][0], 8))
    put("mn", cols(a["mem_norm_2"][0], 8))
    put("f2n", cols(a["ffn2_norm_2"][0], 8))
    put("fn", cols(a["final_norm_2"], 8))
    put("dtb", a["ssm_dt_bias_2"][0][:, None])
    put("alog", a["ssm_a_log_2"][0][:, None])

    def fm(x):
        return np.ascontiguousarray(x.reshape(x.shape[0], 8, 128).transpose(2, 1, 0))

    arrays = {
        "x_dram": fm(np.concatenate([a["meta_tokens"], a["x"][0]], 0)), "par_dram": p, "con_dram": constants(),
        "mem_dram": fm(a["mem_2"][0]), "w_dram": w,
    }
    r = _run(nc, [arrays], core_ids=[0])
    o = np.asarray(r.results[0]["out_dram"])
    return np.ascontiguousarray(o.transpose(2, 1, 0)).reshape(1, S, 1024)
```
